# Optimizing a Trainium2 kernel written in Bass

```python
import math
import jax, jax.numpy as jnp
from jax import lax
import numpy as np

D_MODEL = 1024
BATCH = 1
SEQ = 512
DEPTH = 1
DEC_BATCH = 8
DEC_SEQ = 4
PAST_LEN = 2048
PAGE_SIZE = 128

HEAD_DIM = 64
N_MLSTM_HEADS = 8
N_NSA_HEADS = 8
N_KV_HEADS = 2
GQ = N_NSA_HEADS // N_KV_HEADS
MLSTM_W = N_MLSTM_HEADS * HEAD_DIM
NSA_W = N_NSA_HEADS * HEAD_DIM
MIX_WIDTH = MLSTM_W + NSA_W
KV_W = N_KV_HEADS * HEAD_DIM
MLSTM_CHUNK = 64
MLSTM_CONV = 4
CMP_BLOCK = 32
SEL_BLOCK = 64
SEL_TOPK = 16
WINDOW = 512
NSA_QBLOCK = 64
N_BUCKETS = 32
MAX_DISTANCE = 128
D_FF = 2688
FFN_CONV = 3
ALPHA = (2.0 * DEPTH) ** 0.25
BETA = (8.0 * DEPTH) ** -0.25
LN_EPS = 1e-5
IN_SIZES = (2 * MLSTM_W, MLSTM_W, MLSTM_W, N_MLSTM_HEADS, N_MLSTM_HEADS,
            NSA_W, KV_W, KV_W, KV_W, KV_W, KV_W, KV_W, 3 * N_NSA_HEADS)
IN_WIDTH = sum(IN_SIZES)

kernel_name = "hymba_mlstm_nsa_convffn_decode_step"

def split_columns(z):
    out, start = [], 0
    for s in IN_SIZES:
        out.append(z[..., start:start + s])
        start += s
    return out

def layer_norm(x, w, b):
    xf = x.astype(jnp.float32)
    mu = jnp.mean(xf, -1, keepdims=True)
    var = jnp.mean(jnp.square(xf - mu), -1, keepdims=True)
    return ((xf - mu) * lax.rsqrt(var + LN_EPS) * w + b).astype(x.dtype)

def head_norm(h, w):
    mu = jnp.mean(h, -1, keepdims=True)
    var = jnp.mean(jnp.square(h - mu), -1, keepdims=True)
    hn = (h - mu) * lax.rsqrt(var + LN_EPS)
    return hn.reshape(h.shape[:2] + (-1,)) * w

def causal_dwconv(u, prev, w, b):
    k_w = w.shape[0]
    t_len = u.shape[1]
    full = jnp.concatenate([prev.astype(u.dtype), u], axis=1)
    out = b
    for j in range(k_w):
        out = out + full[:, j:j + t_len] * w[j]
    return out, full[:, full.shape[1] - (k_w - 1):]

def masked_softmax(s, mask, axes):
    s = jnp.where(mask, s.astype(jnp.float32), -jnp.inf)
    mx = jnp.max(s, axis=axes, keepdims=True)
    mx = jnp.where(jnp.isfinite(mx), mx, 0.0)
    e = jnp.exp(s - mx)
    den = jnp.sum(e, axis=axes, keepdims=True)
    return e / jnp.maximum(den, 1e-30)

def t5_bucket(dist):
    n = jnp.maximum(dist, 0)
    max_exact = N_BUCKETS // 2
    large = max_exact + (jnp.log(jnp.maximum(n, 1).astype(jnp.float32) / max_exact)
                         / math.log(MAX_DISTANCE / max_exact) * (N_BUCKETS - max_exact)).astype(jnp.int32)
    large = jnp.minimum(large, N_BUCKETS - 1)
    return jnp.where(n < max_exact, n, large)

def head_bias(rel_bias, dist):
    b = rel_bias[t5_bucket(dist)].astype(jnp.float32)
    b = b.reshape(dist.shape + (N_KV_HEADS, GQ))
    return jnp.transpose(b, (2, 3, 0, 1))

def group_bias(rel_bias, dist):
    table = jnp.transpose(rel_bias.reshape(N_BUCKETS, N_KV_HEADS, GQ), (1, 0, 2))
    buckets = t5_bucket(dist)
    b = jax.vmap(lambda tb, bk: tb[bk], in_axes=(0, 1), out_axes=1)(table, buckets)
    return jnp.moveaxis(b, -1, 2).astype(jnp.float32)

def mlstm_chunkwise(q, k, v, ig, lf, c0, n0, m0):
    f32 = jnp.float32
    bsz, t_len, n_h, d = q.shape
    q, k, v, ig, lf = (a.astype(f32) for a in (q, k, v, ig, lf))
    k = k * (d ** -0.5)
    c_len = MLSTM_CHUNK if t_len % MLSTM_CHUNK == 0 else t_len
    n_c = t_len // c_len

    def to_chunks(a):
        return jnp.moveaxis(a.reshape((bsz, n_c, c_len) + a.shape[2:]), 1, 0)

    causal = jnp.tril(jnp.ones((c_len, c_len), bool))

    def step(carry, xs):
        c_st, n_st, m_st = carry
        qc, kc, vc, ic, fc = xs
        b = jnp.moveaxis(jnp.cumsum(fc, axis=1), 2, 1)
        ih = jnp.moveaxis(ic, 2, 1)
        dmat = jnp.where(causal, b[..., :, None] - b[..., None, :] + ih[..., None, :], -jnp.inf)
        inter = b + m_st[..., None]
        m_t = jnp.maximum(inter, jnp.max(dmat, -1))
        w_intra = jnp.exp(dmat - m_t[..., None])
        w_inter = jnp.exp(inter - m_t)
        a = w_intra * jnp.einsum('blhd,bshd->bhls', qc, kc)
        num = (jnp.einsum('bhls,bshd->blhd', a, vc)
               + jnp.einsum('bhed,blhd->blhe', c_st, qc) * jnp.moveaxis(w_inter, 1, 2)[..., None])
        den = jnp.sum(a, -1) + w_inter * jnp.einsum('bhd,blhd->bhl', n_st, qc)
        den = jnp.maximum(jnp.abs(den), jnp.exp(-m_t))
        h = num / jnp.moveaxis(den, 1, 2)[..., None]
        b_end = b[..., -1]
        dec = b_end[..., None] - b + ih
        m_new = jnp.maximum(b_end + m_st, jnp.max(dec, -1))
        wk = jnp.exp(dec - m_new[..., None])
        sc = jnp.exp(b_end + m_st - m_new)
        c_new = sc[..., None, None] * c_st + jnp.einsum('bhl,blhe,blhd->bhed', wk, vc, kc)
        n_new = sc[..., None] * n_st + jnp.einsum('bhl,blhd->bhd', wk, kc)
        return (c_new, n_new, m_new), h

    carry0 = (c0.astype(f32), n0.astype(f32), m0.astype(f32))
    (c_f, n_f, m_f), hs = lax.scan(step, carry0, tuple(to_chunks(a) for a in (q, k, v, ig, lf)))
    h = jnp.moveaxis(hs, 0, 1).reshape(bsz, t_len, n_h, d)
    return h, c_f, n_f, m_f

def nsa_attend(q, q_pos0, kv_all, win_all, w_pos0, pool_w, rel_bias):
    bsz, t_q = q.shape[:2]
    t_k = kv_all.shape[1]
    qg = (q.astype(jnp.float32) * HEAD_DIM ** -0.5).reshape(bsz, t_q, N_KV_HEADS, GQ, HEAD_DIM)
    n_cmp = t_k // CMP_BLOCK
    cmp_rows = kv_all[:, :n_cmp * CMP_BLOCK, :2].reshape(bsz, n_cmp, CMP_BLOCK, 2, N_KV_HEADS, HEAD_DIM)
    kv_cmp = jnp.einsum('bcjegd,ejg->ebcgd', cmp_rows, pool_w)
    k_cmp, v_cmp = kv_cmp[0], kv_cmp[1]
    cmp_end = jnp.arange(n_cmp) * CMP_BLOCK + (CMP_BLOCK - 1)
    n_sel = -(-t_k // SEL_BLOCK)
    sel_rows = jnp.pad(kv_all[:, :, 2:], ((0, 0), (0, n_sel * SEL_BLOCK - t_k), (0, 0), (0, 0), (0, 0)))
    sel_blocks = jnp.transpose(sel_rows.reshape(bsz, n_sel, SEL_BLOCK, 2, N_KV_HEADS, HEAD_DIM),
                               (0, 4, 1, 2, 3, 5))
    top_k = min(SEL_TOPK, n_sel)
    ratio = SEL_BLOCK // CMP_BLOCK
    win_pad = jnp.pad(win_all, ((0, 0), (WINDOW, 0), (0, 0), (0, 0), (0, 0)))
    qb_len = NSA_QBLOCK if t_q % NSA_QBLOCK == 0 else t_q
    gather = jax.vmap(jax.vmap(lambda blocks, idx: blocks[idx]))

    def one_block(i):
        qs = i * qb_len
        qb = lax.dynamic_slice_in_dim(qg, qs, qb_len, axis=1)
        t0 = q_pos0 + qs
        t = t0 + jnp.arange(qb_len)
        dist_c = t[:, None] - cmp_end[None, :]
        s_c = jnp.einsum('bqgjd,bcgd->bgjqc', qb, k_cmp) + head_bias(rel_bias, dist_c)
        p_c = masked_softmax(s_c, dist_c >= 0, (-1,))
        o_c = jnp.einsum('bgjqc,bcgd->bqgjd', p_c, v_cmp)
        imp = jnp.pad(jnp.sum(p_c, 2), ((0, 0), (0, 0), (0, 0), (0, n_sel * ratio - n_cmp)))
        imp = imp.reshape(bsz, N_KV_HEADS, qb_len, n_sel, ratio).sum(-1)
        blk = jnp.arange(n_sel)[None, :]
        cur = (t // SEL_BLOCK)[:, None]
        score = jnp.where(blk == cur, jnp.inf, jnp.where(blk < cur, imp, -jnp.inf))
        top_s, top_i = lax.top_k(score, top_k)
        kv_sel = gather(sel_blocks, top_i)
        key_pos = top_i[..., None] * SEL_BLOCK + jnp.arange(SEL_BLOCK)
        dist_s = t[:, None, None] - key_pos
        mask_s = (top_s > -jnp.inf)[..., None] & (dist_s >= 0)
        s_s = jnp.einsum('bqgjd,bgqksd->bgjqks', qb, kv_sel[..., 0, :]) + group_bias(rel_bias, dist_s)
        p_s = masked_softmax(s_s, mask_s[:, :, None], (-2, -1))
        o_s = jnp.einsum('bgjqks,bgqksd->bqgjd', p_s, kv_sel[..., 1, :])
        kv_w = lax.dynamic_slice_in_dim(win_pad, t0 - w_pos0, WINDOW + qb_len, axis=1)
        wpos = t0 - WINDOW + jnp.arange(WINDOW + qb_len)
        dist_w = t[:, None] - wpos[None, :]
        mask_w = (dist_w >= 0) & (dist_w <= WINDOW) & (wpos[None, :] >= w_pos0)
        s_w = jnp.einsum('bqgjd,bsgd->bgjqs', qb, kv_w[:, :, 0]) + head_bias(rel_bias, dist_w)
        p_w = masked_softmax(s_w, mask_w, (-1,))
        o_w = jnp.einsum('bgjqs,bsgd->bqgjd', p_w, kv_w[:, :, 1])
        return o_c, o_s, o_w

    outs = lax.map(one_block, jnp.arange(t_q // qb_len))

    def unblock(o):
        return jnp.moveaxis(o, 0, 1).reshape(bsz, t_q, N_NSA_HEADS, HEAD_DIM)

    return unblock(outs[0]), unblock(outs[1]), unblock(outs[2])

def hybrid_layer(x, pos0, kv_past, win_past, c0, n0, m0, mconv_prev, fconv_prev,
                 w_in, b_in, mlstm_conv_w, mlstm_conv_b, mlstm_norm_w, nsa_pool_w, rel_bias,
                 w_out, ln1_w, ln1_b, w_up, b_up, ffn_conv_w, ffn_conv_b, w_down, b_down, ln2_w, ln2_b):
    bsz, t_len, _ = x.shape
    z = jnp.einsum('btd,de->bte', x, w_in) + b_in
    m_qk, m_v, m_o, m_i, m_f, n_q, c_k, c_v, s_k, s_v, w_k, w_v, n_g = split_columns(z)
    qk, mconv_new = causal_dwconv(m_qk, mconv_prev, mlstm_conv_w, mlstm_conv_b)
    qk = jax.nn.silu(qk)
    hm = lambda a: a.reshape(bsz, t_len, N_MLSTM_HEADS, HEAD_DIM)
    h, c_new, n_new, m_new = mlstm_chunkwise(hm(qk[..., :MLSTM_W]), hm(qk[..., MLSTM_W:]), hm(m_v),
                                             m_i, jax.nn.log_sigmoid(m_f.astype(jnp.float32)), c0, n0, m0)
    mix_m = jax.nn.sigmoid(m_o.astype(jnp.float32)) * head_norm(h, mlstm_norm_w)
    hk = lambda a: a.reshape(bsz, t_len, N_KV_HEADS, HEAD_DIM)
    kv_new = jnp.stack([hk(c_k), hk(c_v), hk(s_k), hk(s_v)], axis=2)
    win_new = jnp.stack([hk(w_k), hk(w_v)], axis=2)
    kv_all = kv_new if kv_past is None else jnp.concatenate([kv_past.astype(kv_new.dtype), kv_new], axis=1)
    win_all = win_new if win_past is None else jnp.concatenate([win_past.astype(win_new.dtype), win_new], axis=1)
    w_pos0 = pos0 + t_len - win_all.shape[1]
    o_c, o_s, o_w = nsa_attend(n_q.reshape(bsz, t_len, N_NSA_HEADS, HEAD_DIM), pos0, kv_all, win_all,
                               w_pos0, nsa_pool_w, rel_bias)
    g = jax.nn.sigmoid(n_g.astype(jnp.float32)).reshape(bsz, t_len, 3, N_NSA_HEADS)[..., None]
    mix_n = (g[:, :, 0] * o_c + g[:, :, 1] * o_s + g[:, :, 2] * o_w).reshape(bsz, t_len, NSA_W)
    mix = jnp.concatenate([mix_m, mix_n], axis=-1).astype(x.dtype)
    x1 = layer_norm(ALPHA * x + mix @ w_out, ln1_w, ln1_b)
    u, fconv_new = causal_dwconv(x1 @ w_up + b_up, fconv_prev, ffn_conv_w, ffn_conv_b)
    ff = (jax.nn.gelu(u[..., :D_FF]) * u[..., D_FF:]) @ w_down + b_down
    y = layer_norm(ALPHA * x1 + ff, ln2_w, ln2_b)
    win_state = win_all[:, win_all.shape[1] - min(WINDOW, pos0 + t_len):]
    return y, kv_new, win_state, c_new, n_new, m_new, mconv_new, fconv_new

def setup_inputs(seed: int = 0) -> dict:
    key = jax.random.key(seed)
    ks = jax.random.split(key, 32)
    nrm = lambda i, shape: jax.random.normal(ks[i], shape, jnp.float32)
    n_pages = PAST_LEN // PAGE_SIZE
    n_used = DEC_BATCH * n_pages
    n_pool = n_used + max(n_used // 4, 1)
    win_buf = min(WINDOW, PAST_LEN)
    page_table = jax.random.permutation(ks[0], n_pool)[:n_used].reshape(DEC_BATCH, n_pages).astype(jnp.int32)
    f_start = 2 * MLSTM_W + 2 * MLSTM_W + N_MLSTM_HEADS
    b_in = 0.02 * nrm(1, (IN_WIDTH,))
    b_in = b_in.at[f_start:f_start + N_MLSTM_HEADS].add(jnp.linspace(3.0, 6.0, N_MLSTM_HEADS))
    return {
        'x_prompt': nrm(2, (BATCH, SEQ, D_MODEL)),
        'x_sample': nrm(3, (DEC_BATCH, DEC_SEQ, D_MODEL)),
        'cache_nsa_kv': nrm(4, (n_pool, PAGE_SIZE, 4, N_KV_HEADS, HEAD_DIM)),
        'cache_win_kv': nrm(5, (DEC_BATCH, win_buf, 2, N_KV_HEADS, HEAD_DIM)),
        'state_mlstm_c': 0.3 * nrm(6, (DEC_BATCH, N_MLSTM_HEADS, HEAD_DIM, HEAD_DIM)),
        'state_mlstm_n': 0.3 * nrm(7, (DEC_BATCH, N_MLSTM_HEADS, HEAD_DIM)),
        'state_mlstm_m': nrm(8, (DEC_BATCH, N_MLSTM_HEADS)),
        'state_mlstm_conv': nrm(9, (DEC_BATCH, MLSTM_CONV - 1, 2 * MLSTM_W)),
        'state_ffn_conv': nrm(10, (DEC_BATCH, FFN_CONV - 1, 2 * D_FF)),
        'page_table': page_table,
        'w_in': nrm(11, (D_MODEL, IN_WIDTH)) * D_MODEL ** -0.5,
        'b_in': b_in,
        'mlstm_conv_w': nrm(12, (MLSTM_CONV, 2 * MLSTM_W)) * MLSTM_CONV ** -0.5,
        'mlstm_conv_b': 0.02 * nrm(13, (2 * MLSTM_W,)),
        'mlstm_norm_w': 1.0 + 0.02 * nrm(14, (MLSTM_W,)),
        'nsa_pool_w': CMP_BLOCK ** -0.5 * (1.0 + 0.1 * nrm(15, (2, CMP_BLOCK, N_KV_HEADS))),
        'rel_bias': 0.1 * nrm(16, (N_BUCKETS, N_NSA_HEADS)),
        'w_out': nrm(17, (MIX_WIDTH, D_MODEL)) * MIX_WIDTH ** -0.5 * BETA,
        'ln1_w': 1.0 + 0.02 * nrm(18, (D_MODEL,)),
        'ln1_b': 0.02 * nrm(19, (D_MODEL,)),
        'w_up': nrm(20, (D_MODEL, 2 * D_FF)) * D_MODEL ** -0.5,
        'b_up': 0.02 * nrm(21, (2 * D_FF,)),
        'ffn_conv_w': nrm(22, (FFN_CONV, 2 * D_FF)) * FFN_CONV ** -0.5,
        'ffn_conv_b': 0.02 * nrm(23, (2 * D_FF,)),
        'w_down': nrm(24, (D_FF, D_MODEL)) * D_FF ** -0.5 * BETA,
        'b_down': 0.02 * nrm(25, (D_MODEL,)),
        'ln2_w': 1.0 + 0.02 * nrm(26, (D_MODEL,)),
        'ln2_b': 0.02 * nrm(27, (D_MODEL,)),
    }

def reference(x_prompt, x_sample, cache_nsa_kv, cache_win_kv, state_mlstm_c, state_mlstm_n, state_mlstm_m,
              state_mlstm_conv, state_ffn_conv, page_table,
              w_in, b_in, mlstm_conv_w, mlstm_conv_b, mlstm_norm_w, nsa_pool_w, rel_bias, w_out,
              ln1_w, ln1_b, w_up, b_up, ffn_conv_w, ffn_conv_b, w_down, b_down, ln2_w, ln2_b):
    weights = (w_in, b_in, mlstm_conv_w, mlstm_conv_b, mlstm_norm_w, nsa_pool_w, rel_bias, w_out,
               ln1_w, ln1_b, w_up, b_up, ffn_conv_w, ffn_conv_b, w_down, b_down, ln2_w, ln2_b)
    bsz = x_prompt.shape[0]
    f32 = jnp.float32
    for _layer in range(DEPTH):
        (y_p, kv_p, win_p, c_p, n_p, m_p, mconv_p, fconv_p) = hybrid_layer(
            x_prompt, 0, None, None,
            jnp.zeros((bsz, N_MLSTM_HEADS, HEAD_DIM, HEAD_DIM), f32),
            jnp.zeros((bsz, N_MLSTM_HEADS, HEAD_DIM), f32),
            jnp.zeros((bsz, N_MLSTM_HEADS), f32),
            jnp.zeros((bsz, MLSTM_CONV - 1, 2 * MLSTM_W), x_prompt.dtype),
            jnp.zeros((bsz, FFN_CONV - 1, 2 * D_FF), x_prompt.dtype),
            *weights)
    dec_b, n_pages = page_table.shape
    kv_past = cache_nsa_kv[page_table].reshape(dec_b, n_pages * PAGE_SIZE, 4, N_KV_HEADS, HEAD_DIM)
    past_len = n_pages * PAGE_SIZE
    for _layer in range(DEPTH):
        (y_s, kv_s, win_s, c_s, n_s, m_s, mconv_s, fconv_s) = hybrid_layer(
            x_sample, past_len, kv_past, cache_win_kv, state_mlstm_c, state_mlstm_n, state_mlstm_m,
            state_mlstm_conv, state_ffn_conv, *weights)
    return (y_p, y_s, kv_p, kv_s, win_p, win_s, c_p, c_s, n_p, n_s, m_p, m_s, mconv_p, mconv_s, fconv_p, fconv_s)


_drawn_inputs = setup_inputs


def setup_inputs(seed=0):
    import zlib

    import numpy as np

    out = dict(_drawn_inputs(seed))
    spreads = {}
    factors = {'mlstm_norm_w': 24.628,
     'nsa_pool_w': 4.414,
     'rel_bias': 7.706,
     'ln1_w': 2.758,
     'ln1_b': 2.71,
     'b_up': 7.435,
     'ffn_conv_b': 6.421,
     'b_down': 11.569,
     'ln2_w': 7.821,
     'ln2_b': 8.722}
    for name, (base, spread) in spreads.items():
        noise = np.random.default_rng([zlib.crc32(name.encode()), seed]).standard_normal(out[name].shape)
        drawn = base * np.exp(spread * noise) if base else spread * noise
        out[name] = __import__('jax').numpy.asarray(drawn.astype(out[name].dtype))
    for name, factor in factors.items():
        out[name] = (out[name] * factor).astype(out[name].dtype)
    return out
```

```python
import math
from contextlib import ExitStack

import numpy as np

import concourse.bass as bass
from concourse import mybir

F32 = mybir.dt.float32
F32R = mybir.dt.float32r
I32 = mybir.dt.int32
ALU = mybir.AluOpType
ACT = mybir.ActivationFunctionType
AX = mybir.AxisListType.X

D = 1024
KD = D // 128
T = 512
QT = T // 128
NB, TS = 8, 4
NS = NB * TS
NT = T + NS
HALF = T // 2
H, HD = 8, 64
NG, GQ = 2, 4
ZT = 27
UP = 42
FT = UP // 2
DOWN_PARTS = 3
KP = FT // DOWN_PARTS
RING = 4
PAGES, PAST = 16, 2048
PAGE_RING = 8
POOL_PAGES = 160
NBLK, TOPK = 32, 16
WIN = 512
ALPHA = 2.0 ** 0.25
EPS = 1e-5
NEG = -1e30
FLOOR = -1e20
DEN_MIN = 1e-30
QS = HD ** -0.5

Z_MQ, Z_MK, Z_MO, Z_G, Z_MV, Z_NQ = 0, 4, 8, 12, 13, 17
Z_CK, Z_CV, Z_SK, Z_SV, Z_WK, Z_WV = 21, 22, 23, 24, 25, 26
G_I, G_F, G_N = 0, 32, 64


def table(*widths):
    at, n = {}, 0
    for name, w in widths:
        at[name] = (n, w)
        n += w
    return at, n


COL, NCOL = table(("b_in", ZT), ("mconv_w", 32), ("mconv_b", 8), ("norm_w", 4), ("ln1_w", 8), ("ln1_b", 8),
                  ("b_up", UP), ("fconv_w", 3 * UP), ("fconv_b", UP), ("b_down", 8), ("ln2_w", 8), ("ln2_b", 8))
C128, NC128 = table(("ident", 128), ("tri", 128), ("avg", 128), ("ones", 128), ("hblk", 8), ("onehot", 580))
C32, NC32 = table(("trib", 32), ("selend", 32), ("selc", 512), ("selb", 8), ("bm", 8), ("maskb", 32),
                  ("rowsel", 256), ("headmask", 8), ("maskw", 516), ("tie", 1024), ("jsum", 32))
NREL = 640
ZW = 124


def bucket(n):
    if n < 16:
        return max(n, 0)
    return min(31, 16 + int(math.log(n / 16) / math.log(8) * 16))


def constants():
    f = np.float32
    p = np.arange(128)
    c = {"ident": np.eye(128), "tri": p[None, :] >= p[:, None], "avg": np.full((128, 128), 1 / D),
         "ones": np.ones((128, 128)), "hblk": (p[:, None] // 16 == np.arange(8)[None, :])}
    oh = np.zeros((TS, 32, 580))
    for q in range(TS):
        for i in range(516):
            pos = PAST - WIN + i
            oh[q, bucket(PAST + q - pos), i] = 1
        for i in range(64):
            oh[q, bucket(PAST + q - (32 * i + 31)), 516 + i] = 1
    c["onehot"] = oh.reshape(128, 580)
    a128 = np.concatenate([np.asarray(c[n], f) for n in C128], axis=1)
    r = np.arange(32)
    same = r[:, None] // 4 == r[None, :] // 4
    d = {"trib": same & (r[:, None] <= r[None, :]),
         "selend": same & (r[:, None] % 4 == 3),
         "selc": np.stack([(r[:, None] == 4 * (2 * bp + p[None, :] // 64)) for bp in range(4)], 1).reshape(32, 512),
         "selb": r[:, None] == 4 * np.arange(8)[None, :],
         "bm": r[:, None] // 4 == np.arange(8)[None, :],
         "maskb": np.where(same & (r[None, :] <= r[:, None]), 0, NEG),
         "headmask": r[:, None] // 4 == np.arange(8)[None, :],
         "tie": np.broadcast_to((r[None, :] < r[:, None]).reshape(1, 1024), (32, 1024)),
         "jsum": (r[:, None] // 16 == r[None, :] // 16) & (r[:, None] % 4 == r[None, :] % 4)}
    rs = np.zeros((32, 8, 32))
    for b in range(8):
        for row in range(32):
            rs[4 * b + row % 4, b, row] = 1
    d["rowsel"] = rs.reshape(32, 256)
    mw = np.zeros((32, 516))
    for row in range(32):
        q = row % 4
        mw[row, :q] = NEG
        mw[row, 512 + q + 1:] = NEG
    d["maskw"] = mw
    a32 = np.concatenate([np.asarray(d[n], f) for n in C32], axis=1)
    rel = np.zeros((32, 2 * NREL))
    for k in range(NREL):
        dist = 511 - k
        if dist >= 0:
            rel[bucket(dist), k] = 1
        else:
            rel[0:8, NREL + k] = NEG
    return a128, a32, rel.astype(f)


def layer(nc, a):
    with ExitStack() as ctx:
        def sb(name, shape, dt=F32):
            return ctx.enter_context(nc.sbuf_tensor(name, shape, dt))

        def sem(name):
            return ctx.enter_context(nc.semaphore(name))

        def large(suffix, dt):
            return [(name + suffix, shape, dt) for name, shape in (
                ("xt", [128, KD, NT]),
                ("zt", [128, ZT, NT]),
                ("wring", [128, RING, 1024]),
                ("whi", [128, 2, 1024]),
                ("mixt", [128, KD, NT]),
                ("arena", [128, 11296]))]

        with ExitStack() as scope:
            xt_r, zt_r, wring_r, whi, mixt_r, arena_r = (
                scope.enter_context(nc.sbuf_tensor(*t)) for t in large("_r", F32R))
        xt, zt, wring, whi_f, mixt, arena = (sb(*t) for t in large("", F32))
        cst = sb("cst", [128, NC128])
        c32 = sb("c32", [32, NC32])
        col = sb("col", [128, NCOL])
        smem = sb("smem", [128, 4112])
        tvs = whi_f[0:32, 0, 0:512]
        gf = sb("gf", [8, NT])
        gi = sb("gi", [8, NT])
        ga = sb("ga", [8, NT])
        gm = sb("gm", [8, T])
        gsig = sb("gsig", [24, NT])
        gcol = sb("gcol", [128, 216])
        lnb = sb("lnb", [8, NT])
        emp = sb("emp", [128, 64])
        s4 = sb("s4", [128, 8])
        var = sb("var", [128, 32])
        epsc = sb("epsc", [128, 1])
        sm = sb("sm", [128, 72])
        wpad = sb("wpad", [128, NG * (4 + ZW + 80)])
        relp = sb("relp", [128, 40])
        ptab = sb("ptab", [1, 128], I32)
        relrow = nc.dram_tensor("relrow", (H, 128, NREL), F32, kind="Internal")

        q4 = [ctx.enter_context(nc.psum_tensor(f"q{i}", [128, 2, 512], F32)) for i in range(4)]
        bank = [q4[i // 2][:, i % 2, :] for i in range(8)]

        def k128(name):
            n, w = C128[name]
            return cst[:, n:n + w]

        def k32(name):
            n, w = C32[name]
            return c32[:, n:n + w]

        def vec(name, i, p0=0, p1=128):
            n = COL[name][0] + i
            return col[p0:p1, n:n + 1]

        wkey = wpad[:, 0:8].rearrange("p (g c) -> p g c", g=NG)
        wval = wpad[:, 8:8 + NG * ZW].rearrange("p (g c) -> p g c", g=NG)
        wrep = wpad[:, 8 + NG * ZW:].rearrange("p (g c) -> p g c", g=NG)
        ident, tri, avg, ones = k128("ident"), k128("tri"), k128("avg"), k128("ones")

        tv = arena[:, 0:2080].rearrange("p (i h c) -> p i h c", i=QT, h=H)
        tk = arena[:, 2080:4640].rearrange("p (i c) -> p i c", i=QT + 1)
        tkv = arena[:, 4640:7200].rearrange("p (i k c) -> p i k c", i=QT + 1, k=4)
        tb = arena[:, 7200:11296].rearrange("p (h x) -> p h x", h=H)
        pages = arena[:, 0:PAGE_RING * 384].rearrange("p (s c) -> p s c", s=PAGE_RING)
        wpage = arena[:, 3072:5120].rearrange("p (s k c) -> p s k c", s=2, k=4)
        vsel = arena[:, 7200:11296].rearrange("p (s k c) -> p s k c", s=2, k=PAGES)

        uq = smem[:, 0:1142].rearrange("p (s c) -> p s c", s=2)
        tq = smem[:, 1142:2284].rearrange("p (s c) -> p s c", s=2)
        hm = smem[:, 2284:2476].rearrange("p (n c) -> p n c", n=8)
        mc = smem[:, 2476:2692].rearrange("p (n c) -> p n c", n=8)
        ohp = smem[0:32, 2700:2700 + 2 * NREL]
        cn = smem[:, 0:2048].rearrange("p (b h d) -> p b h d", b=4, h=H)
        vexp = smem[0:32, 2048:4096].rearrange("p (s c) -> p s c", s=2)
        score = smem[0:32, 0:4104].rearrange("p (s c) -> p s c", s=2)

        work = xt[:, :, :].rearrange("p k c -> p (k c)")
        aw = work[:, 0:2560].rearrange("p (s c) -> p s c", s=2)
        ww = work[:, 2560:3584].rearrange("p (s c) -> p s c", s=2)
        cout = work[0:65, 3584:4096]
        sq = work[:, 4096:4352].rearrange("p (j d) -> p j d", j=4)
        hc = zt[:, 13:17, :].rearrange("p k c -> p (k c)")[:, 0:2048].rearrange("p (j h d) -> p j h d", j=4, h=H)
        wv = mixt[:, 4:8, :].rearrange("p k c -> p (k c)")[:, 0:2080].rearrange("p (i h c) -> p i h c", i=4, h=H)

        ctv = work[:, 0:2048].rearrange("p (c n) -> p c n", c=4)
        aa = work[0:32, 2048:2304]
        at_sb = work[0:32, 2304:2560]
        n0 = work[0:8, 2560:3072]
        gd = work[0:32, 3072:3328]
        gmk = work[0:32, 3328:3584]
        mfree = mixt[0:32, 4:8, :].rearrange("p k c -> p (k c)")
        hcs = mfree[:, 0:512].rearrange("p (h d) -> p h d", h=H)
        inter = mfree[:, 512:1024].rearrange("p (h d) -> p h d", h=H)
        tmp = mfree[:, 1024:1536].rearrange("p (b e) -> p b e", b=NB)
        sqs = mfree[:, 1536:2048].rearrange("p (h d) -> p h d", h=H)
        wvs = zt[0:32, 0, 0:512]
        wks = zt[0:32, 1, 0:512]
        m0 = sm[0:32, 0:8]
        ntv = sm[:, 8:40].rearrange("p (c b) -> p c b", c=4)
        scb = sm[:, 40:72]
        pb = work[:, 0:1024].rearrange("p (s c) -> p s c", s=2)
        ptb = work[:, 1024:2048].rearrange("p (s c) -> p s c", s=2)
        mxa = work[:, 2048:2560]
        mxt = work[:, 2560:3072]
        vblk = work[:, 3072:3584].rearrange("p (h d) -> p h d", h=H)
        scp = work[:, 3584:3712].rearrange("p (h c) -> p h c", h=H)
        cpt = work[:, 3712:3840]
        kcp = work[:, 3840:3856]
        mxs = work[:, 3856:3872]
        den = work[:, 3872:3896].rearrange("p (k h) -> p k h", k=3)
        cmx = work[:, 3896:3904]
        gsc = work[:, 3904:3912]
        sqb = smem[:, 0:2 * NT].rearrange("p (s c) -> p s c", s=2)
        rstd = smem[:, 2 * NT:3 * NT]
        tf = smem[:, 0:2248].rearrange("p (s c) -> p s c", s=4)
        hf = smem[:, 2248:2248 + 672].rearrange("p (n c) -> p n c", n=UP)
        fc = smem[:, 2920:2920 + 756].rearrange("p (n c) -> p n c", n=UP)
        uf = zt[:, 21:27, :].rearrange("p k c -> p (k c)")[:, 0:2248].rearrange("p (s c) -> p s c", s=4)
        ybuf = zt[:, 21:27, :].rearrange("p k c -> p (k c)")[:, 0:2 * NT].rearrange("p (s c) -> p s c", s=2)
        s32 = whi_f[0:32, 1, 0:160]
        sc8 = sb("sc8", [8, 8])

        pts = work[:, 0:512]
        ptn = work[0:4, 512:576]
        ptc = work[0:64, 576:608]
        ptw = work[:, 608:736]
        skt = work[:, 736:1760].rearrange("p (s c) -> p s c", s=2)
        kct = work[:, 1760:1824]
        vcs = work[0:64, 1824:1952]
        sw = work[0:32, 1952:2984].rearrange("p (s c) -> p s c", s=2)
        qb = work[:, 2984:3240].rearrange("p (b m) -> p b m", b=NB)
        pc = work[0:32, 3240:3368].rearrange("p (s c) -> p s c", s=2)
        gr = work[0:32, 3368:3392]
        oacc = work[0:32, 3392:3520]
        otmp = work[0:32, 3520:3648]
        impt = work[0:32, 3648:3680]
        rank = work[0:32, 3680:3712]
        pair = work[0:32, 3712:3744]
        st = work[0:32, 3744:3760]
        gtmp = work[0:32, 3760:3952]
        z01 = zt[0:32, 0:2, :].rearrange("p k c -> p (k c)")
        biasw, biasc = z01[:, 0:516], z01[:, 516:580]
        rk1 = zt[0:32, 2:4, :].rearrange("p k c -> p (k c)")[:, 0:1024].rearrange("p (j i) -> p j i", j=NBLK)
        rk2 = zt[0:32, 4:6, :].rearrange("p k c -> p (k c)")[:, 0:1024].rearrange("p (j i) -> p j i", j=NBLK)
        vn = zt[0:4, 13:17, :].rearrange("p k c -> p (k c)")[:, 0:2048].rearrange("p (b c) -> p b c", b=NB)

        def wide(t, n=KD):
            return t[:, 0:n * NT].rearrange("p (k c) -> p k c", k=n)

        xt_lo, mixt_lo, zt_lo = xt_r, mixt_r, zt_r
        arena_hi = wide(arena_r)
        x1_hi = mixt_lo
        f_hi_arena = wide(arena_r, FT - 1)
        f_hi_last = zt_r[:, 21:27, :].rearrange("p k c -> p (k c)")[:, 2256:2256 + NT]

        def f_hi_of(i):
            return f_hi_arena[:, i, :] if i < FT - 1 else f_hi_last

        consts = sem("consts")
        xin = [sem(f"x_part{k}") for k in range(KD // 2)]
        w_hi, w_lo = sem("w_hi"), sem("w_lo")
        x_hi, x_lo, m_hi, m_lo = sem("x_hi"), sem("x_lo"), sem("m_hi"), sem("m_lo")
        y_hi, y_lo, f_hi, f_lo = sem("y_hi"), sem("y_lo"), sem("f_hi"), sem("f_lo")
        w_land = [sem(f"w_land{i}") for i in range(RING)]
        w_used = sem("w_used")
        z_act, z_dve = sem("z_act"), sem("z_dve")
        conv_done, silu_done = sem("conv_done"), sem("silu_done")
        dve_step, act_step, pool_step, pe_step = (sem(n) for n in ("dve_step", "act_step", "pool_step", "pe_step"))
        prep = sem("prep")
        stored = sem("stored")
        rel_mm, rel_sb, rel_out, tb_in = sem("rel_mm"), sem("rel_sb"), sem("rel_out"), sem("tb_in")
        g_pre, g_ln, g_rdy, g_tr, g_col, g_em = (sem(n) for n in ("g_pre", "g_ln", "g_rdy", "g_tr", "g_col", "g_em"))
        tok_v, tok_k, tok_kv = sem("tok_v"), sem("tok_k"), sem("tok_kv")
        tok_v_ev, tok_k_ev, tok_kv_ev = sem("tok_v_ev"), sem("tok_k_ev"), sem("tok_kv_ev")
        ml_s, ml_mb, ml_x, ml_w, ml_wm, ml_a = (sem(n) for n in ("ml_s", "ml_mb", "ml_x", "ml_w", "ml_wm", "ml_a"))
        ml_o, ml_n, ml_wv, ml_c, ml_ce = (sem(n) for n in ("ml_o", "ml_n", "ml_wv", "ml_c", "ml_ce"))
        ml_sd, ml_hn, ml_t, ml_mx = (sem(n) for n in ("ml_sd", "ml_hn", "ml_t", "ml_mx"))

        sd_in, sd_pe, sd_dve, sd_x, sd_e, sd_at = (sem(n) for n in ("sd_in", "sd_pe", "sd_dve", "sd_x", "sd_e", "sd_at"))
        sd_int, sd_iv, sd_hn, sd_vx, sd_u, sd_cn = (sem(n) for n in ("sd_int", "sd_iv", "sd_hn", "sd_vx", "sd_u", "sd_cn"))
        sd_end = sem("sd_end")
        np_kv, np_kvs, np_cs, np_cx, np_ce, np_ct = (sem(n) for n in ("np_kv", "np_kvs", "np_cs", "np_cx", "np_ce", "np_ct"))
        np_cv, np_z = sem("np_cv"), sem("np_z")
        np_s, np_x, np_e, np_t, np_te, np_o = (sem(n) for n in ("np_s", "np_x", "np_e", "np_t", "np_te", "np_o"))
        np_pv, sd_ir = sem("np_pv"), sem("sd_ir")
        st_cp, st_n, st_cs = sem("st_cp"), sem("st_n"), sem("st_cs")
        np_g, np_mt, np_mx = sem("np_g"), sem("np_mt"), sem("np_mx")
        xin2, hist = sem("xin2"), sem("hist")
        ln_r, ln_m, ln_c, ln_q, ln_v, ln_s, ln_h, ln_y = (sem(n) for n in (
            "ln_r", "ln_m", "ln_c", "ln_q", "ln_v", "ln_s", "ln_h", "ln_y"))
        f_u, f_conv, f_gelu, f_done, f_y = (sem(n) for n in ("f_u", "f_conv", "f_gelu", "f_done", "f_y"))
        attn_done = sem("attn_done")

        pg_land = [sem(f"pg_land{i}") for i in range(PAGE_RING)]
        wp_land = [sem(f"wp_land{i}") for i in range(2)]
        pg_used, nd_z, nd_qb, nd_pp, nd_pe, nd_vn = (sem(n) for n in ("pg_used", "nd_z", "nd_qb", "nd_pp", "nd_pe", "nd_vn"))
        nd_t, nd_te, nd_s, nd_se, nd_kve = (sem(n) for n in ("nd_t", "nd_te", "nd_s", "nd_se", "nd_kve"))
        nd_cx, nd_ce, nd_wx, nd_we, nd_sx, nd_sel = (sem(n) for n in ("nd_cx", "nd_ce", "nd_wx", "nd_we", "nd_sx", "nd_sel"))
        nd_pr, nd_im, nd_ie = (sem(n) for n in ("nd_pr", "nd_im", "nd_ie"))
        nd_p1, nd_p1e, nd_p2, nd_p2e = (sem(n) for n in ("nd_p1", "nd_p1e", "nd_p2", "nd_p2e"))
        nd_o1, nd_o2, nd_oa, nd_ot, nd_mx = (sem(n) for n in ("nd_o1", "nd_o2", "nd_oa", "nd_ot", "nd_mx"))
        NCONST = 16 * 9
        count = {"dve": 0, "act": 0, "pool": 0, "pe": 0}

        def step(eng, which, ins):
            s = {"dve": dve_step, "act": act_step, "pool": pool_step, "pe": pe_step}[which]
            count[which] += 1
            ins.then_inc(s, 1)
            eng.wait_ge(s, count[which])

        def landed(eng, i):
            eng.wait_ge(w_land[i % RING], 16 * (i // RING + 1))

        def by_sequence(buf, n, width):
            at = buf.shape[2] - NB * width
            return buf[:, n % buf.shape[1], at:at + NB * width].rearrange("p (b t) -> p b t", b=NB)

        def bc(ap, n):
            return ap.unsqueeze(len(ap.shape)).broadcast_to(list(ap.shape) + [n])

        ITEMS = [(a["w_in"], n, 1024) for n in range(ZT)] + [(a["w_out"], n, 1024) for n in range(KD)] \
            + [(a["w_up"], n, 1024) for n in range(UP)] \
            + [(a["w_down"], n, KP * 128) for n in range(KD * DOWN_PARTS)]
        I_OUT, I_UP, I_DOWN = ZT, ZT + KD, ZT + KD + UP

        def high(eng, out, src):
            return eng.activation(out, src, ACT.Copy)

        def low(eng, out, src, hi):
            return eng.tensor_tensor(out, src, hi.bitcast(F32), ALU.subtract)

        def split_hi(act, i):
            landed(act, i)
            if i >= 2:
                act.wait_ge(w_used, i - 1)
            w = ITEMS[i][2]
            high(act, whi[:, i % 2, 0:w], wring[:, i % RING, 0:w]).then_inc(w_hi, 1)

        def split_lo(dve, i):
            dve.wait_ge(w_hi, i + 1)
            w = ITEMS[i][2]
            low(dve, wring_r[:, i % RING, 0:w], wring[:, i % RING, 0:w],
                whi[:, i % 2, 0:w]).then_inc(w_lo, 1)

        block = ctx.enter_context(nc.Block())

        @block.sync
        def _(sp):
            def load_weights(i):
                if i >= RING:
                    sp.wait_ge(w_used, i - RING + 1)
                w, n, width = ITEMS[i]
                sp.dma_start(wring[:, i % RING, 0:width], w[n]).then_inc(w_land[i % RING], 16)

            for k in range(KD // 2):
                sp.dma_start(xt[:, 2 * k:2 * k + 2, :], a["xt"][:, 2 * k:2 * k + 2, :]).then_inc(xin[k], 16)
                if k in (0, 2):
                    load_weights(k // 2)
            for i in range(2, I_OUT):
                load_weights(i)
            sp.wait_ge(rel_sb, 1)
            sp.dma_start(relrow.ap(), ohp[0:8, NREL:2 * NREL].unsqueeze(1).broadcast_to([8, 128, NREL])).then_inc(rel_out, 16)
            sp.wait_ge(rel_out, 16)
            shifted = bass.AP(tensor=relrow, offset=127, ap=[[NREL - 1, 128], [128 * NREL, H], [1, 512]])
            sp.dma_start(tb, shifted).then_inc(tb_in, 16)
            sp.dma_start(a["out_win_s"], a["win"][:, TS:, :]).then_inc(stored, 16)
            sp.wait_ge(z_dve, ZT - Z_MV)
            sp.dma_start(a["out_zkv"], zt[:, Z_CK:ZT, :]).then_inc(stored, 16)
            sp.wait_ge(conv_done, Z_MO)
            sp.dma_start(a["out_mconv"], mc).then_inc(stored, 16)
            sp.wait_ge(g_rdy, 1)
            sp.dma_start(a["out_m_p"], lnb[:, T - 1:T]).then_inc(stored, 16)
            sp.wait_ge(stored, 48 + 16)
            sp.wait_ge(silu_done, Z_MO)
            sp.dma_start(cn, a["cn"]).then_inc(sd_in, 16)
            sp.dma_start(ntv, a["nt"]).then_inc(sd_in, 16)
            sp.wait_ge(ml_o, H)
            sp.dma_start(ctv, a["ct"]).then_inc(sd_in, 16)
            sp.wait_ge(ml_a, 4 * H)
            sp.dma_start(n0, a["n0"]).then_inc(sd_in, 16)
            sp.wait_ge(ml_ce, 1)
            sp.dma_start(a["out_c_p"], cout).then_inc(st_cp, 16)
            for i in range(I_OUT, I_OUT + RING):
                load_weights(i)
            sp.wait_ge(sd_dve, 4)
            sp.dma_start(a["out_m_s"], s32[:, 24:32]).then_inc(stored, 16)
            sp.wait_ge(sd_cn, 4)
            sp.dma_start(a["out_c_s"], cn).then_inc(st_cs, 16)
            sp.wait_ge(sd_end, 1)
            sp.dma_start(a["out_n_s"], n0).then_inc(st_n, 16)
            sp.wait_ge(sd_end, 2)
            for n in range(NB * PAGES):
                b, p = n // PAGES, n % PAGES
                if n == 0:
                    sp.wait_ge(np_mx, QT)
                if n >= PAGE_RING:
                    sp.wait_ge(pg_used, n - PAGE_RING + 1)
                if p == 0 and b >= 2:
                    sp.wait_ge(nd_o2, b - 1)
                if p == 0:
                    if b == 0:
                        sp.wait_ge(nd_pe, 4)
                    if b >= 2:
                        sp.wait_ge(nd_o1, b - 1)
                    sp.dma_start(wpage[:, b % 2], a["win"][b].rearrange("(k p) c -> p k c", k=4)).then_inc(wp_land[b % 2], 16)
                page = sp.value_load(ptab[0:1, n:n + 1], min_val=0, max_val=POOL_PAGES - 1)
                src = a["pool"][bass.DynSlice(page, 1), :, :].rearrange("a p c -> (a p) c")
                sp.dma_start(pages[:, n % PAGE_RING, :], src[:, 0:384]).then_inc(pg_land[n % PAGE_RING], 16)
                sp.dma_start(vsel[:, b % 2, p, :], src[:, 384:512]).then_inc(pg_land[n % PAGE_RING], 16)
            sp.wait_ge(attn_done, 1)
            for k in range(KD):
                sp.dma_start(xt[:, k, :], a["xt"][:, k, :]).then_inc(xin2, 16)
            sp.dma_start(hf, a["hf"]).then_inc(hist, 16)
            for i in range(I_OUT + RING, len(ITEMS)):
                load_weights(i)
            sp.wait_ge(f_conv, UP)
            sp.dma_start(a["out_fconv"], fc).then_inc(stored, 16)
            for m in range(KD):
                sp.wait_ge(ln_y, KD + m + 1)
                sp.dma_start(a["out_y"][:, m, :], xt[:, m, :]).then_inc(stored, 16)
            sp.wait_ge(stored, 16 * (6 + KD))
            for s in (st_cp, st_n, st_cs):
                sp.wait_ge(s, 16)

        @block.gpsimd
        def _(pool):
            pool.memset(uq[:, :, 0:3], 0.0).then_inc(prep, 1)
            pool.memset(ga[:, 0:T], 1.0).then_inc(prep, 1)
            pool.wait_ge(w_used, ZT)
            pool.memset(tv[:, :, :, HD:HD + 1], 1.0).then_inc(prep, 1)

            for u in range(4 * H):
                pool.wait_ge(ml_w, u + 1)
                pool.tensor_tensor(ww[:, u % 2, 0:128], ww[:, u % 2, 0:128], tri, ALU.mult).then_inc(ml_wm, 1)
            pool.wait_ge(st_cp, 16)
            pool.memset(scp, 0.0).then_inc(np_z, 1)
            pool.wait_ge(np_mx, QT)
            pool.memset(qb, 0.0).then_inc(nd_z, 1)
            pool.wait_ge(attn_done, 1)
            pool.wait_ge(hist, 16)
            pool.memset(uf[:, :, 0:2], 0.0).then_inc(prep, 1)

        @block.scalar
        def _(act):
            def link(ins):
                step(act, "act", ins)

            for dst, name in ((col, "cols"), (cst, "c128"), (c32, "c32"), (relp, "relp"), (ohp, "ohp"), (hm, "hm"),
                              (wpad, "wpad"), (ptab, "ptab"), (sm[0:32, 0:8], "m0")):
                act.dma_start(dst if name in ("ohp", "hm", "m0") else dst[tuple(slice(None) for _ in dst.shape)],
                              a[name]).then_inc(consts, 16)
            split_hi(act, 0)
            for k in range(KD):
                act.wait_ge(xin[k // 2], 16)
                high(act, arena_hi[:, k, :], xt[:, k, :]).then_inc(x_hi, 1)
            split_hi(act, 1)
            act.wait_ge(consts, NCONST)

            def silu(n):
                act.wait_ge(conv_done, n + 1)
                t = tq[:, n % 2, :]
                act.activation(zt[:, n, 0:T], t[:, 0:T], ACT.Silu)
                act.activation(zt[:, n, T:NT].rearrange("p (b t) -> p b t", b=NB),
                               by_sequence(tq, n, 7)[:, :, 0:TS], ACT.Silu).then_inc(silu_done, 1)

            for n in range(Z_MO):
                split_hi(act, n + 2)
                if n == 0:
                    act.wait_ge(prep, 1)
                if n >= 2:
                    act.wait_ge(conv_done, n - 1)
                u = uq[:, n % 2, :]
                us = u[:, 515:571].rearrange("p (b t) -> p b t", b=NB)
                act.activation(us[:, :, 0:3], hm[:, n, :].rearrange("p (b t) -> p b t", b=NB), ACT.Copy)
                act.activation(u[:, 3:515].rearrange("p (c t) -> p c t", c=2), q4[n % 2][:, :, 0:HALF],
                               ACT.Identity, bias=vec("b_in", n))
                act.activation(us[:, :, 3:7], q4[n % 2][:, 1, HALF:HALF + NS].rearrange("p (b t) -> p b t", b=NB),
                               ACT.Identity, bias=vec("b_in", n)).then_inc(z_act, 1)
                if n >= 1:
                    silu(n - 1)
            silu(Z_MO - 1)
            for n in range(Z_MO, Z_G + 1):
                split_hi(act, n + 2)
                if n < Z_G:
                    dst, src, b = zt[:, n, :], q4[n % 2], vec("b_in", n)
                else:
                    dst, src, b = gsig[:, :], q4[n % 2][G_N:G_N + 24], vec("b_in", n, G_N, G_N + 24)
                act.activation(dst[:, 0:T].rearrange("p (c t) -> p c t", c=2), src[:, :, 0:HALF],
                               ACT.Sigmoid, bias=b)
                act.activation(dst[:, T:NT], src[:, 1, HALF:HALF + NS], ACT.Sigmoid, bias=b).then_inc(z_act, 1)

            act.wait_ge(g_pre, 1)
            link(act.activation(lnb[:, :], gf[:, :], ACT.Abs))
            link(act.activation(lnb[:, :], lnb[:, :], ACT.Exp, scale=-1.0))
            act.activation(lnb[:, :], lnb[:, :], ACT.Ln, bias=1.0).then_inc(g_ln, 1)

            for n in range(Z_MV, ZT - 2):
                split_hi(act, n + 2)

            for i in range(QT + 1):
                n = 128 if i < QT else NS
                act.wait_ge(tok_k, i + 1)
                act.activation(tk[0:n, i, :], bank[5][0:n, :], ACT.Copy, scale=QS).then_inc(tok_k_ev, 1)
                act.wait_ge(tok_kv, i + 1)
                act.activation(tkv[0:n, i, :, :].rearrange("p k c -> p (k c)"), bank[7][0:n, :],
                               ACT.Copy).then_inc(tok_kv_ev, 1)

            act.wait_ge(g_col, 1)
            act.activation(emp[:, 0:32], gcol[:, 32:64], ACT.Exp, scale=-1.0)
            act.activation(emp[:, 32:64], emp[:, 32:64], ACT.Exp).then_inc(g_em, 1)

            for u in range(4 * H):
                act.wait_ge(ml_x, u + 1)
                n = T - 128 * (u % 4)
                act.activation(ww[:, u % 2, 0:n], ww[:, u % 2, 0:n], ACT.Exp, scale=-1.0).then_inc(ml_w, 1)
            act.wait_ge(ml_c, 1)
            act.activation(cout[:, :], bank[6][0:65, :], ACT.Copy).then_inc(ml_ce, 1)
            act.wait_ge(ml_n, H)
            act.activation(var[:, :], var[:, :], ACT.Sqrt, bias=epsc[:, :], scale=1.0 / HD).then_inc(ml_sd, 1)

            act.wait_ge(sd_x, 1)
            act.activation(gmk, gmk, ACT.Exp)
            act.wait_ge(sd_x, 2)
            act.activation(s32[:, 64:96], s32[:, 32:64], ACT.Exp).then_inc(sd_e, 1)
            act.wait_ge(sd_pe, 5)
            act.activation(at_sb, bank[4][0:32, 0:256], ACT.Copy).then_inc(sd_at, 1)
            act.wait_ge(sd_hn, 1)
            act.activation(s32[:, 120:128], s32[:, 120:128], ACT.Sqrt, bias=epsc[0:32, :], scale=1.0 / HD).then_inc(sd_at, 1)

            act.wait_ge(np_kv, 1)
            act.wait_ge(st_cp, 16)
            act.activation(kcp, bank[6][:, 0:16], ACT.Copy).then_inc(np_kvs, 1)

            def cmp_exp(i):
                act.wait_ge(np_cx, i + 1)
                act.activation(scp[:, :, 0:4 * i + 4], scp[:, :, 0:4 * i + 4], ACT.Exp).then_inc(np_ce, 1)
                act.wait_ge(np_ct, i + 1)
                if i >= 1:
                    act.wait_ge(np_o, i)
                act.activation(cpt, bank[7][:, 0:128], ACT.Copy).then_inc(np_cv, 1)

            def probs(n):
                i = n // 16
                act.wait_ge(np_x, n + 1)
                act.activation(pb[:, n % 2, 0:128 * i + 128], pb[:, n % 2, 0:128 * i + 128], ACT.Exp,
                               bias=mxs[:, n % 2:n % 2 + 1], accum_out=den[:, 1 + n // 8 % 2, n % 8:n % 8 + 1]).then_inc(np_e, 1)

            def probs_t(n):
                i = n // 16
                act.wait_ge(np_t, n + 1)
                if n >= 2:
                    act.wait_ge(np_pv, n - 1)
                act.activation(ptb[:, n % 2, 0:128 * i + 128], bank[2 + n % 2][:, 0:128 * i + 128],
                               ACT.Copy).then_inc(np_te, 1)

            for i in range(QT):
                cmp_exp(i)
                for n in range(16 * i, 16 * i + 17):
                    if n < 16 * i + 16:
                        probs(n)
                    if n > 16 * i:
                        probs_t(n - 1)
            for c in range(4):
                act.wait_ge(nd_pe, 4)
                act.activation(vn[:, 2 * c:2 * c + 2, :].rearrange("p b c -> p (b c)"), bank[4 + c][0:4, :],
                               ACT.Copy).then_inc(nd_vn, 1)

            def keys_t(b, u):
                n = 5 * b + u
                act.wait_ge(nd_t, n + 1)
                if n >= 2:
                    m = n - 2
                    act.wait_ge(nd_s, 6 * (m // 5) + (m % 5 + 1 if m % 5 < 4 else 6))
                act.activation(skt[:, n % 2, :], bank[n % 2], ACT.Copy).then_inc(nd_te, 1)

            def compressed(b):
                act.wait_ge(pg_used, PAGES * (b + 1))
                if b >= 1:
                    act.wait_ge(nd_o1, b)
                act.activation(kct, bank[6][:, 0:64], ACT.Copy)
                act.activation(vcs, bank[7][0:64, 0:128], ACT.Copy).then_inc(nd_kve, 1)

            def exps_cw(b):
                act.wait_ge(nd_cx, b + 1)
                act.activation(pc[:, b % 2, :], pc[:, b % 2, :], ACT.Exp, bias=st[:, 0:1],
                               accum_out=st[:, 1:2]).then_inc(nd_ce, 1)
                act.wait_ge(nd_wx, b + 1)
                act.activation(sw[:, b % 2, :], sw[:, b % 2, :], ACT.Exp, bias=st[:, 4:5],
                               accum_out=st[:, 5:6]).then_inc(nd_we, 1)

            def small_t(b):
                act.wait_ge(nd_p1, b + 1)
                act.activation(ptc, bank[4][0:64, 0:32], ACT.Copy)
                act.activation(ptw, bank[4][:, 32:160], ACT.Copy)
                act.activation(ptn[:, 32:64], bank[4][0:4, 160:192], ACT.Copy).then_inc(nd_p1e, 1)

            def exps_s(b):
                act.wait_ge(nd_sx, b + 1)
                act.activation(score[:, b % 2, :], score[:, b % 2, :], ACT.Exp, bias=st[:, 8:9],
                               accum_out=st[:, 9:10]).then_inc(nd_sel, 1)

            def selected_t(b):
                act.wait_ge(nd_p2, b + 1)
                act.activation(pts, bank[4], ACT.Copy)
                act.activation(ptn[:, 0:32], bank[5][0:4, 448:480], ACT.Copy).then_inc(nd_p2e, 1)

            for b in range(NB + 1):
                if b < NB:
                    keys_t(b, 0)
                if b >= 1:
                    small_t(b - 1)
                if b < NB:
                    keys_t(b, 1)
                if b >= 1:
                    exps_s(b - 1)
                if b < NB:
                    keys_t(b, 2)
                if b >= 1:
                    selected_t(b - 1)
                if b < NB:
                    keys_t(b, 3)
                    compressed(b)
                    keys_t(b, 4)
                    exps_cw(b)

            act.wait_ge(stored, 16 * 5)
            split_hi(act, I_OUT)
            split_hi(act, I_OUT + 1)
            act.wait_ge(attn_done, 1)
            for k in range(KD):
                high(act, arena_hi[:, k, :], mixt[:, k, :]).then_inc(m_hi, 1)
            for m in range(KD):
                split_hi(act, I_OUT + m + 2)

            def norm_act(base, w, b):
                for m in range(KD):
                    act.wait_ge(ln_c, base + m + 1)
                    if m >= 2 or base:
                        act.wait_ge(ln_v, base + m - 1)
                    act.activation(sqb[:, m % 2, :], xt[:, m, :], ACT.Square).then_inc(ln_q, 1)
                act.wait_ge(ln_v, base + KD)
                act.activation(rstd[:, 0:T].rearrange("p (c t) -> p c t", c=2), q4[3][:, :, 0:HALF], ACT.Sqrt,
                               bias=epsc[:, :])
                act.activation(rstd[:, T:NT], q4[3][:, 1, HALF:HALF + NS], ACT.Sqrt, bias=epsc[:, :]).then_inc(ln_s, 1)
                for m in range(KD):
                    act.wait_ge(ln_h, base + m + 1)
                    act.activation(xt[:, m, :], xt[:, m, :], ACT.Identity, bias=vec(b, m),
                                   scale=vec(w, m)).then_inc(ln_y, 1)
                    if base == 0:
                        act.wait_ge(ln_y, m + 1)
                        high(act, x1_hi[:, m, :], xt[:, m, :]).then_inc(y_hi, 1)

            norm_act(0, "ln1_w", "ln1_b")

            act.wait_ge(hist, 16)
            act.wait_ge(prep, 4)

            def gelu(i):
                act.wait_ge(f_conv, 2 * i + 1)
                t = tf[:, 2 * i % 4, 0:560]
                act.activation(t, t, ACT.Gelu_apprx_tanh).then_inc(f_gelu, 1)

            def gated_hi(i):
                act.wait_ge(f_done, i + 1)
                high(act, f_hi_of(i), zt[:, i, :]).then_inc(f_hi, 1)

            for n in range(UP):
                split_hi(act, I_UP + n + 2)
                if n >= 4:
                    act.wait_ge(f_conv, n - 3)
                u = uf[:, n % 4, :]
                us = by_sequence(uf, n, 6)
                act.activation(us[:, :, 0:2], hf[:, n, :].rearrange("p (b t) -> p b t", b=NB), ACT.Copy)
                act.activation(u[:, 2:514].rearrange("p (c t) -> p c t", c=2), q4[n % 2][:, :, 0:HALF],
                               ACT.Identity, bias=vec("b_up", n))
                act.activation(us[:, :, 2:6], q4[n % 2][:, 1, HALF:HALF + NS].rearrange("p (b t) -> p b t", b=NB),
                               ACT.Identity, bias=vec("b_up", n)).then_inc(f_u, 1)
                if n % 2 == 1:
                    gelu(n // 2)
                    if n >= 3:
                        gated_hi(n // 2 - 1)
            gated_hi(FT - 1)
            for m in range(KD):
                for c in range(DOWN_PARTS):
                    i = I_DOWN + DOWN_PARTS * m + c
                    if i + 2 < len(ITEMS):
                        split_hi(act, i + 2)
                act.wait_ge(w_used, I_DOWN + DOWN_PARTS * (m + 1))
                if m >= 2:
                    act.wait_ge(ln_r, KD + m - 1)
                act.activation(ybuf[:, m % 2, 0:T].rearrange("p (c t) -> p c t", c=2), q4[m % 2][:, :, 0:HALF],
                               ACT.Identity, bias=vec("b_down", m))
                act.activation(ybuf[:, m % 2, T:NT], q4[m % 2][:, 1, HALF:HALF + NS],
                               ACT.Identity, bias=vec("b_down", m)).then_inc(f_y, 1)
            norm_act(KD, "ln2_w", "ln2_b")

        @block.vector
        def _(dve):
            def link(ins):
                step(dve, "dve", ins)

            split_lo(dve, 0)
            for k in range(KD):
                dve.wait_ge(x_hi, k + 1)
                low(dve, xt_lo[:, k, :], xt[:, k, :], arena_hi[:, k, :]).then_inc(x_lo, 1)
            split_lo(dve, 1)
            dve.memset(epsc[:, :], EPS)
            dve.wait_ge(consts, NCONST)

            for n in range(Z_MO):
                split_lo(dve, n + 2)
                if n == 2:
                    dve.wait_ge(rel_mm, 1)
                    dve.tensor_tensor(ohp[0:8, NREL:2 * NREL].rearrange("p (c n) -> p c n", c=2),
                                      ohp[0:8, NREL:2 * NREL].rearrange("p (c n) -> p c n", c=2),
                                      q4[3][0:8, :, 0:NREL // 2], ALU.add).then_inc(rel_sb, 1)
                dve.wait_ge(z_act, n + 1)
                if n >= 2:
                    dve.wait_ge(silu_done, n - 1)
                u, t = uq[:, n % 2, :], tq[:, n % 2, 0:568]
                link(dve.tensor_scalar(t, u[:, 0:568], vec("mconv_w", n), vec("mconv_b", n), ALU.mult, ALU.add))
                for j in range(1, 3):
                    link(dve.scalar_tensor_tensor(out=t, in0=u[:, j:568 + j], scalar=vec("mconv_w", 8 * j + n),
                                                  in1=t, op0=ALU.mult, op1=ALU.add))
                dve.tensor_copy(mc[:, n, 0:3], u[:, 512:515])
                dve.tensor_copy(mc[:, n, 3:27].rearrange("p (b t) -> p b t", b=NB),
                                u[:, 515:571].rearrange("p (b t) -> p b t", b=NB)[:, :, 4:7])
                dve.scalar_tensor_tensor(out=t, in0=u[:, 3:571], scalar=vec("mconv_w", 24 + n),
                                         in1=t, op0=ALU.mult, op1=ALU.add).then_inc(conv_done, 1)

            for n in range(Z_MO, Z_G + 1):
                split_lo(dve, n + 2)
            dve.wait_ge(w_used, Z_G + 1)
            for dst, p in ((gi, G_I), (gf, G_F)):
                src, b = q4[Z_G % 2][p:p + 8], vec("b_in", Z_G, p, p + 8)
                dve.tensor_scalar(dst[:, 0:T].rearrange("p (c t) -> p c t", c=2), src[:, :, 0:HALF], b, None, ALU.add)
                last = dve.tensor_scalar(dst[:, T:NT], src[:, 1, HALF:HALF + NS], b, None, ALU.add)
            last.then_inc(g_pre, 1)
            dve.wait_ge(g_ln, 1)
            dve.wait_ge(g_pre, 1)
            link(dve.scalar_tensor_tensor(out=gf[:, :], in0=gf[:, :], scalar=0.0, in1=lnb[:, :],
                                          op0=ALU.min, op1=ALU.subtract))
            dve.wait_ge(prep, 2)
            link(dve.tensor_tensor_scan(out=lnb[:, 0:T], data0=ga[:, 0:T], data1=gf[:, 0:T], initial=0.0,
                                        op0=ALU.mult, op1=ALU.add))
            link(dve.tensor_tensor(gi[:, 0:T], gi[:, 0:T], lnb[:, 0:T], ALU.subtract))
            link(dve.tensor_tensor_scan(out=gm[:, :], data0=ga[:, 0:T], data1=gi[:, 0:T], initial=0.0,
                                        op0=ALU.mult, op1=ALU.max))
            dve.tensor_scalar(ga[:, 512:520], ident[0:8, 0:8], gm[:, T - 1:T], None, ALU.mult)
            dve.tensor_tensor(lnb[:, 0:T], lnb[:, 0:T], gm[:, :], ALU.add).then_inc(g_rdy, 1)

            for n in range(Z_MV, ZT):
                if n + 2 < ZT:
                    split_lo(dve, n + 2)
                dve.wait_ge(w_used, n + 1)
                s2 = QS if Z_NQ <= n < Z_CK else 1.0
                dve.tensor_scalar(zt[:, n, 0:T].rearrange("p (c t) -> p c t", c=2), q4[n % 2][:, :, 0:HALF],
                                  vec("b_in", n), s2, ALU.add, ALU.mult)
                dve.tensor_scalar(zt[:, n, T:NT], q4[n % 2][:, 1, HALF:HALF + NS], vec("b_in", n), s2,
                                  ALU.add, ALU.mult).then_inc(z_dve, 1)

            dve.wait_ge(g_tr, 1)
            dve.tensor_copy(gcol[:, 0:72], bank[6][:, 0:72])
            dve.tensor_copy(gcol[0:32, 72:88], bank[6][0:32, 72:88])
            dve.tensor_copy(gcol[:, 96:192], bank[6][:, 96:192])
            link(dve.tensor_copy(gcol[0:32, 192:216], bank[6][0:32, 192:216]))
            dve.tensor_tensor(emp[:, 32:64].rearrange("p (i h) -> p i h", i=QT),
                              gcol[:, 0:32].rearrange("p (i h) -> p i h", i=QT),
                              gcol[:, 64:72].unsqueeze(1).broadcast_to([128, QT, 8]), ALU.subtract).then_inc(g_col, 1)

            dve.wait_ge(prep, 3)
            for i in range(QT + 1):
                dve.wait_ge(tok_v, i + 1)
                if i < QT:
                    dve.tensor_copy(tv[:, i, :, 0:HD], bank[4].rearrange("p (h c) -> p h c", h=H)).then_inc(tok_v_ev, 1)
                else:
                    dve.tensor_copy(tvs, bank[4][0:NS, :]).then_inc(tok_v_ev, 1)

            def weights(u):
                h, i = u // 4, u % 4
                if i == 0:
                    dve.wait_ge(ml_mb, h + 1)
                if u >= 2:
                    dve.wait_ge(ml_a, u - 1)
                dve.tensor_scalar(ww[:, u % 2, 0:T - 128 * i], bank[2 + h % 2][:, 128 * i:T],
                                  gcol[:, 8 * i + h:8 * i + h + 1], 0.0, ALU.subtract, ALU.max).then_inc(ml_x, 1)

            def products(u):
                h, i = u // 4, u % 4
                dve.wait_ge(ml_s, u + 1)
                dve.wait_ge(ml_wm, u + 1)
                if i == 0 and h >= 2:
                    dve.wait_ge(ml_o, h - 1)
                at = (0, 512, 896, 1152)[i]
                dve.scalar_tensor_tensor(out=aw[:, h % 2, at:at + T - 128 * i], in0=bank[u % 2][:, 0:T - 128 * i],
                                         scalar=QS, in1=ww[:, u % 2, 0:T - 128 * i],
                                         op0=ALU.mult, op1=ALU.mult).then_inc(ml_a, 1)

            def normed(h):
                dve.wait_ge(ml_o, h + 1)
                o = bank[4 + h % 2][:, 0:260].rearrange("p (j c) -> p j c", j=QT)
                link(dve.tensor_scalar(s4[:, 0:4], o[:, :, HD], -1.0, None, ALU.mult))
                link(dve.tensor_tensor(s4[:, 0:4], s4[:, 0:4], o[:, :, HD], ALU.max))
                link(dve.tensor_tensor(s4[:, 0:4], s4[:, 0:4],
                                       emp[:, 0:32].rearrange("p (j h) -> p j h", j=QT)[:, :, h], ALU.max))
                link(dve.reciprocal(s4[:, 4:8], s4[:, 0:4]))
                hv = hc[:, :, h, :]
                link(dve.tensor_tensor(hv, o[:, :, 0:HD], bc(s4[:, 4:8], HD), ALU.mult))
                link(dve.tensor_reduce(s4[:, 0:4], hv, AX, ALU.add))
                link(dve.scalar_tensor_tensor(out=hv, in0=bc(s4[:, 0:4], HD), scalar=-1.0 / HD, in1=hv,
                                              op0=ALU.mult, op1=ALU.add))
                link(dve.tensor_tensor(sq[:, :, :], hv, hv, ALU.mult))
                dve.tensor_reduce(var[:, :].rearrange("p (j h) -> p j h", j=QT)[:, :, h], sq[:, :, :],
                                  AX, ALU.add).then_inc(ml_n, 1)

            dve.wait_ge(g_em, 1)
            dve.wait_ge(tok_v_ev, QT)
            for i in range(QT):
                dve.tensor_tensor(wv[:, i, :, :], tv[:, i, :, :], bc(emp[:, 32 + 8 * i:40 + 8 * i], HD + 1),
                                  ALU.mult).then_inc(ml_wv, 1)
            for u in range(4 * H + 1):
                if u < 4 * H:
                    weights(u)
                if u >= 1:
                    products(u - 1)
                if u % 4 == 3 and u >= 7:
                    normed(u // 4 - 1)
            normed(H - 1)
            dve.wait_ge(ml_sd, 1)
            link(dve.reciprocal(var[:, :], var[:, :]))
            dve.tensor_tensor(hc[:, :, :, :].rearrange("p j h d -> p (j h) d"),
                              hc[:, :, :, :].rearrange("p j h d -> p (j h) d"), bc(var[:, :], HD),
                              ALU.mult).then_inc(ml_hn, 1)
            for t in range(4):
                dve.wait_ge(ml_t, t + 1)
                dve.scalar_tensor_tensor(out=mixt[:, t, 0:T], in0=bank[t % 2], scalar=vec("norm_w", t),
                                         in1=zt[:, Z_MO + t, 0:T], op0=ALU.mult, op1=ALU.mult).then_inc(ml_mx, 1)

            s = lambda c: s32[:, 8 * c:8 * c + 8]
            F_, G_, M_, MT, X1, X3, X4, XN, WI, WKE, SCE, EM, DN, QN, T1, VS = (s(c) for c in range(16))
            dve.wait_ge(sd_pe, 1)
            link(dve.tensor_copy(F_, bank[7][0:32, 0:8]))
            link(dve.tensor_tensor(G_, gcol[0:32, 72:80], F_, ALU.subtract))
            g3 = gd.rearrange("p (h s) -> p h s", h=H)
            w3 = gmk.rearrange("p (h s) -> p h s", h=H)
            dve.tensor_tensor(g3, bc(G_, 32), ident[0:32, 0:32].unsqueeze(1).broadcast_to([32, 8, 32]),
                              ALU.mult).then_inc(sd_dve, 1)
            dve.wait_ge(sd_pe, 2)
            link(dve.tensor_tensor(w3, bank[7][0:32, 64:320].rearrange("p (h s) -> p h s", h=H),
                                   k32("maskb").unsqueeze(1).broadcast_to([32, 8, 32]), ALU.add))
            link(dve.tensor_reduce(M_, w3, AX, ALU.max))
            dve.tensor_tensor(M_, M_, m0, ALU.max).then_inc(sd_dve, 1)
            dve.wait_ge(sd_dve, 2)
            dve.tensor_tensor(w3, w3, bc(M_, 32), ALU.subtract).then_inc(sd_x, 1)
            link(dve.tensor_tensor(MT, F_, M_, ALU.add))
            dve.tensor_tensor(X1, m0, M_, ALU.subtract)
            dve.tensor_scalar(XN, MT, -1.0, None, ALU.mult)
            dve.wait_ge(sd_pe, 4)
            dve.tensor_tensor(X3, G_, bank[7][0:32, 8:16], ALU.subtract)
            dve.tensor_tensor(X4, m0, bank[7][0:32, 8:16], ALU.subtract).then_inc(sd_x, 1)
            dve.wait_ge(sd_e, 1)
            dve.wait_ge(sd_pe, 3)
            dve.scalar_tensor_tensor(out=aa, in0=bank[5][0:32, 0:256], scalar=QS, in1=gmk,
                                     op0=ALU.mult, op1=ALU.mult).then_inc(sd_dve, 1)
            dve.tensor_tensor(wvs.rearrange("p (h d) -> p h d", h=H), tvs.rearrange("p (h d) -> p h d", h=H),
                              bc(WKE, HD), ALU.mult)
            dve.tensor_tensor(wks.rearrange("p (h d) -> p h d", h=H), tk[0:32, QT, :].rearrange("p (h d) -> p h d", h=H),
                              bc(WKE, HD), ALU.mult).then_inc(sd_dve, 1)
            dve.wait_ge(sd_dve, 4)
            dve.tensor_reduce(DN, aa.rearrange("p (h s) -> p h s", h=H), AX, ALU.add)
            q8 = tmp[:, 0, :].rearrange("p (h b) -> p h b", h=H)
            link(dve.tensor_tensor(q8, bank[5][0:32, 256:320].rearrange("p (h b) -> p h b", h=H),
                                   k32("bm").unsqueeze(1).broadcast_to([32, 8, 8]), ALU.mult))
            link(dve.tensor_reduce(QN, q8, AX, ALU.add))
            link(dve.tensor_tensor(QN, QN, WI, ALU.mult))
            dve.tensor_tensor(DN, DN, QN, ALU.add).then_inc(sd_dve, 1)
            for h in range(H):
                dve.wait_ge(sd_int, h + 1)
                if h >= 1:
                    dve.wait_ge(sd_ir, h)
                ins = dve.tensor_tensor(tmp, bank[2 + h % 2][0:32, :].rearrange("p (b e) -> p b e", b=NB),
                                        bc(k32("bm"), HD), ALU.mult)
                ins.then_inc(sd_iv, 1)
                dve.wait_ge(sd_iv, h + 1)
                dve.tensor_reduce(inter[:, h, :], tmp.rearrange("p b e -> p e b"), AX, ALU.add).then_inc(sd_ir, 1)
            dve.wait_ge(sd_ir, H)
            link(dve.tensor_tensor(inter, inter, bc(WI, HD), ALU.mult))
            dve.wait_ge(sd_pe, 6)
            link(dve.tensor_tensor(hcs, inter, bank[6][0:32, :].rearrange("p (h d) -> p h d", h=H), ALU.add))
            dve.wait_ge(sd_dve, 5)
            link(dve.tensor_scalar(T1, DN, -1.0, None, ALU.mult))
            link(dve.tensor_tensor(T1, T1, DN, ALU.max))
            link(dve.tensor_tensor(T1, T1, EM, ALU.max))
            link(dve.reciprocal(T1, T1))
            link(dve.tensor_tensor(hcs, hcs, bc(T1, HD), ALU.mult))
            link(dve.tensor_reduce(T1, hcs, AX, ALU.add))
            link(dve.scalar_tensor_tensor(out=hcs, in0=bc(T1, HD), scalar=-1.0 / HD, in1=hcs,
                                          op0=ALU.mult, op1=ALU.add))
            link(dve.tensor_tensor(sqs, hcs, hcs, ALU.mult))
            dve.tensor_reduce(VS, sqs, AX, ALU.add).then_inc(sd_hn, 1)
            dve.wait_ge(sd_pe, 7)
            dve.tensor_copy(scb, bank[7][:, 320:352])
            link(dve.tensor_copy(sc8[:, :], bank[7][0:8, 352:360]))
            dve.wait_ge(sd_in, 64)

            def expand(bp):
                if bp >= 2:
                    dve.wait_ge(sd_u, bp - 1)
                for b2 in range(2):
                    b = 2 * bp + b2
                    last = dve.tensor_scalar(vexp[:, bp % 2].rearrange("p (h b e) -> p h b e", h=H, b=2)[:, :, b2, :],
                                             wvs.rearrange("p (h e) -> p h e", h=H), k32("bm")[:, b:b + 1], None, ALU.mult)
                last.then_inc(sd_vx, 1)

            expand(0)
            expand(1)
            n3 = n0.rearrange("p (h d) -> p h d", h=H)
            link(dve.tensor_tensor(n3, n3, bc(sc8[:, :], HD), ALU.mult))
            dve.wait_ge(sd_pe, 8)
            dve.tensor_tensor(n3, n3, bank[5][0:8, :].rearrange("p (h d) -> p h d", h=H), ALU.add).then_inc(sd_end, 1)
            for bp in range(4):
                link(dve.tensor_tensor(cn[:, bp], cn[:, bp], bc(scb[:, 8 * bp:8 * bp + 8], HD), ALU.mult))
                dve.wait_ge(sd_u, bp + 1)
                dve.tensor_tensor(cn[:, bp], cn[:, bp], bank[2 + bp % 2].rearrange("p (h d) -> p h d", h=H),
                                  ALU.add).then_inc(sd_cn, 1)
                if bp + 2 < 4:
                    expand(bp + 2)
            dve.wait_ge(sd_at, 2)
            link(dve.reciprocal(VS, VS))
            dve.tensor_tensor(hcs, hcs, bc(VS, HD), ALU.mult).then_inc(sd_hn, 1)
            dve.wait_ge(sd_pe, 9)
            for t in range(4):
                last = dve.scalar_tensor_tensor(out=mixt[:, t, T:NT], in0=bank[4][:, 32 * t:32 * t + 32],
                                                scalar=vec("norm_w", t), in1=zt[:, Z_MO + t, T:NT],
                                                op0=ALU.mult, op1=ALU.mult)
            last.then_inc(sd_end, 1)

            dve.wait_ge(np_kv, 1)
            dve.tensor_tensor(vblk, bank[7][:, 0:HD].unsqueeze(1).broadcast_to([128, H, HD]),
                              bc(k128("hblk"), HD), ALU.mult).then_inc(np_kvs, 1)
            dve.wait_ge(tb_in, 16)
            dve.wait_ge(np_z, 1)
            dve.wait_ge(st_n, 16)

            def cmp_scores(i):
                n, x0 = 4 * i + 4, 415 - 128 * i
                dve.wait_ge(np_cs, i + 1)
                if i >= 1:
                    dve.wait_ge(np_ct, i)
                v = scp[:, :, 0:n]
                link(dve.tensor_tensor(v, bank[6][:, 0:128].rearrange("p (h c) -> p h c", h=H)[:, :, 0:n],
                                       tb[:, :, x0:x0 + 32 * (n - 1) + 1:32], ALU.add))
                link(dve.tensor_reduce(cmx, v, AX, ALU.max))
                link(dve.tensor_scalar(cmx, cmx, FLOOR, None, ALU.max))
                dve.tensor_tensor(v, v, bc(cmx, n), ALU.subtract).then_inc(np_cx, 1)

            def logits(n):
                i, h = n // 16, n % 8
                w = 128 * i + 128
                dve.wait_ge(np_s, n + 1)
                if n >= 2:
                    dve.wait_ge(np_t, n - 1)
                link(dve.tensor_tensor_reduce(out=pb[:, n % 2, 0:w], in0=bank[n % 2][:, 0:w],
                                              in1=tb[:, h, 384 - 128 * i:512], scale=1.0, scalar=-3e38,
                                              op0=ALU.add, op1=ALU.max, accum_out=mxs[:, 2 + n % 2:3 + n % 2]))
                dve.tensor_scalar(mxs[:, n % 2:n % 2 + 1], mxs[:, 2 + n % 2:3 + n % 2], -1.0, None,
                                  ALU.mult).then_inc(np_x, 1)

            def gated(i, k):
                o = bank[4 + (3 * i + k) % 2].rearrange("p (g j d) -> p g j d", g=NG, j=GQ)
                by_head = lambda m: m.rearrange("p (j g d) -> p g j d", j=GQ, g=NG)
                scale = bc(gsc.rearrange("p (g j) -> p g j", g=NG), HD)
                if k == 0:
                    dve.wait_ge(np_ce, i + 1)
                    link(dve.tensor_reduce(den[:, 0, :], scp[:, :, 0:4 * i + 4], AX, ALU.add))
                    link(dve.tensor_scalar(den[:, 0, :], den[:, 0, :], DEN_MIN, None, ALU.max))
                else:
                    dve.wait_ge(np_e, 16 * i + 8 * k)
                link(dve.reciprocal(gsc, den[:, k, :]))
                link(dve.tensor_tensor(gsc, gsc, gcol[:, 96 + 24 * i + 8 * k:104 + 24 * i + 8 * k], ALU.mult))
                if k == 0:
                    dve.wait_ge(np_o, i + 1)
                else:
                    dve.wait_ge(np_pv, 16 * i + 8 * k)
                if k == 0:
                    if i >= 1:
                        dve.wait_ge(np_mt, i)
                    dve.tensor_tensor(by_head(mxa), o, scale, ALU.mult).then_inc(np_g, 1)
                else:
                    dve.wait_ge(np_g, 3 * i + k)
                    link(dve.tensor_tensor(by_head(mxt), o, scale, ALU.mult))
                    dve.tensor_tensor(mxa, mxa, mxt, ALU.add).then_inc(np_g, 1)

            def mixed(i):
                dve.wait_ge(np_mt, i + 1)
                dve.tensor_copy(mixt[:, 4:8, 128 * i:128 * i + 128],
                                bank[6].rearrange("p (j t) -> p j t", j=4)).then_inc(np_mx, 1)

            for i in range(QT):
                cmp_scores(i)
                for n in range(16 * i, 16 * i + 16):
                    logits(n)
                    if n % 16 == 2:
                        gated(i, 0)
                    if n % 16 == 10:
                        gated(i, 1)
                gated(i, 2)
                mixed(i)
            dve.wait_ge(nd_z, 1)
            for g in range(NG):
                p = slice(64 * g, 64 * g + 64)
                last = dve.tensor_copy(qb[p, :, 16 * g:16 * g + 16].rearrange("p b (j q) -> p b j q", j=GQ),
                                       zt[p, Z_NQ:Z_NQ + 4, T:NT].rearrange("p j (b q) -> p b j q", b=NB))
            last.then_inc(nd_qb, 1)
            dve.wait_ge(nd_pe, 1)
            dve.tensor_tensor(biasw[:, 0:512], bank[0][0:32, :], k32("maskw")[:, 0:512], ALU.add)
            dve.wait_ge(nd_pe, 2)
            dve.tensor_tensor(biasw[:, 512:516], bank[1][0:32, 0:4], k32("maskw")[:, 512:516], ALU.add)
            dve.tensor_copy(biasc, bank[1][0:32, 4:68])
            dve.wait_ge(nd_pe, 3)
            link(dve.tensor_tensor(gtmp.rearrange("p (n h) -> p n h", h=H),
                                   bank[2][0:32, 0:192].rearrange("p (n h) -> p n h", h=H),
                                   k32("headmask").unsqueeze(1).broadcast_to([32, 24, H]), ALU.mult))
            dve.tensor_reduce(gr, gtmp.rearrange("p (n h) -> p n h", h=H), AX, ALU.add).then_inc(nd_pp, 1)
            dve.wait_ge(nd_pp, 1)

            def page_scores(b, u):
                dve.wait_ge(nd_s, 6 * b + u + 1)
                if u == 0 and b >= 2:
                    dve.wait_ge(nd_p2, b - 1)
                ps = bank[2 + (6 * b + u) % 2][0:32, :]
                if u < 3:
                    dve.tensor_scalar(score[:, b % 2, 512 * u:512 * u + 512], ps, biasw[:, 100:101], None,
                                      ALU.add).then_inc(nd_se, 1)
                else:
                    dve.tensor_scalar(score[:, b % 2, 1536:1920], ps[:, 0:384], biasw[:, 100:101], None, ALU.add)
                    dve.tensor_tensor(score[:, b % 2, 1920:2048], ps[:, 384:512], biasw[:, 384:512],
                                      ALU.add).then_inc(nd_se, 1)

            def other_scores(b):
                dve.wait_ge(nd_s, 6 * b + 5)
                if b >= 2:
                    dve.wait_ge(nd_p1, b - 1)
                ps = bank[2 + 6 * b % 2][0:32, :]
                dve.tensor_tensor(score[:, b % 2, 2048:2052], ps[:, 0:4], biasw[:, 512:516], ALU.add)
                dve.tensor_tensor(sw[:, b % 2, 512:516], ps[:, 4:8], biasw[:, 512:516], ALU.add)
                link(dve.tensor_tensor(pc[:, b % 2, :], ps[:, 8:72], biasc, ALU.add))
                link(dve.tensor_reduce(st[:, 2:3], pc[:, b % 2, :], AX, ALU.max))
                dve.tensor_scalar(st[:, 0:1], st[:, 2:3], -1.0, None, ALU.mult).then_inc(nd_cx, 1)
                dve.wait_ge(nd_s, 6 * b + 6)
                dve.tensor_tensor(sw[:, b % 2, 0:512], bank[2 + (6 * b + 1) % 2][0:32, :], biasw[:, 0:512],
                                  ALU.add).then_inc(nd_se, 2)
                dve.wait_ge(nd_se, 6 * b + 6)
                link(dve.tensor_reduce(st[:, 6:7], sw[:, b % 2, :], AX, ALU.max))
                dve.tensor_scalar(st[:, 4:5], st[:, 6:7], -1.0, None, ALU.mult).then_inc(nd_wx, 1)

            def importance(b):
                dve.wait_ge(nd_ce, b + 1)
                link(dve.reciprocal(st[:, 3:4], st[:, 1:2]))
                link(dve.tensor_scalar(pc[:, b % 2, :], pc[:, b % 2, :], st[:, 3:4], None, ALU.mult))
                dve.tensor_reduce(pair, pc[:, b % 2, :].rearrange("p (n r) -> p n r", r=2), AX,
                                  ALU.add).then_inc(nd_pr, 1)

            def select(b):
                dve.wait_ge(nd_im, b + 1)
                dve.tensor_copy(impt, bank[5][0:32, 384:416]).then_inc(nd_ie, 1)
                dve.wait_ge(nd_ie, b + 1)
                by_i, by_j = impt.unsqueeze(1).broadcast_to([32, NBLK, NBLK]), bc(impt, NBLK)
                dve.tensor_tensor(rk1, by_i, by_j, ALU.is_gt)
                link(dve.tensor_tensor(rk2, by_i, by_j, ALU.is_equal))
                link(dve.tensor_tensor(rk2, rk2, k32("tie").rearrange("p (j i) -> p j i", j=NBLK), ALU.mult))
                link(dve.tensor_tensor(rk1, rk1, rk2, ALU.add))
                link(dve.tensor_reduce(rank, rk1, AX, ALU.add))
                link(dve.tensor_scalar(rank, rank, TOPK - 1.5, NEG, ALU.is_gt, ALU.mult))
                s3 = score[:, b % 2, 0:PAST].rearrange("p (n c) -> p n c", n=NBLK)
                link(dve.tensor_tensor(s3, s3, bc(rank, PAST // NBLK), ALU.add))
                link(dve.tensor_reduce(st[:, 10:11], score[:, b % 2, :], AX, ALU.max))
                dve.tensor_scalar(st[:, 8:9], st[:, 10:11], -1.0, None, ALU.mult).then_inc(nd_sx, 1)

            def combine(b):
                g = lambda k: gr[:, 3 * b + k:3 * b + k + 1]
                dve.wait_ge(nd_we, b + 1)
                dve.wait_ge(nd_o2, b + 1)
                link(dve.tensor_scalar(oacc, bank[5][0:32, 256:384], g(0), None, ALU.mult))
                dve.reciprocal(st[:, 7:8], st[:, 5:6])
                dve.wait_ge(nd_sel, b + 1)
                link(dve.reciprocal(st[:, 11:12], st[:, 9:10]))
                dve.tensor_tensor(st[:, 7:8], st[:, 7:8], g(2), ALU.mult)
                link(dve.tensor_tensor(st[:, 11:12], st[:, 11:12], g(1), ALU.mult))
                for c, k in ((128, 7), (0, 11)):
                    link(dve.tensor_scalar(otmp, bank[5][0:32, c:c + 128], st[:, k:k + 1], None, ALU.mult))
                    ins = dve.tensor_tensor(oacc, oacc, otmp, ALU.add)
                    if k == 7:
                        link(ins)
                ins.then_inc(nd_oa, 1)

            def to_mix(b):
                dve.wait_ge(nd_ot, b + 1)
                for g in range(NG):
                    p = slice(64 * g, 64 * g + 64)
                    last = dve.tensor_copy(mixt[p, 4:8, T + TS * b:T + TS * b + TS],
                                           bank[5][p, 416 + 16 * g:432 + 16 * g].rearrange("p (j q) -> p j q", j=GQ))
                last.then_inc(nd_mx, 1)

            for b in range(NB + 1):
                if b < NB:
                    page_scores(b, 0)
                if b >= 1:
                    select(b - 1)
                if b < NB:
                    page_scores(b, 1)
                    page_scores(b, 2)
                if b >= 1:
                    combine(b - 1)
                if b < NB:
                    page_scores(b, 3)
                    other_scores(b)
                    importance(b)
                if b >= 1:
                    to_mix(b - 1)
            dve.wait_ge(nd_mx, NB)
            dve.tensor_copy(st[:, 12:13], st[:, 11:12]).then_inc(attn_done, 1)

            split_lo(dve, I_OUT)
            split_lo(dve, I_OUT + 1)
            for k in range(KD):
                dve.wait_ge(m_hi, k + 1)
                low(dve, mixt_lo[:, k, :], mixt[:, k, :], arena_hi[:, k, :]).then_inc(m_lo, 1)

            def norm_dve(base):
                for m in range(KD):
                    if base == 0:
                        split_lo(dve, I_OUT + m + 2)
                        dve.wait_ge(w_used, I_OUT + m + 1)
                        dve.wait_ge(xin2, 16 * KD)
                        dve.scalar_tensor_tensor(out=xt[:, m, 0:T].rearrange("p (c t) -> p c t", c=2),
                                                 in0=xt[:, m, 0:T].rearrange("p (c t) -> p c t", c=2), scalar=ALPHA,
                                                 in1=q4[m % 2][:, :, 0:HALF], op0=ALU.mult, op1=ALU.add)
                        dve.scalar_tensor_tensor(out=xt[:, m, T:NT], in0=xt[:, m, T:NT], scalar=ALPHA,
                                                 in1=q4[m % 2][:, 1, HALF:HALF + NS], op0=ALU.mult,
                                                 op1=ALU.add).then_inc(ln_r, 1)
                    else:
                        for c in range(DOWN_PARTS):
                            i = I_DOWN + DOWN_PARTS * m + c
                            if i + 2 < len(ITEMS):
                                split_lo(dve, i + 2)
                        dve.wait_ge(f_y, m + 1)
                        link(dve.tensor_tensor(xt[:, m, :], xt_lo[:, m, :].bitcast(F32), x1_hi[:, m, :].bitcast(F32), ALU.add))
                        dve.scalar_tensor_tensor(out=xt[:, m, :], in0=xt[:, m, :], scalar=ALPHA,
                                                 in1=ybuf[:, m % 2, :], op0=ALU.mult, op1=ALU.add).then_inc(ln_r, 1)
                dve.wait_ge(ln_m, base // KD + 1)
                for m in range(KD):
                    dve.tensor_tensor(xt[:, m, 0:T].rearrange("p (c t) -> p c t", c=2),
                                      xt[:, m, 0:T].rearrange("p (c t) -> p c t", c=2), q4[2][:, :, 0:HALF],
                                      ALU.subtract)
                    dve.tensor_tensor(xt[:, m, T:NT], xt[:, m, T:NT], q4[2][:, 1, HALF:HALF + NS],
                                      ALU.subtract).then_inc(ln_c, 1)
                dve.wait_ge(ln_s, base // KD + 1)
                link(dve.reciprocal(rstd, rstd))
                dve.wait_ge(ln_q, base + KD)
                for m in range(KD):
                    dve.tensor_tensor(xt[:, m, :], xt[:, m, :], rstd, ALU.mult).then_inc(ln_h, 1)

            norm_dve(0)
            for m in range(KD):
                dve.wait_ge(y_hi, m + 1)
                low(dve, xt_lo[:, m, :], xt[:, m, :], x1_hi[:, m, :]).then_inc(y_lo, 1)

            def gated_lo(i):
                dve.wait_ge(f_hi, i + 1)
                low(dve, zt_lo[:, i, :], zt[:, i, :], f_hi_of(i)).then_inc(f_lo, 1)

            def gate(i):
                dve.wait_ge(f_gelu, i + 1)
                dve.wait_ge(f_conv, 2 * i + 2)
                t1, t2 = tf[:, 2 * i % 4, :], tf[:, (2 * i + 1) % 4, :]
                s1, s2 = (by_sequence(tf, n, 6)[:, :, 0:TS] for n in (2 * i, 2 * i + 1))
                dve.tensor_tensor(zt[:, i, 0:T], t1[:, 0:T], t2[:, 0:T], ALU.mult)
                dve.tensor_tensor(zt[:, i, T:NT].rearrange("p (b t) -> p b t", b=NB), s1, s2,
                                  ALU.mult).then_inc(f_done, 1)

            for n in range(UP):
                split_lo(dve, I_UP + n + 2)
                dve.wait_ge(f_u, n + 1)
                u, t = uf[:, n % 4, :], tf[:, n % 4, 0:560]
                link(dve.tensor_scalar(t, u[:, 0:560], vec("fconv_w", n), vec("fconv_b", n), ALU.mult, ALU.add))
                link(dve.scalar_tensor_tensor(out=t, in0=u[:, 1:561], scalar=vec("fconv_w", UP + n),
                                              in1=t, op0=ALU.mult, op1=ALU.add))
                dve.tensor_copy(fc[:, n, 0:2], u[:, 512:514])
                dve.tensor_copy(fc[:, n, 2:18].rearrange("p (b t) -> p b t", b=NB), by_sequence(uf, n, 6)[:, :, 4:6])
                dve.scalar_tensor_tensor(out=t, in0=u[:, 2:562], scalar=vec("fconv_w", 2 * UP + n),
                                         in1=t, op0=ALU.mult, op1=ALU.add).then_inc(f_conv, 1)
                if n % 2 == 0 and n >= 2:
                    gate(n // 2 - 1)
                    if n >= 4:
                        gated_lo(n // 2 - 2)
            gate(FT - 1)
            gated_lo(FT - 2)
            gated_lo(FT - 1)
            norm_dve(KD)

        @block.tensor
        def _(pe):
            def project(out, first, parts, hi, lo, kt, split=None):
                for c in range(parts):
                    i = first + c
                    pe.wait_ge(w_lo, i + 1)
                    for k in range(kt):
                        kk = c * kt + k
                        if split is not None:
                            pe.wait_ge(split, kk + 1)
                        wh = whi[:, i % 2, 128 * k:128 * k + 128]
                        wl = wring_r[:, i % RING, 128 * k:128 * k + 128]
                        end = kk == parts * kt - 1
                        for n, (w, x) in enumerate(((wh, hi(kk)), (wh, lo(kk)), (wl, hi(kk)))):
                            pe.matmul(out[:, 0, 0:HALF], w, x[:, 0:HALF], start=(kk == 0 and n == 0),
                                      stop=(end and n == 2))
                            mm = pe.matmul(out[:, 1, 0:HALF + NS], w, x[:, HALF:NT], start=(kk == 0 and n == 0),
                                           stop=(end and n == 2))
                    mm.then_inc(w_used, 1)

            def by_k(t):
                return lambda k: t[:, k, :]

            for n in range(ZT):
                if 2 <= n <= Z_G + 2:
                    pe.wait_ge(z_act, n - 1)
                if n == Z_G + 2:
                    pe.wait_ge(g_pre, 1)
                if n > Z_G + 2:
                    pe.wait_ge(z_dve, n - Z_G - 2)
                if n == 2:
                    pe.wait_ge(consts, NCONST)
                    for c in range(2):
                        mm = pe.matmul(q4[3][0:8, c, 0:NREL // 2], relp[0:32, 32:40],
                                       ohp[:, c * NREL // 2:(c + 1) * NREL // 2], start=True, stop=True)
                    mm.then_inc(rel_mm, 1)
                project(q4[n % 2], n, 1, by_k(arena_hi), by_k(xt_lo), KD, x_lo if n == 0 else None)

            pe.wait_ge(rel_sb, 1)
            pe.wait_ge(g_rdy, 1)
            b6 = bank[6]
            for i in range(QT):
                pe.transpose(b6[:, 8 * i:8 * i + 8], gi[:, 128 * i:128 * i + 128], ident[0:8, 0:8])
                pe.transpose(b6[:, 32 + 8 * i:40 + 8 * i], lnb[:, 128 * i:128 * i + 128], ident[0:8, 0:8])
            pe.matmul(b6[:, 64:72], ones[0:8, :], ga[:, 512:520], start=True, stop=True)
            pe.transpose(b6[0:32, 72:80], gi[:, T:NT], ident[0:8, 0:8])
            pe.transpose(b6[0:32, 80:88], gf[:, T:NT], ident[0:8, 0:8])
            pe.wait_ge(z_act, Z_G + 1)
            for i in range(QT + 1):
                n = 128 if i < QT else NS
                mm = pe.transpose(b6[0:n, 96 + 24 * i:120 + 24 * i], gsig[:, 128 * i:128 * i + n], ident[0:24, 0:24])
            mm.then_inc(g_tr, 1)

            pe.wait_ge(silu_done, Z_MO)
            pe.wait_ge(z_dve, ZT - Z_MV)
            for i in range(QT + 1):
                n = 128 if i < QT else NS
                for b, tiles, done, free in ((4, range(Z_MV, Z_MV + 4), tok_v, tok_v_ev),
                                             (5, range(Z_MK, Z_MK + 4), tok_k, tok_k_ev),
                                             (7, (Z_CK, Z_CV, Z_SV, Z_WV), tok_kv, tok_kv_ev)):
                    if i >= 1:
                        pe.wait_ge(free, i)
                    for c, t in enumerate(tiles):
                        mm = pe.transpose(bank[b][0:n, 128 * c:128 * c + 128], zt[:, t, 128 * i:128 * i + n], ident)
                    mm.then_inc(done, 1)

            def scores(u):
                h, i = u // 4, u % 4
                p = slice(64 * (h % 2), 64 * (h % 2) + 64)
                if i == 0:
                    if h >= 2:
                        pe.wait_ge(ml_x, 4 * (h - 1))
                    pe.matmul(bank[2 + h % 2], ident[0:8, h:h + 1].broadcast_to([8, 128]), gm[:, :],
                              start=True, stop=True).then_inc(ml_mb, 1)
                if u >= 2:
                    pe.wait_ge(ml_a, u - 1)
                pe.matmul(bank[u % 2][:, 0:T - 128 * i], zt[p, Z_MK + h // 2, 128 * i:128 * i + 128],
                          zt[p, Z_MQ + h // 2, 128 * i:T], start=True, stop=True).then_inc(ml_s, 1)

            def values(h):
                pe.wait_ge(ml_a, 4 * h + 4)
                if h == 0:
                    pe.wait_ge(tok_v_ev, QT + 1)
                    pe.wait_ge(tok_k_ev, QT + 1)
                if h >= 2:
                    pe.wait_ge(ml_n, h - 1)
                for j in range(QT):
                    for i in range(j + 1):
                        at = (0, 512, 896, 1152)[i] + 128 * (j - i)
                        mm = pe.matmul(bank[4 + h % 2][:, 65 * j:65 * j + 65], aw[:, h % 2, at:at + 128],
                                       tv[:, i, h, :], start=(i == 0 and j == 0), stop=(i == j),
                                       skip_group_check=True)
                mm.then_inc(ml_o, 1)

            for u in range(4 * H):
                scores(u)
                if u % 4 == 1 and u >= 5:
                    values(u // 4 - 1)
            values(H - 1)
            pe.wait_ge(ml_wv, QT)
            pe.wait_ge(g_col, 1)
            for h in range(H):
                for i in range(QT):
                    mm = pe.matmul(b6[0:65, HD * h:HD * h + HD], wv[:, i, h, :], tk[:, i, HD * h:HD * h + HD],
                                   start=(i == 0), stop=(i == QT - 1))
            mm.then_inc(ml_c, 1)
            pe.wait_ge(ml_hn, 1)
            for t in range(4):
                if t >= 2:
                    pe.wait_ge(ml_mx, t - 1)
                for j in range(QT):
                    mm = pe.transpose(bank[t % 2][:, 128 * j:128 * j + 128],
                                      hc[:, j, 2 * t:2 * t + 2, :].rearrange("p h d -> p (h d)"), ident)
                mm.then_inc(ml_t, 1)

            b7, b5, b4 = bank[7], bank[5], bank[4]
            half = lambda h: slice(64 * (h % 2), 64 * (h % 2) + 64)
            pe.matmul(b7[0:32, 0:8], k32("trib"), gcol[0:32, 80:88], start=True, stop=True).then_inc(sd_pe, 1)
            pe.wait_ge(sd_dve, 1)
            pe.matmul(b7[0:32, 64:320], ones[0:32, 0:32], gd, start=True, stop=True).then_inc(sd_pe, 1)
            pe.wait_ge(ml_n, H)
            pe.wait_ge(sd_in, 64)
            for h in (0, 2, 4, 6, 1, 3, 5, 7):
                if h == 1:
                    step(pe, "pe", mm)
                q = zt[half(h), Z_MQ + h // 2, T:NT]
                pe.matmul(b5[0:32, 32 * h:32 * h + 32], q, zt[half(h), Z_MK + h // 2, T:NT], start=True, stop=True)
                mm = pe.matmul(b5[0:32, 256 + 8 * h:264 + 8 * h], q, ntv[half(h), h // 2, :], start=True, stop=True)
            mm.then_inc(sd_pe, 1)
            pe.wait_ge(sd_dve, 2)
            pe.matmul(b7[0:32, 8:16], k32("selend"), s32[:, 16:24], start=True, stop=True).then_inc(sd_pe, 1)
            pe.wait_ge(sd_dve, 3)
            for h in range(H):
                mm = pe.transpose(b4[0:32, 32 * h:32 * h + 32], aa[:, 32 * h:32 * h + 32], ident[0:32, 0:32])
            mm.then_inc(sd_pe, 1)
            for h in range(H):
                if h >= 2:
                    pe.wait_ge(sd_iv, h - 1)
                pe.matmul(bank[2 + h % 2][0:32, :], zt[half(h), Z_MQ + h // 2, T:NT], ctv[half(h), h // 2, :],
                          start=True, stop=True).then_inc(sd_int, 1)
            pe.wait_ge(sd_at, 1)
            pe.wait_ge(ml_ce, 1)
            for h in range(H):
                mm = pe.matmul(b6[0:32, HD * h:HD * h + HD], at_sb[:, 32 * h:32 * h + 32],
                               tvs[:, HD * h:HD * h + HD], start=True, stop=True)
            mm.then_inc(sd_pe, 1)
            pe.wait_ge(sd_e, 1)
            for bp in range(4):
                pe.matmul(b7[:, 320 + 8 * bp:328 + 8 * bp], k32("selc")[:, 128 * bp:128 * bp + 128], s32[:, 80:88],
                          start=True, stop=True)
            pe.matmul(b7[0:8, 352:360], k32("selb"), s32[:, 80:88], start=True, stop=True).then_inc(sd_pe, 1)
            pe.wait_ge(sd_dve, 5)
            pe.matmul(b5[0:8, :], k32("bm"), wks, start=True, stop=True).then_inc(sd_pe, 1)
            for bp in range(4):
                pe.wait_ge(sd_vx, bp + 1)
                if bp < 2:
                    pe.wait_ge(sd_iv, H)
                else:
                    pe.wait_ge(sd_cn, bp - 1)
                for h in range(H):
                    mm = pe.matmul(bank[2 + bp % 2][:, HD * h:HD * h + HD],
                                   vexp[:, bp % 2, 128 * h:128 * h + 128], tk[0:32, QT, HD * h:HD * h + HD],
                                   start=True, stop=True)
                mm.then_inc(sd_u, 1)
            pe.wait_ge(sd_hn, 2)
            for t in range(4):
                mm = pe.transpose(b4[:, 32 * t:32 * t + 32], hcs[:, 2 * t:2 * t + 2, :].rearrange("p h d -> p (h d)"),
                                  ident[0:32, 0:32])
            mm.then_inc(sd_pe, 1)

            for i in range(QT):
                for g in range(NG):
                    p = slice(64 * g, 64 * g + 64)
                    pe.matmul(b6[p, 4 * i:4 * i + 4], tkv[:, i, 0, p], wkey[:, g, :], start=True, stop=True)
                    mm = pe.matmul(b7[p, 0:HD], wrep[:, g, 16 - 4 * i:80 - 4 * i], tkv[:, i, 1, p], start=(i == 0), stop=(i == QT - 1))
            mm.then_inc(np_kv, 1)
            pe.wait_ge(np_kvs, 2)
            pe.wait_ge(sd_end, 2)

            def q_of(h, i):
                return zt[64 * (h // 4):64 * (h // 4) + 64, Z_NQ + h % 4, 128 * i:128 * i + 128]

            def cmp_scores(i):
                if i >= 1:
                    pe.wait_ge(np_mx, i)
                for h in range(H):
                    if h == GQ:
                        step(pe, "pe", mm)
                    mm = pe.matmul(b6[:, 16 * h:16 * h + 4 * i + 4], q_of(h, i),
                                   kcp[64 * (h // 4):64 * (h // 4) + 64, 0:4 * i + 4], start=True, stop=True)
                mm.then_inc(np_cs, 1)

            def cmp_values(i):
                pe.wait_ge(np_ce, i + 1)
                if i >= 1:
                    pe.wait_ge(np_cv, i)
                pe.transpose(b7[:, 0:128], scp.rearrange("p h c -> p (h c)"), ident).then_inc(np_ct, 1)
                pe.wait_ge(np_cv, i + 1)
                if i >= 1:
                    pe.wait_ge(np_g, 3 * i - 1)
                pe.matmul(bank[4 + 3 * i % 2], cpt, vblk.rearrange("p h d -> p (h d)"), start=True,
                          stop=True).then_inc(np_o, 1)

            def scores_n(n):
                i, k, h = n // 16, n // 8 % 2, n % 8
                if n >= 2:
                    pe.wait_ge(np_x, n - 1)
                w = 128 * i + 128
                pe.matmul(bank[n % 2][:, 0:w], q_of(h, i),
                          zt[64 * (h // 4):64 * (h // 4) + 64, (Z_SK, Z_WK)[k], 0:w],
                          start=True, stop=True).then_inc(np_s, 1)

            def transposed(n):
                pe.wait_ge(np_e, n + 1)
                if n >= 2:
                    pe.wait_ge(np_te, n - 1)
                for kk in range(n // 16 + 1):
                    mm = pe.transpose(bank[2 + n % 2][:, 128 * kk:128 * kk + 128],
                                      pb[:, n % 2, 128 * kk:128 * kk + 128], ident)
                mm.then_inc(np_t, 1)

            def values_n(n):
                i, k, h = n // 16, n // 8 % 2, n % 8
                o = 3 * i + 1 + k
                pe.wait_ge(np_te, n + 1)
                if h == 0 and o >= 2:
                    pe.wait_ge(np_g, o - 1)
                for kk in range(i + 1):
                    mm = pe.matmul(bank[4 + o % 2][:, HD * h:HD * h + HD], ptb[:, n % 2, 128 * kk:128 * kk + 128],
                                   tkv[:, kk, 2 + k, 64 * (h // 4):64 * (h // 4) + 64],
                                   start=(h == 0 and kk == 0), stop=(kk == i), skip_group_check=True)
                mm.then_inc(np_pv, 1)

            for i in range(QT):
                cmp_scores(i)
                for n in range(16 * i, 16 * i + 18):
                    if n < 16 * i + 16:
                        scores_n(n)
                    if n == 16 * i:
                        cmp_values(i)
                    if 16 * i + 1 <= n < 16 * i + 17:
                        transposed(n - 1)
                    if n >= 16 * i + 2:
                        values_n(n - 2)
                pe.wait_ge(np_g, 3 * i + 3)
                for j in range(GQ):
                    mm = pe.transpose(b6[:, 128 * j:128 * j + 128],
                                      mxa[:, 128 * j:128 * j + 128], ident)
                mm.then_inc(np_mt, 1)
            pe.wait_ge(np_mx, QT)
            pe.wait_ge(np_g, 3 * QT)
            pe.matmul(bank[0][0:32, :], relp[:, 0:32], k128("onehot")[:, 0:512], start=True, stop=True).then_inc(nd_pe, 1)
            pe.matmul(bank[1][0:32, 0:68], relp[:, 0:32], k128("onehot")[:, 512:580], start=True,
                      stop=True).then_inc(nd_pe, 1)
            for b in range(NB):
                mm = pe.matmul(bank[2][0:32, 24 * b:24 * b + 24], k32("rowsel")[:, 32 * b:32 * b + 32],
                               gcol[0:32, 192:216], start=True, stop=True)
            mm.then_inc(nd_pe, 1)
            for b in range(NB):
                mm = pe.matmul(bank[4 + b // 2][0:4, 256 * (b % 2):256 * (b % 2) + 256], ident[0:32, TS * b:TS * b + TS],
                               tkv[0:32, QT, 2:4, :].rearrange("p k c -> p (k c)"), start=True, stop=True)
            mm.then_inc(nd_pe, 1)
            pe.wait_ge(nd_qb, 1)
            pe.wait_ge(nd_pp, 1)
            pe.wait_ge(nd_vn, 4)

            def page(b, p):
                n, u = PAGES * b + p, 5 * b + p // 4
                pe.wait_ge(pg_land[n % PAGE_RING], 32 * (n // PAGE_RING + 1))
                if p % 4 == 0 and u >= 2:
                    pe.wait_ge(nd_te, u - 1)
                pg = pages[:, n % PAGE_RING, :]
                mm = pe.transpose(bank[u % 2][:, 128 * (p % 4):128 * (p % 4) + 128], pg[:, 256:384], ident)
                if p % 4 == 3:
                    mm.then_inc(nd_t, 1)
                if p == 0 and b >= 1:
                    pe.wait_ge(nd_kve, b)
                for g in range(NG):
                    s = slice(64 * g, 64 * g + 64)
                    pe.matmul(bank[6][s, 4 * p:4 * p + 4], pg[:, s], wkey[:, g, :], start=True, stop=True)
                    mm = pe.matmul(bank[7][0:64, s], wval[:, g, 60 - 4 * p:124 - 4 * p], pg[:, 128 + 64 * g:192 + 64 * g],
                                   start=(p == 0 and g == 0), stop=(p == PAGES - 1), skip_group_check=True)
                mm.then_inc(pg_used, 1)

            def scores_d(b, u):
                n = 6 * b + u
                if n >= 2:
                    pe.wait_ge(nd_se, n - 1)
                out = bank[2 + n % 2][0:32, :]
                q = qb[:, b, :]
                if u == 4:
                    pe.wait_ge(nd_kve, b + 1)
                    pe.matmul(out[:, 0:4], q, zt[:, Z_SK, T + TS * b:T + TS * b + TS], start=True, stop=True)
                    pe.matmul(out[:, 4:8], q, zt[:, Z_WK, T + TS * b:T + TS * b + TS], start=True, stop=True)
                    mm = pe.matmul(out[:, 8:72], q, kct, start=True, stop=True)
                else:
                    t = 5 * b + min(u, 4)
                    pe.wait_ge(nd_te, t + 1)
                    mm = pe.matmul(out, q, skt[:, t % 2, :], start=True, stop=True)
                mm.then_inc(nd_s, 1)

            def window_t(b):
                pe.wait_ge(wp_land[b % 2], 16 * (b // 2 + 1))
                pe.wait_ge(nd_te, 5 * b + 3)
                for k in range(4):
                    mm = pe.transpose(bank[(5 * b + 4) % 2][:, 128 * k:128 * k + 128], wpage[:, b % 2, k, 0:128], ident)
                mm.then_inc(nd_t, 1)

            def importance_d(b):
                pe.wait_ge(nd_pr, b + 1)
                if b >= 1:
                    pe.wait_ge(nd_mx, b)
                pe.matmul(bank[5][0:32, 384:416], k32("jsum"), pair, start=True, stop=True).then_inc(nd_im, 1)

            def small_td(b):
                pe.wait_ge(nd_we, b + 1)
                if b >= 1:
                    pe.wait_ge(nd_p2e, b)
                o = bank[4]
                pe.transpose(o[0:64, 0:32], pc[:, b % 2, :], ident[0:32, 0:32])
                for k in range(4):
                    pe.transpose(o[:, 32 + 32 * k:64 + 32 * k], sw[:, b % 2, 128 * k:128 * k + 128], ident[0:32, 0:32])
                pe.transpose(o[0:4, 160:192], sw[:, b % 2, 512:516], ident[0:32, 0:32]).then_inc(nd_p1, 1)

            def values_cw(b):
                pe.wait_ge(nd_p1e, b + 1)
                pe.wait_ge(nd_ie, b + 1)
                pe.matmul(bank[5][0:32, 256:384], ptc, vcs, start=True, stop=True)
                for k in range(4):
                    pe.matmul(bank[5][0:32, 128:256], ptw[:, 32 * k:32 * k + 32], wpage[:, b % 2, k, 128:256],
                              start=(k == 0), stop=False)
                pe.matmul(bank[5][0:32, 128:256], ptn[:, 32:64], vn[:, b, 128:256], start=False,
                          stop=True).then_inc(nd_o1, 1)

            def selected_td(b):
                pe.wait_ge(nd_sel, b + 1)
                pe.wait_ge(nd_p1e, b + 1)
                for k in range(PAGES):
                    pe.transpose(bank[4][:, 32 * k:32 * k + 32], score[:, b % 2, 128 * k:128 * k + 128],
                                 ident[0:32, 0:32])
                pe.transpose(bank[5][0:4, 448:480], score[:, b % 2, PAST:PAST + TS],
                             ident[0:32, 0:32]).then_inc(nd_p2, 1)

            def values_s(b):
                pe.wait_ge(nd_p2e, b + 1)
                for k in range(PAGES):
                    pe.matmul(bank[5][0:32, 0:128], pts[:, 32 * k:32 * k + 32], vsel[:, b % 2, k, :],
                              start=(k == 0), stop=False)
                pe.matmul(bank[5][0:32, 0:128], ptn[:, 0:32], vn[:, b, 0:128], start=False,
                          stop=True).then_inc(nd_o2, 1)

            def mixed_t(b):
                pe.wait_ge(nd_oa, b + 1)
                pe.transpose(bank[5][:, 416:448], oacc, ident[0:32, 0:32]).then_inc(nd_ot, 1)

            for b in range(NB + 1):
                for p in range(PAGES):
                    if b < NB:
                        page(b, p)
                    if b < NB and p in (5, 9, 13):
                        scores_d(b, p // 4 - 1)
                    if b >= 1 and p == 4:
                        importance_d(b - 1)
                        small_td(b - 1)
                    if b >= 1 and p == 8:
                        values_cw(b - 1)
                    if b >= 1 and p == 11:
                        selected_td(b - 1)
                    if b >= 1 and p == 13:
                        values_s(b - 1)
                if b < NB:
                    window_t(b)
                    scores_d(b, 3)
                    scores_d(b, 4)
                    scores_d(b, 5)
                if b >= 1:
                    mixed_t(b - 1)

            def average(base, src, out, m):
                pe.matmul(out[:, 0, 0:HALF], avg, src[:, 0:HALF], start=(m == 0), stop=(m == KD - 1))
                return pe.matmul(out[:, 1, 0:HALF + NS], avg, src[:, HALF:NT], start=(m == 0), stop=(m == KD - 1))

            def norm_pe(base, tile):
                for m in range(KD + 1):
                    if m < KD:
                        tile(m)
                    if m >= 1:
                        pe.wait_ge(ln_r, base + m)
                        mm = average(base, xt[:, m - 1, :], q4[2], m - 1)
                mm.then_inc(ln_m, 1)
                for m in range(KD):
                    pe.wait_ge(ln_q, base + m + 1)
                    mm = average(base, sqb[:, m % 2, :], q4[3], m)
                    mm.then_inc(ln_v, 1)

            def out_tile(m):
                if m >= 2:
                    pe.wait_ge(ln_r, m - 1)
                project(q4[m % 2], I_OUT + m, 1, by_k(arena_hi), by_k(mixt_lo), KD, m_lo if m == 0 else None)

            def down_tile(m):
                if m >= 2:
                    pe.wait_ge(f_y, m - 1)
                else:
                    pe.wait_ge(f_u, UP - 1 + m)
                project(q4[m % 2], I_DOWN + DOWN_PARTS * m, DOWN_PARTS, f_hi_of, by_k(zt_lo), KP,
                        f_lo if m == 0 else None)

            pe.wait_ge(attn_done, 1)
            norm_pe(0, out_tile)
            for n in range(UP):
                if n >= 2:
                    pe.wait_ge(f_u, n - 1)
                project(q4[n % 2], I_UP + n, 1, by_k(x1_hi), by_k(xt_lo), KD, y_lo if n == 0 else None)
            norm_pe(KD, down_tile)


def feature_columns():
    groups = [2 * 512, 512, 512, 8, 8, 512] + [128] * 6 + [24]
    start = np.cumsum([0] + groups)
    qk, v, o, i, f, nq = start[0:6]
    tiles = [list(range(qk + 128 * n, qk + 128 * n + 128)) for n in range(8)]
    tiles += [list(range(o + 128 * n, o + 128 * n + 128)) for n in range(4)]
    gates = [-1] * 128
    gates[G_I:G_I + 8] = range(i, i + 8)
    gates[G_F:G_F + 8] = range(f, f + 8)
    gates[G_N:G_N + 24] = range(start[12], start[12] + 24)
    tiles.append(gates)
    tiles += [list(range(v + 128 * n, v + 128 * n + 128)) for n in range(4)]
    tiles += [[nq + HD * (g * GQ + j) + d for g in range(NG) for d in range(HD)] for j in range(GQ)]
    tiles += [list(range(start[6 + n], start[6 + n] + 128)) for n in range(6)]
    return np.array(tiles)


def take(w, tiles):
    out = np.zeros(w.shape[:-1] + tiles.shape, w.dtype)
    out[..., tiles >= 0] = w[..., tiles[tiles >= 0]]
    return out


def pieces(w, kt):
    k, n, _ = w.shape
    w = w.reshape(k // (128 * kt), kt, 128, n, 128).transpose(3, 0, 2, 1, 4)
    return np.ascontiguousarray(w.reshape(-1, 128, kt * 128))


def columns(v):
    return v.reshape(-1, 128).T


def lay_out(i):
    f = np.float32
    g = {k: np.asarray(v) for k, v in i.items()}
    o = {}
    x = np.concatenate([g["x_prompt"].reshape(T, D), g["x_sample"].reshape(NS, D)], 0)
    o["xt"] = x.T.reshape(KD, 128, NT).transpose(1, 0, 2)
    tiles = feature_columns()
    up = np.array([[128 * (n // 2) + 128 * FT * (n % 2) + c for c in range(128)] for n in range(UP)])
    o["w_in"] = pieces(take(g["w_in"], tiles), KD)
    o["w_up"] = pieces(take(g["w_up"], up), KD)
    o["w_down"] = pieces(g["w_down"].reshape(FT * 128, KD, 128), KP)
    rows = list(range(512)) + [512 + HD * (gg * GQ + j) + d for j in range(GQ) for gg in range(NG) for d in range(HD)]
    o["w_out"] = pieces(g["w_out"][rows].reshape(D, KD, 128), KD)
    o["cols"] = np.concatenate([
        take(g["b_in"], tiles).T, *[columns(g["mlstm_conv_w"][j]) for j in range(4)], columns(g["mlstm_conv_b"]),
        columns(g["mlstm_norm_w"]), columns(g["ln1_w"]), columns(g["ln1_b"]), take(g["b_up"], up).T,
        *[take(g["ffn_conv_w"][j], up).T for j in range(3)], take(g["ffn_conv_b"], up).T, columns(g["b_down"]),
        columns(g["ln2_w"]), columns(g["ln2_b"])], 1)
    rel = g["rel_bias"]
    relp = np.zeros((4, 32, 40), f)
    for q in range(TS):
        for h in range(H):
            relp[q, :, h * TS + q] = rel[:, h]
    relp[0, :, 32:40] = rel
    o["relp"] = relp.reshape(128, 40)
    wkey, wval, wrep = (np.zeros((128, NG, w), f) for w in (4, ZW, 80))
    for c in range(4):
        rows = slice(32 * c, 32 * c + 32)
        wkey[rows, :, c], wval[rows, :, 60 + c] = g["nsa_pool_w"]
        for x in range(c, 80, 16):
            wrep[rows, :, x] = g["nsa_pool_w"][1]
    o["wpad"] = np.concatenate([w.reshape(128, -1) for w in (wkey, wval, wrep)], 1)
    o["hm"] = g["state_mlstm_conv"].transpose(2, 0, 1).reshape(8, 128, NB * 3).transpose(1, 0, 2)
    o["hf"] = g["state_ffn_conv"].transpose(2, 0, 1).reshape(2 * FT * 128, NB * 2)[up.reshape(-1)] \
        .reshape(UP, 128, NB * 2).transpose(1, 0, 2)
    o["m0"] = np.repeat(g["state_mlstm_m"], TS, 0)
    c = g["state_mlstm_c"]
    o["cn"] = c.reshape(4, 2, H, HD, HD).transpose(1, 3, 0, 2, 4).reshape(128, 4, H, HD)
    o["ct"] = c.reshape(NB, 4, 2, HD, HD).transpose(2, 4, 1, 0, 3).reshape(128, 4, NB * HD)
    o["n0"] = g["state_mlstm_n"].reshape(NB, H * HD)
    o["nt"] = g["state_mlstm_n"].reshape(NB, 4, 2, HD).transpose(2, 3, 1, 0).reshape(128, 4, NB)
    o["pool"] = g["cache_nsa_kv"].reshape(POOL_PAGES, 128, 512)
    o["win"] = g["cache_win_kv"].reshape(NB, WIN, 256)
    o["ptab"] = g["page_table"].reshape(1, NB * PAGES)
    o["c128"], o["c32"], o["ohp"] = constants()
    return {k: np.ascontiguousarray(v) for k, v in o.items()}


OUTS = {"y": (128, KD, NT), "zkv": (128, 6, NT), "mconv": (128, 8, 27), "fconv": (128, UP, 18),
        "c_p": (65, H * HD), "m_p": (8, 1), "c_s": (128, 4, H, HD), "n_s": (NB, H * HD), "m_s": (NS, H),
        "win_s": (NB, WIN - TS, 256)}


def kernel(**inputs):
    import concourse.bacc as bacc
    from concourse.bass_utils import run_bass_kernel_spmd

    nc = bacc.Bacc("TRN2", target_bir_lowering=False, num_devices=1)
    arrays = {f"in_{k}": v for k, v in lay_out(inputs).items()}
    a = {k[3:]: nc.dram_tensor(k, v.shape, mybir.dt.from_np(v.dtype), kind="ExternalInput").ap()
         for k, v in arrays.items()}
    for k, shape in OUTS.items():
        a["out_" + k] = nc.dram_tensor(f"out_{k}", shape, F32, kind="ExternalOutput").ap()
    layer(nc, a)
    r = run_bass_kernel_spmd(nc, [arrays], core_ids=[0]).results[0]
    o = {k: np.asarray(r[f"out_{k}"]) for k in OUTS}

    y = o["y"].transpose(2, 1, 0).reshape(NT, D)
    z = o["zkv"].transpose(2, 1, 0)
    z = z.reshape(NT, 6, NG, HD)
    kv, win = z[:, 0:4], z[:, 4:6]
    mc = o["mconv"].transpose(1, 0, 2).reshape(D, 27)
    inv = np.empty(2 * FT * 128, np.int64)
    inv[np.array([[128 * (n // 2) + 128 * FT * (n % 2) + c for c in range(128)] for n in range(UP)]).reshape(-1)] = \
        np.arange(2 * FT * 128)
    fc = o["fconv"].transpose(1, 0, 2).reshape(-1, 18)[inv]
    cp = o["c_p"].reshape(65, H, HD)
    cs = o["c_s"].reshape(2, HD, 4, H, HD).transpose(2, 0, 3, 1, 4).reshape(NB, H, HD, HD)
    win_s = np.concatenate([o["win_s"].reshape(NB, WIN - TS, 2, NG, HD), win[T:].reshape(NB, TS, 2, NG, HD)], 1)
    return (y[None, :T], y[T:].reshape(NB, TS, D), kv[None, :T], kv[T:].reshape(NB, TS, 4, NG, HD),
            win[None, :T], win_s, cp[None, :64].transpose(0, 2, 1, 3), cs, cp[None, 64], o["n_s"].reshape(NB, H, HD),
            o["m_p"].reshape(1, H), o["m_s"].reshape(NB, TS, H)[:, TS - 1],
            mc[:, 0:3].T[None], mc[:, 3:].reshape(D, NB, 3).transpose(1, 2, 0),
            fc[:, 0:2].T[None], fc[:, 2:].reshape(-1, NB, 2).transpose(1, 2, 0))
```

```python
import math
from contextlib import ExitStack

import numpy as np

import concourse.bass as bass
from concourse import mybir

F32 = mybir.dt.float32
F32R = mybir.dt.float32r
I32 = mybir.dt.int32
ALU = mybir.AluOpType
ACT = mybir.ActivationFunctionType
AX = mybir.AxisListType.X

D = 1024
KD = D // 128
T = 512
QT = T // 128
NB, TS = 8, 4
SG, GROUPS = 4, 2
ROWS = 32
NS = NB * TS
NT = T + NS
HALF = T // 2
H, HD = 8, 64
NG, GQ = 2, 4
ZT = 27
UP = 42
FT = UP // 2
DOWN_PARTS = 3
KP = FT // DOWN_PARTS
RING = 4
PAGES, PAST = 16, 2048
PAGE_RING = 8
QUADS = PAGES // 4
KEY_BUNDLES = SG + SG * QUADS
BUNDLES = 1 + KEY_BUNDLES + 2 * SG + 2
LATE = 6
CW = 44
SCW = PAST + NB * TS
POOL_PAGES = 160
NBLK, TOPK = 32, 16
WIN = 512
ALPHA = 2.0 ** 0.25
EPS = 1e-5
NEG = -1e30
FLOOR = -1e20
DEN_MIN = 1e-30
QS = HD ** -0.5

Z_MQ, Z_MK, Z_MO, Z_G, Z_MV, Z_NQ = 0, 4, 8, 12, 13, 17
Z_CK, Z_CV, Z_SK, Z_SV, Z_WK, Z_WV = 21, 22, 23, 24, 25, 26
G_I, G_F, G_N = 0, 32, 64


def table(*widths):
    at, n = {}, 0
    for name, w in widths:
        at[name] = (n, w)
        n += w
    return at, n


COL, NCOL = table(("b_in", ZT), ("mconv_w", 32), ("mconv_b", 8), ("norm_w", 4), ("ln1_w", 8), ("ln1_b", 8),
                  ("b_up", UP), ("fconv_w", 3 * UP), ("fconv_b", UP), ("b_down", 8), ("ln2_w", 8), ("ln2_b", 8))
C128, NC128 = table(("ident", 128), ("tri", 128), ("avg", 128), ("ones", 128), ("hblk", 8), ("onehot", 580),
                      ("maskw", 512), ("maskn", 64), ("tie", 1024), ("jsum", 128), ("headmask", 8), ("kvmask", 2))
C32, NC32 = table(("trib", 32), ("selend", 32), ("selc", 512), ("selb", 8), ("bm", 8), ("maskb", 32),
                  ("rowsel", 256))
NREL = 640


def bucket(n):
    if n < 16:
        return max(n, 0)
    return min(31, 16 + int(math.log(n / 16) / math.log(8) * 16))


def constants():
    f = np.float32
    p = np.arange(128)
    c = {"ident": np.eye(128), "tri": p[None, :] >= p[:, None], "avg": np.full((128, 128), 1 / D),
         "ones": np.ones((128, 128)), "hblk": (p[:, None] // 16 == np.arange(8)[None, :])}
    oh = np.zeros((TS, 32, 580))
    for q in range(TS):
        for i in range(516):
            pos = PAST - WIN + i
            oh[q, bucket(PAST + q - pos), i] = 1
        for i in range(64):
            oh[q, bucket(PAST + q - (32 * i + 31)), 516 + i] = 1
    c["onehot"] = oh.reshape(128, 580)
    r = np.arange(32)
    c["maskw"] = np.where(np.arange(512)[None, :] < p[:, None] % 4, NEG, 0)
    new = np.arange(32)
    c["maskn"] = np.concatenate([np.where((new[None, :] // 4 == SG * g + p[:, None] // ROWS)
                                          & (new[None, :] % 4 <= p[:, None] % 4), 0, NEG) for g in range(GROUPS)], 1)
    c["tie"] = np.broadcast_to((r[None, :] < r[:, None]).reshape(1, 1024), (128, 1024))
    c["jsum"] = (p[:, None] // 16 == p[None, :] // 16) & (p[:, None] % 4 == p[None, :] % 4)
    c["headmask"] = p[:, None] // 4 % 8 == np.arange(8)[None, :]
    c["kvmask"] = p[:, None] // 16 % 2 == np.arange(2)[None, :]
    a128 = np.concatenate([np.asarray(c[n], f) for n in C128], axis=1)
    same = r[:, None] // 4 == r[None, :] // 4
    d = {"trib": same & (r[:, None] <= r[None, :]),
         "selend": same & (r[:, None] % 4 == 3),
         "selc": np.stack([(r[:, None] == 4 * (2 * bp + p[None, :] // 64)) for bp in range(4)], 1).reshape(32, 512),
         "selb": r[:, None] == 4 * np.arange(8)[None, :],
         "bm": r[:, None] // 4 == np.arange(8)[None, :],
         "maskb": np.where(same & (r[None, :] <= r[:, None]), 0, NEG),
         }
    rs = np.zeros((32, 8, 32))
    for b in range(8):
        for row in range(32):
            rs[4 * b + row % 4, b, row] = 1
    d["rowsel"] = rs.reshape(32, 256)
    a32 = np.concatenate([np.asarray(d[n], f) for n in C32], axis=1)
    rel = np.zeros((32, 2 * NREL))
    for k in range(NREL):
        dist = 511 - k
        if dist >= 0:
            rel[bucket(dist), k] = 1
        else:
            rel[0:8, NREL + k] = NEG
    return a128, a32, rel.astype(f)


def layer(nc, a):
    with ExitStack() as ctx:
        def sb(name, shape, dt=F32):
            return ctx.enter_context(nc.sbuf_tensor(name, shape, dt))

        def sem(name):
            return ctx.enter_context(nc.semaphore(name))

        def large(suffix, dt):
            return [(name + suffix, shape, dt) for name, shape in (
                ("xt", [128, KD, NT]),
                ("zt", [128, ZT, NT]),
                ("wring", [128, RING, 1024]),
                ("whi", [128, 2, 1024]),
                ("mixt", [128, KD, NT]),
                ("arena", [128, 11296]))]

        with ExitStack() as scope:
            xt_r, zt_r, wring_r, whi, mixt_r, arena_r = (
                scope.enter_context(nc.sbuf_tensor(*t)) for t in large("_r", F32R))
        xt, zt, wring, whi_f, mixt, arena = (sb(*t) for t in large("", F32))
        cst = sb("cst", [128, NC128])
        c32 = sb("c32", [32, NC32])
        col = sb("col", [128, NCOL])
        smem = sb("smem", [128, 2 * SCW])
        tvs = whi_f[0:32, 0, 0:512]
        gf = sb("gf", [8, NT])
        gi = sb("gi", [8, NT])
        ga = sb("ga", [8, NT])
        gm = sb("gm", [8, T])
        gsig = sb("gsig", [24, NT])
        gcol = sb("gcol", [128, 216])
        lnb = sb("lnb", [8, NT])
        emp = sb("emp", [128, 64])
        s4 = sb("s4", [128, 8])
        var = sb("var", [128, 32])
        epsc = sb("epsc", [128, 1])
        sm = sb("sm", [128, 72])
        wpad = sb("wpad", [128, NG * (4 + 80 + CW)])
        relp = sb("relp", [128, 136])
        ptab = sb("ptab", [1, 128], I32)
        relrow = nc.dram_tensor("relrow", (H, 128, NREL), F32, kind="Internal")

        q4 = [ctx.enter_context(nc.psum_tensor(f"q{i}", [128, 2, 512], F32)) for i in range(4)]
        bank = [q4[i // 2][:, i % 2, :] for i in range(8)]

        def k128(name):
            n, w = C128[name]
            return cst[:, n:n + w]

        def k32(name):
            n, w = C32[name]
            return c32[:, n:n + w]

        def vec(name, i, p0=0, p1=128):
            n = COL[name][0] + i
            return col[p0:p1, n:n + 1]

        wkey = wpad[:, 0:8].rearrange("p (g c) -> p g c", g=NG)
        wrep = wpad[:, 8:168].rearrange("p (g c) -> p g c", g=NG)
        wslide = wpad[:, 168:].rearrange("p (e c) -> p e c", e=2)
        ident, tri, avg, ones = k128("ident"), k128("tri"), k128("avg"), k128("ones")

        tv = arena[:, 0:2080].rearrange("p (i h c) -> p i h c", i=QT, h=H)
        tk = arena[:, 2080:4640].rearrange("p (i c) -> p i c", i=QT + 1)
        tkv = arena[:, 4640:7200].rearrange("p (i k c) -> p i k c", i=QT + 1, k=4)
        tb = arena[:, 7200:11296].rearrange("p (h x) -> p h x", h=H)

        uq = smem[:, 0:1142].rearrange("p (s c) -> p s c", s=2)
        tq = smem[:, 1142:2284].rearrange("p (s c) -> p s c", s=2)
        hm = smem[:, 2284:2476].rearrange("p (n c) -> p n c", n=8)
        mc = smem[:, 2476:2692].rearrange("p (n c) -> p n c", n=8)
        ohp = smem[0:32, 2700:2700 + 2 * NREL]
        cn = smem[:, 0:2048].rearrange("p (b h d) -> p b h d", b=4, h=H)
        vexp = smem[0:32, 2048:4096].rearrange("p (s c) -> p s c", s=2)

        work = xt[:, :, :].rearrange("p k c -> p (k c)")
        aw = work[:, 0:2560].rearrange("p (s c) -> p s c", s=2)
        ww = work[:, 2560:3584].rearrange("p (s c) -> p s c", s=2)
        cout = work[0:65, 3584:4096]
        sq = work[:, 4096:4352].rearrange("p (j d) -> p j d", j=4)
        hc = zt[:, 13:17, :].rearrange("p k c -> p (k c)")[:, 0:2048].rearrange("p (j h d) -> p j h d", j=4, h=H)
        wv = mixt[:, 4:8, :].rearrange("p k c -> p (k c)")[:, 0:2080].rearrange("p (i h c) -> p i h c", i=4, h=H)

        ctv = work[:, 0:2048].rearrange("p (c n) -> p c n", c=4)
        aa = work[0:32, 2048:2304]
        at_sb = work[0:32, 2304:2560]
        n0 = work[0:8, 2560:3072]
        gd = work[0:32, 3072:3328]
        gmk = work[0:32, 3328:3584]
        mfree = mixt[0:32, 4:8, :].rearrange("p k c -> p (k c)")
        hcs = mfree[:, 0:512].rearrange("p (h d) -> p h d", h=H)
        inter = mfree[:, 512:1024].rearrange("p (h d) -> p h d", h=H)
        tmp = mfree[:, 1024:1536].rearrange("p (b e) -> p b e", b=NB)
        sqs = mfree[:, 1536:2048].rearrange("p (h d) -> p h d", h=H)
        wvs = zt[0:32, 0, 0:512]
        wks = zt[0:32, 1, 0:512]
        m0 = sm[0:32, 0:8]
        ntv = sm[:, 8:40].rearrange("p (c b) -> p c b", c=4)
        scb = sm[:, 40:72]
        pb = work[:, 0:1024].rearrange("p (s c) -> p s c", s=2)
        ptb = work[:, 1024:2048].rearrange("p (s c) -> p s c", s=2)
        mxa = work[:, 2048:2560]
        mxt = work[:, 2560:3072]
        vblk = work[:, 3072:3584].rearrange("p (h d) -> p h d", h=H)
        scp = work[:, 3584:3712].rearrange("p (h c) -> p h c", h=H)
        cpt = work[:, 3712:3840]
        kcp = work[:, 3840:3856]
        mxs = work[:, 3856:3872]
        den = work[:, 3872:3896].rearrange("p (k h) -> p k h", k=3)
        cmx = work[:, 3896:3904]
        gsc = work[:, 3904:3912]
        sqb = smem[:, 0:2 * NT].rearrange("p (s c) -> p s c", s=2)
        rstd = smem[:, 2 * NT:3 * NT]
        tf = smem[:, 0:2248].rearrange("p (s c) -> p s c", s=4)
        hf = smem[:, 2248:2248 + 672].rearrange("p (n c) -> p n c", n=UP)
        fc = smem[:, 2920:2920 + 756].rearrange("p (n c) -> p n c", n=UP)
        uf = zt[:, 21:27, :].rearrange("p k c -> p (k c)")[:, 0:2248].rearrange("p (s c) -> p s c", s=4)
        ybuf = zt[:, 21:27, :].rearrange("p k c -> p (k c)")[:, 0:2 * NT].rearrange("p (s c) -> p s c", s=2)
        s32 = whi_f[0:32, 1, 0:160]
        sc8 = sb("sc8", [8, 8])

        flat = zt[:, :, :].rearrange("p k c -> p (k c)")
        pages = wring[:, :, :].rearrange("p s c -> p (s c)")[:, 0:PAGE_RING * 384] \
            .rearrange("p (s c) -> p s c", s=PAGE_RING)
        vsel = [t[:, 0:SG * PAGES * 128].rearrange("p (s k c) -> p s k c", s=SG, k=PAGES) for t in (flat, arena)]
        wk = arena[:, 8192:9216].rearrange("p (s k c) -> p s k c", s=2, k=4)
        wvl = arena[:, 9216:11264].rearrange("p (s k c) -> p s k c", s=SG, k=4)
        score = smem[:, :].rearrange("p (g c) -> p g c", g=GROUPS)
        pts = whi_f[:, :, :].rearrange("p s c -> p (s c)")
        biasw = work[:, 0:512]
        biasn = work[:, 512:576].rearrange("p (g c) -> p g c", g=GROUPS)
        biasc = work[:, 576:640]
        skt = work[:, 640:1664].rearrange("p (s c) -> p s c", s=2)
        sw = work[:, 1664:2208]
        pc = work[:, 2208:2272]
        kct = work[:, 2272:2336]
        vcs = work[:, 2400:3424].rearrange("p (b c) -> p b c", b=NB)
        ptw = work[:, 3424:3936]
        ptc = work[:, 3936:4064]
        craw = gcol[:, 0:128]
        qb = work[:, 4064:4320].rearrange("p (b m) -> p b m", b=NB)
        rk1 = flat[:, 8704:9728].rearrange("p (j i) -> p j i", j=NBLK)
        rk2 = flat[:, 9728:10752].rearrange("p (j i) -> p j i", j=NBLK)
        gtmp, osb = flat[:, 8704:8752], flat[:, 8704:8832]
        pext = flat[:, 9728:9856]
        impt, rank, pair = (flat[:, 10752 + 32 * k:10784 + 32 * k] for k in range(3))
        ptn = flat[0:32, 10880:11136].rearrange("p (k c) -> p k c", k=2)
        vnt = flat[0:32, 11136:11392].rearrange("p (k c) -> p k c", k=2)
        st = sm[:, 0:16]
        gr = sm[:, 16:24]

        def wide(t, n=KD):
            return t[:, 0:n * NT].rearrange("p (k c) -> p k c", k=n)

        xt_lo, mixt_lo, zt_lo = xt_r, mixt_r, zt_r
        arena_hi = wide(arena_r)
        x1_hi = mixt_lo
        f_hi_arena = wide(arena_r, FT - 1)
        f_hi_last = zt_r[:, 21:27, :].rearrange("p k c -> p (k c)")[:, 2256:2256 + NT]

        def f_hi_of(i):
            return f_hi_arena[:, i, :] if i < FT - 1 else f_hi_last

        consts = sem("consts")
        xin = [sem(f"x_part{k}") for k in range(KD // 2)]
        w_hi, w_lo = sem("w_hi"), sem("w_lo")
        x_hi, x_lo, m_hi, m_lo = sem("x_hi"), sem("x_lo"), sem("m_hi"), sem("m_lo")
        y_hi, y_lo, f_hi, f_lo = sem("y_hi"), sem("y_lo"), sem("f_hi"), sem("f_lo")
        w_land = [sem(f"w_land{i}") for i in range(RING)]
        w_used = sem("w_used")
        z_act, z_dve = sem("z_act"), sem("z_dve")
        conv_done, silu_done = sem("conv_done"), sem("silu_done")
        dve_step, act_step, pool_step, pe_step = (sem(n) for n in ("dve_step", "act_step", "pool_step", "pe_step"))
        prep = sem("prep")
        stored = sem("stored")
        rel_mm, rel_sb, rel_out, tb_in = sem("rel_mm"), sem("rel_sb"), sem("rel_out"), sem("tb_in")
        g_pre, g_ln, g_rdy, g_tr, g_col, g_em = (sem(n) for n in ("g_pre", "g_ln", "g_rdy", "g_tr", "g_col", "g_em"))
        tok_v, tok_k, tok_kv = sem("tok_v"), sem("tok_k"), sem("tok_kv")
        tok_v_ev, tok_k_ev, tok_kv_ev = sem("tok_v_ev"), sem("tok_k_ev"), sem("tok_kv_ev")
        ml_s, ml_mb, ml_x, ml_w, ml_wm, ml_a = (sem(n) for n in ("ml_s", "ml_mb", "ml_x", "ml_w", "ml_wm", "ml_a"))
        ml_o, ml_n, ml_wv, ml_c, ml_ce = (sem(n) for n in ("ml_o", "ml_n", "ml_wv", "ml_c", "ml_ce"))
        ml_sd, ml_hn, ml_t, ml_mx = (sem(n) for n in ("ml_sd", "ml_hn", "ml_t", "ml_mx"))

        sd_in, sd_pe, sd_dve, sd_x, sd_e, sd_at = (sem(n) for n in ("sd_in", "sd_pe", "sd_dve", "sd_x", "sd_e", "sd_at"))
        sd_int, sd_iv, sd_hn, sd_vx, sd_u, sd_cn = (sem(n) for n in ("sd_int", "sd_iv", "sd_hn", "sd_vx", "sd_u", "sd_cn"))
        sd_end = sem("sd_end")
        np_kv, np_kvs, np_cs, np_cx, np_ce, np_ct = (sem(n) for n in ("np_kv", "np_kvs", "np_cs", "np_cx", "np_ce", "np_ct"))
        np_cv, np_z = sem("np_cv"), sem("np_z")
        np_s, np_x, np_e, np_t, np_te, np_o = (sem(n) for n in ("np_s", "np_x", "np_e", "np_t", "np_te", "np_o"))
        np_pv, sd_ir = sem("np_pv"), sem("sd_ir")
        st_cp, st_n, st_cs = sem("st_cp"), sem("st_n"), sem("st_cs")
        np_g, np_mt, np_mx = sem("np_g"), sem("np_mt"), sem("np_mx")
        xin2, hist = sem("xin2"), sem("hist")
        ln_r, ln_m, ln_c, ln_q, ln_v, ln_s, ln_h, ln_y = (sem(n) for n in (
            "ln_r", "ln_m", "ln_c", "ln_q", "ln_v", "ln_s", "ln_h", "ln_y"))
        f_u, f_conv, f_gelu, f_done, f_y = (sem(n) for n in ("f_u", "f_conv", "f_gelu", "f_done", "f_y"))
        pg_land = [sem(f"pg_land{i}") for i in range(PAGE_RING)]
        v_land = [sem(f"v_land{i}") for i in range(3)]
        wk_land = [sem(f"wk_land{i}") for i in range(2)]
        wv_land = sem("wv_land")
        pg_used, nd_z, nd_qb, nd_pp, nd_pe = (sem(n) for n in ("pg_used", "nd_z", "nd_qb", "nd_pp", "nd_pe"))
        nd_t, nd_te, nd_s, nd_se, nd_wr, nd_ce = (sem(n) for n in ("nd_t", "nd_te", "nd_s", "nd_se", "nd_wr", "nd_ce"))
        nw_x, nw_e, nw_p, nc_x, nc_e, nc_pr, nc_p = (sem(n) for n in (
            "nw_x", "nw_e", "nw_p", "nc_x", "nc_e", "nc_pr", "nc_p"))
        ns_i, ns_x, ns_e, ns_p = (sem(n) for n in ("ns_i", "ns_x", "ns_e", "ns_p"))
        nd_ow, nd_o, nd_oc, nd_ot, nd_mx = (sem(n) for n in ("nd_ow", "nd_o", "nd_oc", "nd_ot", "nd_mx"))
        NCONST = 16 * 9
        count = {"dve": 0, "act": 0, "pool": 0, "pe": 0}

        def step(eng, which, ins):
            s = {"dve": dve_step, "act": act_step, "pool": pool_step, "pe": pe_step}[which]
            count[which] += 1
            ins.then_inc(s, 1)
            eng.wait_ge(s, count[which])

        def landed(eng, i):
            eng.wait_ge(w_land[i % RING], 16 * (i // RING + 1))

        def by_sequence(buf, n, width):
            at = buf.shape[2] - NB * width
            return buf[:, n % buf.shape[1], at:at + NB * width].rearrange("p (b t) -> p b t", b=NB)

        def bc(ap, n):
            return ap.unsqueeze(len(ap.shape)).broadcast_to(list(ap.shape) + [n])

        ITEMS = [(a["w_in"], n, 1024) for n in range(ZT)] + [(a["w_out"], n, 1024) for n in range(KD)] \
            + [(a["w_up"], n, 1024) for n in range(UP)] \
            + [(a["w_down"], n, KP * 128) for n in range(KD * DOWN_PARTS)]
        I_OUT, I_UP, I_DOWN = ZT, ZT + KD, ZT + KD + UP

        def high(eng, out, src):
            return eng.activation(out, src, ACT.Copy)

        def low(eng, out, src, hi):
            return eng.tensor_tensor(out, src, hi.bitcast(F32), ALU.subtract)

        def split_hi(act, i):
            landed(act, i)
            if i >= 2:
                act.wait_ge(w_used, i - 1)
            w = ITEMS[i][2]
            high(act, whi[:, i % 2, 0:w], wring[:, i % RING, 0:w]).then_inc(w_hi, 1)

        def split_lo(dve, i):
            dve.wait_ge(w_hi, i + 1)
            w = ITEMS[i][2]
            low(dve, wring_r[:, i % RING, 0:w], wring[:, i % RING, 0:w],
                whi[:, i % 2, 0:w]).then_inc(w_lo, 1)

        def pool_rows(eng, n):
            page = eng.value_load(ptab[0:1, n:n + 1], min_val=0, max_val=POOL_PAGES - 1)
            return a["pool"][bass.DynSlice(page, 1), :, :].rearrange("a p c -> (a p) c")

        def page_values(eng, n, rows, landed):
            g, m = n // (SG * PAGES), n % (SG * PAGES)
            eng.dma_start(vsel[g][:, m // PAGES, m % PAGES, :], rows[:, 384:512]).then_inc(landed, 16)

        def page_keys(eng, n, rows):
            eng.dma_start(pages[:, n % PAGE_RING, :], rows[:, 0:384]).then_inc(pg_land[n % PAGE_RING], 16)

        def stream_page(eng, n, part):
            if n >= PAGE_RING:
                rows = pool_rows(eng, n)
                eng.wait_ge(pg_used, n - PAGE_RING + 1)
                page_keys(eng, n, rows)
            if n // 2 % 2 == part:
                v = SG * PAGES + n // 2
                page_values(eng, v, pool_rows(eng, v), v_land[1 + part])

        block = ctx.enter_context(nc.Block())

        @block.sync
        def _(sp):
            def load_weights(i):
                if i >= RING:
                    sp.wait_ge(w_used, i - RING + 1)
                w, n, width = ITEMS[i]
                sp.dma_start(wring[:, i % RING, 0:width], w[n]).then_inc(w_land[i % RING], 16)

            for k in range(KD // 2):
                sp.dma_start(xt[:, 2 * k:2 * k + 2, :], a["xt"][:, 2 * k:2 * k + 2, :]).then_inc(xin[k], 16)
                if k in (0, 2):
                    load_weights(k // 2)
            for i in range(2, I_OUT):
                load_weights(i)
            sp.wait_ge(rel_sb, 1)
            sp.dma_start(relrow.ap(), ohp[0:8, NREL:2 * NREL].unsqueeze(1).broadcast_to([8, 128, NREL])).then_inc(rel_out, 16)
            sp.wait_ge(rel_out, 16)
            shifted = bass.AP(tensor=relrow, offset=127, ap=[[NREL - 1, 128], [128 * NREL, H], [1, 512]])
            sp.dma_start(tb, shifted).then_inc(tb_in, 16)
            sp.dma_start(a["out_win_s"], a["win"][:, TS:, :]).then_inc(stored, 16)
            sp.wait_ge(z_dve, ZT - Z_MV)
            sp.dma_start(a["out_zkv"], zt[:, Z_CK:ZT, :]).then_inc(stored, 16)
            sp.wait_ge(conv_done, Z_MO)
            sp.dma_start(a["out_mconv"], mc).then_inc(stored, 16)
            sp.wait_ge(g_rdy, 1)
            sp.dma_start(a["out_m_p"], lnb[:, T - 1:T]).then_inc(stored, 16)
            sp.wait_ge(stored, 48 + 16)
            sp.wait_ge(silu_done, Z_MO)
            sp.dma_start(cn, a["cn"]).then_inc(sd_in, 16)
            sp.dma_start(ntv, a["nt"]).then_inc(sd_in, 16)
            sp.wait_ge(ml_o, H)
            sp.dma_start(ctv, a["ct"]).then_inc(sd_in, 16)
            sp.wait_ge(ml_a, 4 * H)
            sp.dma_start(n0, a["n0"]).then_inc(sd_in, 16)
            sp.wait_ge(ml_ce, 1)
            sp.dma_start(a["out_c_p"], cout).then_inc(st_cp, 16)
            sp.wait_ge(sd_dve, 4)
            sp.dma_start(a["out_m_s"], s32[:, 24:32]).then_inc(stored, 16)
            sp.wait_ge(sd_cn, 4)
            sp.dma_start(a["out_c_s"], cn).then_inc(st_cs, 16)
            sp.wait_ge(sd_end, 1)
            sp.dma_start(a["out_n_s"], n0).then_inc(st_n, 16)
            sp.wait_ge(sd_end, 2)

            for n in range(SG * PAGES):
                rows = pool_rows(sp, n)
                page_values(sp, n, rows, v_land[0])
                if n < PAGE_RING and n % 2 == 0:
                    page_keys(sp, n, rows)
            sp.wait_ge(np_mx, QT)
            sp.wait_ge(nd_pp, 1)
            for g in range(GROUPS):
                if g >= 1:
                    sp.wait_ge(nd_ow, g)
                for s in range(SG):
                    b = SG * g + s
                    if s >= 2:
                        sp.wait_ge(nd_s, KEY_BUNDLES * g + s - 1)
                    win = a["win"][b].rearrange("(k p) c -> p k c", k=4)
                    sp.dma_start(wk[:, b % 2], win[:, :, 0:128]).then_inc(wk_land[b % 2], 16)
                    sp.dma_start(wvl[:, s], win[:, :, 128:256]).then_inc(wv_land, 16)
                for n in range(SG * PAGES * g, SG * PAGES * (g + 1), 2):
                    stream_page(sp, n, 0)
            sp.wait_ge(pg_used, NB * PAGES)
            for i in range(I_OUT, I_OUT + RING):
                load_weights(i)
            sp.wait_ge(nd_mx, GROUPS)
            for k in range(KD):
                sp.dma_start(xt[:, k, :], a["xt"][:, k, :]).then_inc(xin2, 16)
            sp.dma_start(hf, a["hf"]).then_inc(hist, 16)
            for i in range(I_OUT + RING, len(ITEMS)):
                load_weights(i)
            sp.wait_ge(f_conv, UP)
            sp.dma_start(a["out_fconv"], fc).then_inc(stored, 16)
            for m in range(KD):
                sp.wait_ge(ln_y, KD + m + 1)
                sp.dma_start(a["out_y"][:, m, :], xt[:, m, :]).then_inc(stored, 16)
            sp.wait_ge(stored, 16 * (6 + KD))
            for s in (st_cp, st_n, st_cs):
                sp.wait_ge(s, 16)

        @block.gpsimd
        def _(pool):
            pool.memset(uq[:, :, 0:3], 0.0).then_inc(prep, 1)
            pool.memset(ga[:, 0:T], 1.0).then_inc(prep, 1)
            pool.wait_ge(w_used, ZT)
            pool.memset(tv[:, :, :, HD:HD + 1], 1.0).then_inc(prep, 1)

            for u in range(4 * H):
                pool.wait_ge(ml_w, u + 1)
                pool.tensor_tensor(ww[:, u % 2, 0:128], ww[:, u % 2, 0:128], tri, ALU.mult).then_inc(ml_wm, 1)
            pool.wait_ge(st_cp, 16)
            pool.memset(scp, 0.0).then_inc(np_z, 1)
            for n in range(1, PAGE_RING, 2):
                page_keys(pool, n, pool_rows(pool, n))
            pool.wait_ge(np_mx, QT)
            pool.memset(qb, 0.0).then_inc(nd_z, 1)
            pool.wait_ge(np_mx, QT)
            pool.wait_ge(nd_pp, 1)
            for n in range(1, NB * PAGES, 2):
                stream_page(pool, n, 1)
            pool.wait_ge(nd_mx, GROUPS)
            pool.wait_ge(hist, 16)
            pool.memset(uf[:, :, 0:2], 0.0).then_inc(prep, 1)

        @block.scalar
        def _(act):
            def link(ins):
                step(act, "act", ins)

            for dst, name in ((col, "cols"), (cst, "c128"), (c32, "c32"), (relp, "relp"), (ohp, "ohp"), (hm, "hm"),
                              (wpad, "wpad"), (ptab, "ptab"), (sm[0:32, 0:8], "m0")):
                act.dma_start(dst if name in ("ohp", "hm", "m0") else dst[tuple(slice(None) for _ in dst.shape)],
                              a[name]).then_inc(consts, 16)
            split_hi(act, 0)
            for k in range(KD):
                act.wait_ge(xin[k // 2], 16)
                high(act, arena_hi[:, k, :], xt[:, k, :]).then_inc(x_hi, 1)
            split_hi(act, 1)
            act.wait_ge(consts, NCONST)

            def silu(n):
                act.wait_ge(conv_done, n + 1)
                t = tq[:, n % 2, :]
                act.activation(zt[:, n, 0:T], t[:, 0:T], ACT.Silu)
                act.activation(zt[:, n, T:NT].rearrange("p (b t) -> p b t", b=NB),
                               by_sequence(tq, n, 7)[:, :, 0:TS], ACT.Silu).then_inc(silu_done, 1)

            for n in range(Z_MO):
                split_hi(act, n + 2)
                if n == 0:
                    act.wait_ge(prep, 1)
                if n >= 2:
                    act.wait_ge(conv_done, n - 1)
                u = uq[:, n % 2, :]
                us = u[:, 515:571].rearrange("p (b t) -> p b t", b=NB)
                act.activation(us[:, :, 0:3], hm[:, n, :].rearrange("p (b t) -> p b t", b=NB), ACT.Copy)
                act.activation(u[:, 3:515].rearrange("p (c t) -> p c t", c=2), q4[n % 2][:, :, 0:HALF],
                               ACT.Identity, bias=vec("b_in", n))
                act.activation(us[:, :, 3:7], q4[n % 2][:, 1, HALF:HALF + NS].rearrange("p (b t) -> p b t", b=NB),
                               ACT.Identity, bias=vec("b_in", n)).then_inc(z_act, 1)
                if n >= 1:
                    silu(n - 1)
            silu(Z_MO - 1)
            for n in range(Z_MO, Z_G + 1):
                split_hi(act, n + 2)
                if n < Z_G:
                    dst, src, b = zt[:, n, :], q4[n % 2], vec("b_in", n)
                else:
                    dst, src, b = gsig[:, :], q4[n % 2][G_N:G_N + 24], vec("b_in", n, G_N, G_N + 24)
                act.activation(dst[:, 0:T].rearrange("p (c t) -> p c t", c=2), src[:, :, 0:HALF],
                               ACT.Sigmoid, bias=b)
                act.activation(dst[:, T:NT], src[:, 1, HALF:HALF + NS], ACT.Sigmoid, bias=b).then_inc(z_act, 1)

            act.wait_ge(g_pre, 1)
            link(act.activation(lnb[:, :], gf[:, :], ACT.Abs))
            link(act.activation(lnb[:, :], lnb[:, :], ACT.Exp, scale=-1.0))
            act.activation(lnb[:, :], lnb[:, :], ACT.Ln, bias=1.0).then_inc(g_ln, 1)

            for n in range(Z_MV, ZT - 2):
                split_hi(act, n + 2)

            for i in range(QT + 1):
                n = 128 if i < QT else NS
                act.wait_ge(tok_k, i + 1)
                act.activation(tk[0:n, i, :], bank[5][0:n, :], ACT.Copy, scale=QS).then_inc(tok_k_ev, 1)
                act.wait_ge(tok_kv, i + 1)
                act.activation(tkv[0:n, i, :, :].rearrange("p k c -> p (k c)"), bank[7][0:n, :],
                               ACT.Copy).then_inc(tok_kv_ev, 1)

            act.wait_ge(g_col, 1)
            act.activation(emp[:, 0:32], gcol[:, 32:64], ACT.Exp, scale=-1.0)
            act.activation(emp[:, 32:64], emp[:, 32:64], ACT.Exp).then_inc(g_em, 1)

            for u in range(4 * H):
                act.wait_ge(ml_x, u + 1)
                n = T - 128 * (u % 4)
                act.activation(ww[:, u % 2, 0:n], ww[:, u % 2, 0:n], ACT.Exp, scale=-1.0).then_inc(ml_w, 1)
            act.wait_ge(ml_c, 1)
            act.activation(cout[:, :], bank[6][0:65, :], ACT.Copy).then_inc(ml_ce, 1)
            act.wait_ge(ml_n, H)
            act.activation(var[:, :], var[:, :], ACT.Sqrt, bias=epsc[:, :], scale=1.0 / HD).then_inc(ml_sd, 1)

            act.wait_ge(sd_x, 1)
            act.activation(gmk, gmk, ACT.Exp)
            act.wait_ge(sd_x, 2)
            act.activation(s32[:, 64:96], s32[:, 32:64], ACT.Exp).then_inc(sd_e, 1)
            act.wait_ge(sd_pe, 5)
            act.activation(at_sb, bank[4][0:32, 0:256], ACT.Copy).then_inc(sd_at, 1)
            act.wait_ge(sd_hn, 1)
            act.activation(s32[:, 120:128], s32[:, 120:128], ACT.Sqrt, bias=epsc[0:32, :], scale=1.0 / HD).then_inc(sd_at, 1)

            act.wait_ge(np_kv, 1)
            act.wait_ge(st_cp, 16)
            act.activation(kcp, bank[6][:, 0:16], ACT.Copy).then_inc(np_kvs, 1)

            def cmp_exp(i):
                act.wait_ge(np_cx, i + 1)
                act.activation(scp[:, :, 0:4 * i + 4], scp[:, :, 0:4 * i + 4], ACT.Exp).then_inc(np_ce, 1)
                act.wait_ge(np_ct, i + 1)
                if i >= 1:
                    act.wait_ge(np_o, i)
                act.activation(cpt, bank[7][:, 0:128], ACT.Copy).then_inc(np_cv, 1)

            def probs(n):
                i = n // 16
                act.wait_ge(np_x, n + 1)
                act.activation(pb[:, n % 2, 0:128 * i + 128], pb[:, n % 2, 0:128 * i + 128], ACT.Exp,
                               bias=mxs[:, n % 2:n % 2 + 1], accum_out=den[:, 1 + n // 8 % 2, n % 8:n % 8 + 1]).then_inc(np_e, 1)

            def probs_t(n):
                i = n // 16
                act.wait_ge(np_t, n + 1)
                if n >= 2:
                    act.wait_ge(np_pv, n - 1)
                act.activation(ptb[:, n % 2, 0:128 * i + 128], bank[2 + n % 2][:, 0:128 * i + 128],
                               ACT.Copy).then_inc(np_te, 1)

            for i in range(QT):
                cmp_exp(i)
                for n in range(16 * i, 16 * i + 17):
                    if n < 16 * i + 16:
                        probs(n)
                    if n > 16 * i:
                        probs_t(n - 1)
            bundles = [0]

            def bundle():
                n = bundles[0]
                bundles[0] += 1
                act.wait_ge(nd_t, n + 1)
                return bank[4 + n % 2]

            def new_scores(g):
                t = bundle()
                act.activation(score[:, g, PAST:SCW], t[:, 0:32], ACT.Copy)
                act.activation(sw[:, 512:544], t[:, 32:64], ACT.Copy).then_inc(nd_te, 1)

            def keys_t(m):
                t = bundle()
                if m >= 2:
                    act.wait_ge(nd_s, m - 1)
                act.activation(skt[:, m % 2, :], t, ACT.Copy).then_inc(nd_te, 1)

            def compressed(b):
                act.wait_ge(pg_used, PAGES * (b + 1))
                act.activation(craw, bank[6][:, 0:128], ACT.Copy)
                act.activation(vcs[:, b, :], bank[6][:, 128:256], ACT.Copy).then_inc(nd_ce, 1)

            def cmp_keys_t(b):
                t = bundle()
                for g in range(NG):
                    p = slice(64 * g, 64 * g + 64)
                    last = act.activation(kct[p].rearrange("p (u k c) -> p u k c", u=QUADS, k=4),
                                          t[p, 0:128].rearrange("p (k g u c) -> p g u k c", k=4, g=NG, u=QUADS)[:, g],
                                          ACT.Copy)
                last.then_inc(nd_te, 1)

            def cmp_scores_d(b):
                t, p = bundle(), slice(ROWS * (b % SG), ROWS * (b % SG) + ROWS)
                act.activation(pc[p], t[p, 0:64], ACT.Copy).then_inc(nd_te, 1)

            def window_exp(g):
                act.wait_ge(nw_x, g + 1)
                act.activation(sw, sw, ACT.Exp, bias=st[:, 0:1], accum_out=st[:, 1:2]).then_inc(nw_e, 1)

            def window_t(g):
                act.activation(ptw, bundle(), ACT.Copy).then_inc(nd_te, 1)
                act.activation(ptn[:, 1, :], bundle()[0:32, 0:128], ACT.Copy).then_inc(nd_te, 1)

            def cmp_exp_d(g):
                act.wait_ge(nc_x, g + 1)
                act.activation(pc, pc, ACT.Exp, bias=st[:, 4:5], accum_out=st[:, 5:6]).then_inc(nc_e, 1)

            def importance_t(g):
                t = bundle()
                act.activation(impt, t[:, 0:32], ACT.Copy).then_inc(ns_i, 1)
                act.activation(ptc, t[:, 128:256], ACT.Copy).then_inc(nd_te, 1)

            def selected_exp(g):
                act.wait_ge(ns_x, g + 1)
                act.activation(score[:, g, :], score[:, g, :], ACT.Exp, bias=st[:, 8:9],
                               accum_out=st[:, 9:10]).then_inc(ns_e, 1)

            def selected_t(g, k):
                if k < 4:
                    act.activation(pts[:, 512 * k:512 * k + 512], bundle(), ACT.Copy).then_inc(nd_te, 1)
                else:
                    act.activation(ptn[:, 0, :], bundle()[0:32, 0:128], ACT.Copy).then_inc(nd_te, 1)

            act.wait_ge(st_cs, 16)
            act.wait_ge(stored, 16 * 5)
            for g in range(GROUPS):
                m = KEY_BUNDLES * g
                new_scores(g)
                for s in range(SG):
                    keys_t(m + s)
                for i in range(SG * QUADS):
                    b = SG * g + i // QUADS
                    keys_t(m + SG + i)
                    if i % QUADS == 0 and i >= QUADS:
                        cmp_keys_t(b - 1)
                    if i % QUADS == 1 and i >= QUADS:
                        cmp_scores_d(b - 1)
                    if i == 1:
                        window_exp(g)
                    if g >= 1:
                        if i == 2:
                            importance_t(g - 1)
                        if i == 7:
                            selected_exp(g - 1)
                        if 8 <= i < 13:
                            selected_t(g - 1, i - 8)
                    if i == 13:
                        window_t(g)
                    if i % QUADS == QUADS - 1:
                        compressed(b)
                cmp_keys_t(SG * g + SG - 1)
                cmp_scores_d(SG * g + SG - 1)
                cmp_exp_d(g)
            importance_t(GROUPS - 1)
            selected_exp(GROUPS - 1)
            for k in range(5):
                selected_t(GROUPS - 1, k)

            act.wait_ge(nd_o, GROUPS)
            split_hi(act, I_OUT)
            split_hi(act, I_OUT + 1)
            act.wait_ge(nd_mx, GROUPS)
            for k in range(KD):
                high(act, arena_hi[:, k, :], mixt[:, k, :]).then_inc(m_hi, 1)
            for m in range(KD):
                split_hi(act, I_OUT + m + 2)

            def norm_act(base, w, b):
                for m in range(KD):
                    act.wait_ge(ln_c, base + m + 1)
                    if m >= 2 or base:
                        act.wait_ge(ln_v, base + m - 1)
                    act.activation(sqb[:, m % 2, :], xt[:, m, :], ACT.Square).then_inc(ln_q, 1)
                act.wait_ge(ln_v, base + KD)
                act.activation(rstd[:, 0:T].rearrange("p (c t) -> p c t", c=2), q4[3][:, :, 0:HALF], ACT.Sqrt,
                               bias=epsc[:, :])
                act.activation(rstd[:, T:NT], q4[3][:, 1, HALF:HALF + NS], ACT.Sqrt, bias=epsc[:, :]).then_inc(ln_s, 1)
                for m in range(KD):
                    act.wait_ge(ln_h, base + m + 1)
                    act.activation(xt[:, m, :], xt[:, m, :], ACT.Identity, bias=vec(b, m),
                                   scale=vec(w, m)).then_inc(ln_y, 1)
                    if base == 0:
                        act.wait_ge(ln_y, m + 1)
                        high(act, x1_hi[:, m, :], xt[:, m, :]).then_inc(y_hi, 1)

            norm_act(0, "ln1_w", "ln1_b")

            act.wait_ge(hist, 16)
            act.wait_ge(prep, 4)

            def gelu(i):
                act.wait_ge(f_conv, 2 * i + 1)
                t = tf[:, 2 * i % 4, 0:560]
                act.activation(t, t, ACT.Gelu_apprx_tanh).then_inc(f_gelu, 1)

            def gated_hi(i):
                act.wait_ge(f_done, i + 1)
                high(act, f_hi_of(i), zt[:, i, :]).then_inc(f_hi, 1)

            for n in range(UP):
                split_hi(act, I_UP + n + 2)
                if n >= 4:
                    act.wait_ge(f_conv, n - 3)
                u = uf[:, n % 4, :]
                us = by_sequence(uf, n, 6)
                act.activation(us[:, :, 0:2], hf[:, n, :].rearrange("p (b t) -> p b t", b=NB), ACT.Copy)
                act.activation(u[:, 2:514].rearrange("p (c t) -> p c t", c=2), q4[n % 2][:, :, 0:HALF],
                               ACT.Identity, bias=vec("b_up", n))
                act.activation(us[:, :, 2:6], q4[n % 2][:, 1, HALF:HALF + NS].rearrange("p (b t) -> p b t", b=NB),
                               ACT.Identity, bias=vec("b_up", n)).then_inc(f_u, 1)
                if n % 2 == 1:
                    gelu(n // 2)
                    if n >= 3:
                        gated_hi(n // 2 - 1)
            gated_hi(FT - 1)
            for m in range(KD):
                for c in range(DOWN_PARTS):
                    i = I_DOWN + DOWN_PARTS * m + c
                    if i + 2 < len(ITEMS):
                        split_hi(act, i + 2)
                act.wait_ge(w_used, I_DOWN + DOWN_PARTS * (m + 1))
                if m >= 2:
                    act.wait_ge(ln_r, KD + m - 1)
                act.activation(ybuf[:, m % 2, 0:T].rearrange("p (c t) -> p c t", c=2), q4[m % 2][:, :, 0:HALF],
                               ACT.Identity, bias=vec("b_down", m))
                act.activation(ybuf[:, m % 2, T:NT], q4[m % 2][:, 1, HALF:HALF + NS],
                               ACT.Identity, bias=vec("b_down", m)).then_inc(f_y, 1)
            norm_act(KD, "ln2_w", "ln2_b")

        @block.vector
        def _(dve):
            def link(ins):
                step(dve, "dve", ins)

            split_lo(dve, 0)
            for k in range(KD):
                dve.wait_ge(x_hi, k + 1)
                low(dve, xt_lo[:, k, :], xt[:, k, :], arena_hi[:, k, :]).then_inc(x_lo, 1)
            split_lo(dve, 1)
            dve.memset(epsc[:, :], EPS)
            dve.wait_ge(consts, NCONST)

            for n in range(Z_MO):
                split_lo(dve, n + 2)
                if n == 2:
                    dve.wait_ge(rel_mm, 1)
                    dve.tensor_tensor(ohp[0:8, NREL:2 * NREL].rearrange("p (c n) -> p c n", c=2),
                                      ohp[0:8, NREL:2 * NREL].rearrange("p (c n) -> p c n", c=2),
                                      q4[3][0:8, :, 0:NREL // 2], ALU.add).then_inc(rel_sb, 1)
                dve.wait_ge(z_act, n + 1)
                if n >= 2:
                    dve.wait_ge(silu_done, n - 1)
                u, t = uq[:, n % 2, :], tq[:, n % 2, 0:568]
                link(dve.tensor_scalar(t, u[:, 0:568], vec("mconv_w", n), vec("mconv_b", n), ALU.mult, ALU.add))
                for j in range(1, 3):
                    link(dve.scalar_tensor_tensor(out=t, in0=u[:, j:568 + j], scalar=vec("mconv_w", 8 * j + n),
                                                  in1=t, op0=ALU.mult, op1=ALU.add))
                dve.tensor_copy(mc[:, n, 0:3], u[:, 512:515])
                dve.tensor_copy(mc[:, n, 3:27].rearrange("p (b t) -> p b t", b=NB),
                                u[:, 515:571].rearrange("p (b t) -> p b t", b=NB)[:, :, 4:7])
                dve.scalar_tensor_tensor(out=t, in0=u[:, 3:571], scalar=vec("mconv_w", 24 + n),
                                         in1=t, op0=ALU.mult, op1=ALU.add).then_inc(conv_done, 1)

            for n in range(Z_MO, Z_G + 1):
                split_lo(dve, n + 2)
            dve.wait_ge(w_used, Z_G + 1)
            for dst, p in ((gi, G_I), (gf, G_F)):
                src, b = q4[Z_G % 2][p:p + 8], vec("b_in", Z_G, p, p + 8)
                dve.tensor_scalar(dst[:, 0:T].rearrange("p (c t) -> p c t", c=2), src[:, :, 0:HALF], b, None, ALU.add)
                last = dve.tensor_scalar(dst[:, T:NT], src[:, 1, HALF:HALF + NS], b, None, ALU.add)
            last.then_inc(g_pre, 1)
            dve.wait_ge(g_ln, 1)
            dve.wait_ge(g_pre, 1)
            link(dve.scalar_tensor_tensor(out=gf[:, :], in0=gf[:, :], scalar=0.0, in1=lnb[:, :],
                                          op0=ALU.min, op1=ALU.subtract))
            dve.wait_ge(prep, 2)
            link(dve.tensor_tensor_scan(out=lnb[:, 0:T], data0=ga[:, 0:T], data1=gf[:, 0:T], initial=0.0,
                                        op0=ALU.mult, op1=ALU.add))
            link(dve.tensor_tensor(gi[:, 0:T], gi[:, 0:T], lnb[:, 0:T], ALU.subtract))
            link(dve.tensor_tensor_scan(out=gm[:, :], data0=ga[:, 0:T], data1=gi[:, 0:T], initial=0.0,
                                        op0=ALU.mult, op1=ALU.max))
            dve.tensor_scalar(ga[:, 512:520], ident[0:8, 0:8], gm[:, T - 1:T], None, ALU.mult)
            dve.tensor_tensor(lnb[:, 0:T], lnb[:, 0:T], gm[:, :], ALU.add).then_inc(g_rdy, 1)

            for n in range(Z_MV, ZT):
                if n + 2 < ZT:
                    split_lo(dve, n + 2)
                dve.wait_ge(w_used, n + 1)
                s2 = QS if Z_NQ <= n < Z_CK else 1.0
                dve.tensor_scalar(zt[:, n, 0:T].rearrange("p (c t) -> p c t", c=2), q4[n % 2][:, :, 0:HALF],
                                  vec("b_in", n), s2, ALU.add, ALU.mult)
                dve.tensor_scalar(zt[:, n, T:NT], q4[n % 2][:, 1, HALF:HALF + NS], vec("b_in", n), s2,
                                  ALU.add, ALU.mult).then_inc(z_dve, 1)

            dve.wait_ge(g_tr, 1)
            dve.tensor_copy(gcol[:, 0:72], bank[6][:, 0:72])
            dve.tensor_copy(gcol[0:32, 72:88], bank[6][0:32, 72:88])
            dve.tensor_copy(gcol[:, 96:192], bank[6][:, 96:192])
            link(dve.tensor_copy(gcol[0:32, 192:216], bank[6][0:32, 192:216]))
            dve.tensor_tensor(emp[:, 32:64].rearrange("p (i h) -> p i h", i=QT),
                              gcol[:, 0:32].rearrange("p (i h) -> p i h", i=QT),
                              gcol[:, 64:72].unsqueeze(1).broadcast_to([128, QT, 8]), ALU.subtract).then_inc(g_col, 1)

            dve.wait_ge(prep, 3)
            for i in range(QT + 1):
                dve.wait_ge(tok_v, i + 1)
                if i < QT:
                    dve.tensor_copy(tv[:, i, :, 0:HD], bank[4].rearrange("p (h c) -> p h c", h=H)).then_inc(tok_v_ev, 1)
                else:
                    dve.tensor_copy(tvs, bank[4][0:NS, :]).then_inc(tok_v_ev, 1)

            def weights(u):
                h, i = u // 4, u % 4
                if i == 0:
                    dve.wait_ge(ml_mb, h + 1)
                if u >= 2:
                    dve.wait_ge(ml_a, u - 1)
                dve.tensor_scalar(ww[:, u % 2, 0:T - 128 * i], bank[2 + h % 2][:, 128 * i:T],
                                  gcol[:, 8 * i + h:8 * i + h + 1], 0.0, ALU.subtract, ALU.max).then_inc(ml_x, 1)

            def products(u):
                h, i = u // 4, u % 4
                dve.wait_ge(ml_s, u + 1)
                dve.wait_ge(ml_wm, u + 1)
                if i == 0 and h >= 2:
                    dve.wait_ge(ml_o, h - 1)
                at = (0, 512, 896, 1152)[i]
                dve.scalar_tensor_tensor(out=aw[:, h % 2, at:at + T - 128 * i], in0=bank[u % 2][:, 0:T - 128 * i],
                                         scalar=QS, in1=ww[:, u % 2, 0:T - 128 * i],
                                         op0=ALU.mult, op1=ALU.mult).then_inc(ml_a, 1)

            def normed(h):
                dve.wait_ge(ml_o, h + 1)
                o = bank[4 + h % 2][:, 0:260].rearrange("p (j c) -> p j c", j=QT)
                link(dve.tensor_scalar(s4[:, 0:4], o[:, :, HD], -1.0, None, ALU.mult))
                link(dve.tensor_tensor(s4[:, 0:4], s4[:, 0:4], o[:, :, HD], ALU.max))
                link(dve.tensor_tensor(s4[:, 0:4], s4[:, 0:4],
                                       emp[:, 0:32].rearrange("p (j h) -> p j h", j=QT)[:, :, h], ALU.max))
                link(dve.reciprocal(s4[:, 4:8], s4[:, 0:4]))
                hv = hc[:, :, h, :]
                link(dve.tensor_tensor(hv, o[:, :, 0:HD], bc(s4[:, 4:8], HD), ALU.mult))
                link(dve.tensor_reduce(s4[:, 0:4], hv, AX, ALU.add))
                link(dve.scalar_tensor_tensor(out=hv, in0=bc(s4[:, 0:4], HD), scalar=-1.0 / HD, in1=hv,
                                              op0=ALU.mult, op1=ALU.add))
                link(dve.tensor_tensor(sq[:, :, :], hv, hv, ALU.mult))
                dve.tensor_reduce(var[:, :].rearrange("p (j h) -> p j h", j=QT)[:, :, h], sq[:, :, :],
                                  AX, ALU.add).then_inc(ml_n, 1)

            dve.wait_ge(g_em, 1)
            dve.wait_ge(tok_v_ev, QT)
            for i in range(QT):
                dve.tensor_tensor(wv[:, i, :, :], tv[:, i, :, :], bc(emp[:, 32 + 8 * i:40 + 8 * i], HD + 1),
                                  ALU.mult).then_inc(ml_wv, 1)
            for u in range(4 * H + 1):
                if u < 4 * H:
                    weights(u)
                if u >= 1:
                    products(u - 1)
                if u % 4 == 3 and u >= 7:
                    normed(u // 4 - 1)
            normed(H - 1)
            dve.wait_ge(ml_sd, 1)
            link(dve.reciprocal(var[:, :], var[:, :]))
            dve.tensor_tensor(hc[:, :, :, :].rearrange("p j h d -> p (j h) d"),
                              hc[:, :, :, :].rearrange("p j h d -> p (j h) d"), bc(var[:, :], HD),
                              ALU.mult).then_inc(ml_hn, 1)
            for t in range(4):
                dve.wait_ge(ml_t, t + 1)
                dve.scalar_tensor_tensor(out=mixt[:, t, 0:T], in0=bank[t % 2], scalar=vec("norm_w", t),
                                         in1=zt[:, Z_MO + t, 0:T], op0=ALU.mult, op1=ALU.mult).then_inc(ml_mx, 1)

            s = lambda c: s32[:, 8 * c:8 * c + 8]
            F_, G_, M_, MT, X1, X3, X4, XN, WI, WKE, SCE, EM, DN, QN, T1, VS = (s(c) for c in range(16))
            dve.wait_ge(sd_pe, 1)
            link(dve.tensor_copy(F_, bank[7][0:32, 0:8]))
            link(dve.tensor_tensor(G_, gcol[0:32, 72:80], F_, ALU.subtract))
            g3 = gd.rearrange("p (h s) -> p h s", h=H)
            w3 = gmk.rearrange("p (h s) -> p h s", h=H)
            dve.tensor_tensor(g3, bc(G_, 32), ident[0:32, 0:32].unsqueeze(1).broadcast_to([32, 8, 32]),
                              ALU.mult).then_inc(sd_dve, 1)
            dve.wait_ge(sd_pe, 2)
            link(dve.tensor_tensor(w3, bank[7][0:32, 64:320].rearrange("p (h s) -> p h s", h=H),
                                   k32("maskb").unsqueeze(1).broadcast_to([32, 8, 32]), ALU.add))
            link(dve.tensor_reduce(M_, w3, AX, ALU.max))
            dve.tensor_tensor(M_, M_, m0, ALU.max).then_inc(sd_dve, 1)
            dve.wait_ge(sd_dve, 2)
            dve.tensor_tensor(w3, w3, bc(M_, 32), ALU.subtract).then_inc(sd_x, 1)
            link(dve.tensor_tensor(MT, F_, M_, ALU.add))
            dve.tensor_tensor(X1, m0, M_, ALU.subtract)
            dve.tensor_scalar(XN, MT, -1.0, None, ALU.mult)
            dve.wait_ge(sd_pe, 4)
            dve.tensor_tensor(X3, G_, bank[7][0:32, 8:16], ALU.subtract)
            dve.tensor_tensor(X4, m0, bank[7][0:32, 8:16], ALU.subtract).then_inc(sd_x, 1)
            dve.wait_ge(sd_e, 1)
            dve.wait_ge(sd_pe, 3)
            dve.scalar_tensor_tensor(out=aa, in0=bank[5][0:32, 0:256], scalar=QS, in1=gmk,
                                     op0=ALU.mult, op1=ALU.mult).then_inc(sd_dve, 1)
            dve.tensor_tensor(wvs.rearrange("p (h d) -> p h d", h=H), tvs.rearrange("p (h d) -> p h d", h=H),
                              bc(WKE, HD), ALU.mult)
            dve.tensor_tensor(wks.rearrange("p (h d) -> p h d", h=H), tk[0:32, QT, :].rearrange("p (h d) -> p h d", h=H),
                              bc(WKE, HD), ALU.mult).then_inc(sd_dve, 1)
            dve.wait_ge(sd_dve, 4)
            dve.tensor_reduce(DN, aa.rearrange("p (h s) -> p h s", h=H), AX, ALU.add)
            q8 = tmp[:, 0, :].rearrange("p (h b) -> p h b", h=H)
            link(dve.tensor_tensor(q8, bank[5][0:32, 256:320].rearrange("p (h b) -> p h b", h=H),
                                   k32("bm").unsqueeze(1).broadcast_to([32, 8, 8]), ALU.mult))
            link(dve.tensor_reduce(QN, q8, AX, ALU.add))
            link(dve.tensor_tensor(QN, QN, WI, ALU.mult))
            dve.tensor_tensor(DN, DN, QN, ALU.add).then_inc(sd_dve, 1)
            for h in range(H):
                dve.wait_ge(sd_int, h + 1)
                if h >= 1:
                    dve.wait_ge(sd_ir, h)
                ins = dve.tensor_tensor(tmp, bank[2 + h % 2][0:32, :].rearrange("p (b e) -> p b e", b=NB),
                                        bc(k32("bm"), HD), ALU.mult)
                ins.then_inc(sd_iv, 1)
                dve.wait_ge(sd_iv, h + 1)
                dve.tensor_reduce(inter[:, h, :], tmp.rearrange("p b e -> p e b"), AX, ALU.add).then_inc(sd_ir, 1)
            dve.wait_ge(sd_ir, H)
            link(dve.tensor_tensor(inter, inter, bc(WI, HD), ALU.mult))
            dve.wait_ge(sd_pe, 6)
            link(dve.tensor_tensor(hcs, inter, bank[6][0:32, :].rearrange("p (h d) -> p h d", h=H), ALU.add))
            dve.wait_ge(sd_dve, 5)
            link(dve.tensor_scalar(T1, DN, -1.0, None, ALU.mult))
            link(dve.tensor_tensor(T1, T1, DN, ALU.max))
            link(dve.tensor_tensor(T1, T1, EM, ALU.max))
            link(dve.reciprocal(T1, T1))
            link(dve.tensor_tensor(hcs, hcs, bc(T1, HD), ALU.mult))
            link(dve.tensor_reduce(T1, hcs, AX, ALU.add))
            link(dve.scalar_tensor_tensor(out=hcs, in0=bc(T1, HD), scalar=-1.0 / HD, in1=hcs,
                                          op0=ALU.mult, op1=ALU.add))
            link(dve.tensor_tensor(sqs, hcs, hcs, ALU.mult))
            dve.tensor_reduce(VS, sqs, AX, ALU.add).then_inc(sd_hn, 1)
            dve.wait_ge(sd_pe, 7)
            dve.tensor_copy(scb, bank[7][:, 320:352])
            link(dve.tensor_copy(sc8[:, :], bank[7][0:8, 352:360]))
            dve.wait_ge(sd_in, 64)

            def expand(bp):
                if bp >= 2:
                    dve.wait_ge(sd_u, bp - 1)
                for b2 in range(2):
                    b = 2 * bp + b2
                    last = dve.tensor_scalar(vexp[:, bp % 2].rearrange("p (h b e) -> p h b e", h=H, b=2)[:, :, b2, :],
                                             wvs.rearrange("p (h e) -> p h e", h=H), k32("bm")[:, b:b + 1], None, ALU.mult)
                last.then_inc(sd_vx, 1)

            expand(0)
            expand(1)
            n3 = n0.rearrange("p (h d) -> p h d", h=H)
            link(dve.tensor_tensor(n3, n3, bc(sc8[:, :], HD), ALU.mult))
            dve.wait_ge(sd_pe, 8)
            dve.tensor_tensor(n3, n3, bank[5][0:8, :].rearrange("p (h d) -> p h d", h=H), ALU.add).then_inc(sd_end, 1)
            for bp in range(4):
                link(dve.tensor_tensor(cn[:, bp], cn[:, bp], bc(scb[:, 8 * bp:8 * bp + 8], HD), ALU.mult))
                dve.wait_ge(sd_u, bp + 1)
                dve.tensor_tensor(cn[:, bp], cn[:, bp], bank[2 + bp % 2].rearrange("p (h d) -> p h d", h=H),
                                  ALU.add).then_inc(sd_cn, 1)
                if bp + 2 < 4:
                    expand(bp + 2)
            dve.wait_ge(sd_at, 2)
            link(dve.reciprocal(VS, VS))
            dve.tensor_tensor(hcs, hcs, bc(VS, HD), ALU.mult).then_inc(sd_hn, 1)
            dve.wait_ge(sd_pe, 9)
            for t in range(4):
                last = dve.scalar_tensor_tensor(out=mixt[:, t, T:NT], in0=bank[4][:, 32 * t:32 * t + 32],
                                                scalar=vec("norm_w", t), in1=zt[:, Z_MO + t, T:NT],
                                                op0=ALU.mult, op1=ALU.mult)
            last.then_inc(sd_end, 1)

            dve.wait_ge(np_kv, 1)
            dve.tensor_tensor(vblk, bank[7][:, 0:HD].unsqueeze(1).broadcast_to([128, H, HD]),
                              bc(k128("hblk"), HD), ALU.mult).then_inc(np_kvs, 1)
            dve.wait_ge(tb_in, 16)
            dve.wait_ge(np_z, 1)
            dve.wait_ge(st_n, 16)

            def cmp_scores(i):
                n, x0 = 4 * i + 4, 415 - 128 * i
                dve.wait_ge(np_cs, i + 1)
                if i >= 1:
                    dve.wait_ge(np_ct, i)
                v = scp[:, :, 0:n]
                link(dve.tensor_tensor(v, bank[6][:, 0:128].rearrange("p (h c) -> p h c", h=H)[:, :, 0:n],
                                       tb[:, :, x0:x0 + 32 * (n - 1) + 1:32], ALU.add))
                link(dve.tensor_reduce(cmx, v, AX, ALU.max))
                link(dve.tensor_scalar(cmx, cmx, FLOOR, None, ALU.max))
                dve.tensor_tensor(v, v, bc(cmx, n), ALU.subtract).then_inc(np_cx, 1)

            def logits(n):
                i, h = n // 16, n % 8
                w = 128 * i + 128
                dve.wait_ge(np_s, n + 1)
                if n >= 2:
                    dve.wait_ge(np_t, n - 1)
                link(dve.tensor_tensor_reduce(out=pb[:, n % 2, 0:w], in0=bank[n % 2][:, 0:w],
                                              in1=tb[:, h, 384 - 128 * i:512], scale=1.0, scalar=-3e38,
                                              op0=ALU.add, op1=ALU.max, accum_out=mxs[:, 2 + n % 2:3 + n % 2]))
                dve.tensor_scalar(mxs[:, n % 2:n % 2 + 1], mxs[:, 2 + n % 2:3 + n % 2], -1.0, None,
                                  ALU.mult).then_inc(np_x, 1)

            def gated(i, k):
                o = bank[4 + (3 * i + k) % 2].rearrange("p (g j d) -> p g j d", g=NG, j=GQ)
                by_head = lambda m: m.rearrange("p (j g d) -> p g j d", j=GQ, g=NG)
                scale = bc(gsc.rearrange("p (g j) -> p g j", g=NG), HD)
                if k == 0:
                    dve.wait_ge(np_ce, i + 1)
                    link(dve.tensor_reduce(den[:, 0, :], scp[:, :, 0:4 * i + 4], AX, ALU.add))
                    link(dve.tensor_scalar(den[:, 0, :], den[:, 0, :], DEN_MIN, None, ALU.max))
                else:
                    dve.wait_ge(np_e, 16 * i + 8 * k)
                link(dve.reciprocal(gsc, den[:, k, :]))
                link(dve.tensor_tensor(gsc, gsc, gcol[:, 96 + 24 * i + 8 * k:104 + 24 * i + 8 * k], ALU.mult))
                if k == 0:
                    dve.wait_ge(np_o, i + 1)
                else:
                    dve.wait_ge(np_pv, 16 * i + 8 * k)
                if k == 0:
                    if i >= 1:
                        dve.wait_ge(np_mt, i)
                    dve.tensor_tensor(by_head(mxa), o, scale, ALU.mult).then_inc(np_g, 1)
                else:
                    dve.wait_ge(np_g, 3 * i + k)
                    link(dve.tensor_tensor(by_head(mxt), o, scale, ALU.mult))
                    dve.tensor_tensor(mxa, mxa, mxt, ALU.add).then_inc(np_g, 1)

            def mixed(i):
                dve.wait_ge(np_mt, i + 1)
                dve.tensor_copy(mixt[:, 4:8, 128 * i:128 * i + 128],
                                bank[6].rearrange("p (j t) -> p j t", j=4)).then_inc(np_mx, 1)

            for i in range(QT):
                cmp_scores(i)
                for n in range(16 * i, 16 * i + 16):
                    logits(n)
                    if n % 16 == 2:
                        gated(i, 0)
                    if n % 16 == 10:
                        gated(i, 1)
                gated(i, 2)
                mixed(i)
            dve.wait_ge(nd_z, 1)
            for g in range(NG):
                p = slice(64 * g, 64 * g + 64)
                last = dve.tensor_copy(qb[p, :, 16 * g:16 * g + 16].rearrange("p b (j q) -> p b j q", j=GQ),
                                       zt[p, Z_NQ:Z_NQ + 4, T:NT].rearrange("p j (b q) -> p b j q", b=NB))
            last.then_inc(nd_qb, 1)
            dve.wait_ge(nd_pe, 1)
            dve.tensor_tensor(biasw, bank[0], k128("maskw"), ALU.add)
            dve.wait_ge(nd_pe, 2)
            for g in range(GROUPS):
                dve.tensor_tensor(biasn[:, g, :].rearrange("p (b t) -> p b t", b=NB),
                                  bank[1][:, 0:TS].unsqueeze(1).broadcast_to([128, NB, TS]),
                                  k128("maskn")[:, 32 * g:32 * g + 32].rearrange("p (b t) -> p b t", b=NB), ALU.add)
            dve.tensor_copy(biasc, bank[1][:, 4:68])
            dve.tensor_copy(vnt.rearrange("p k c -> p (k c)"), tkv[0:32, QT, 2:4, :].rearrange("p k c -> p (k c)"))
            dve.wait_ge(nd_pe, 3)
            link(dve.tensor_tensor(gtmp.rearrange("p (n h) -> p n h", h=H),
                                   bank[2][:, 0:48].rearrange("p (n h) -> p n h", h=H),
                                   k128("headmask").unsqueeze(1).broadcast_to([128, 6, H]), ALU.mult))
            dve.tensor_reduce(gr[:, 0:6], gtmp.rearrange("p (n h) -> p n h", h=H), AX, ALU.add).then_inc(nd_pp, 1)
            dve.wait_ge(nd_pp, 1)

            def gate_over_sum(g, k, c):
                link(dve.reciprocal(st[:, c + 2:c + 3], st[:, c + 1:c + 2]))
                link(dve.tensor_tensor(st[:, c + 3:c + 4], st[:, c + 2:c + 3], gr[:, 3 * g + k:3 * g + k + 1], ALU.mult))

            def negated_max(c, v):
                link(dve.tensor_reduce(st[:, 12:13], v, AX, ALU.max))
                return dve.tensor_scalar(st[:, c:c + 1], st[:, 12:13], -1.0, None, ALU.mult)

            def window_scores(g):
                dve.wait_ge(nd_s, KEY_BUNDLES * g + SG)
                dve.tensor_tensor(sw[:, 0:512], bank[3], biasw, ALU.add).then_inc(nd_wr, 1)
                dve.tensor_tensor(score[:, g, PAST:SCW], score[:, g, PAST:SCW], biasn[:, g, :], ALU.add)
                link(dve.tensor_tensor(sw[:, 512:544], sw[:, 512:544], biasn[:, g, :], ALU.add))
                dve.wait_ge(nd_wr, g + 1)
                negated_max(0, sw).then_inc(nw_x, 1)
                dve.wait_ge(nw_e, g + 1)
                gate_over_sum(g, 2, 0)
                dve.tensor_scalar(sw, sw, st[:, 3:4], None, ALU.mult).then_inc(nw_p, 1)

            def past_scores(g):
                for u in range(QUADS):
                    dve.wait_ge(nd_s, KEY_BUNDLES * (g + 1) - QUADS + u + 1)
                    n = 512 if u < QUADS - 1 else 384
                    ins = dve.tensor_scalar(score[:, g, 512 * u:512 * u + n], bank[u][:, 0:n], biasw[:, 100:101], None,
                                            ALU.add)
                    if n < 512:
                        ins = dve.tensor_tensor(score[:, g, 1920:2048], bank[u][:, n:512], biasw[:, 384:512], ALU.add)
                    ins.then_inc(nd_se, 1)

            def compressed_probs(g):
                dve.wait_ge(nd_te, BUNDLES * (g + 1) + LATE * g)
                link(dve.tensor_tensor(pc, pc, biasc, ALU.add))
                negated_max(4, pc).then_inc(nc_x, 1)
                dve.wait_ge(nc_e, g + 1)
                gate_over_sum(g, 0, 4)
                link(dve.tensor_scalar(pc, pc, st[:, 6:7], None, ALU.mult))
                dve.tensor_reduce(pair, pc.rearrange("p (n r) -> p n r", r=2), AX, ALU.add).then_inc(nc_pr, 1)
                dve.wait_ge(nc_pr, g + 1)
                link(dve.tensor_scalar(st[:, 13:15], k128("kvmask"), gr[:, 3 * g:3 * g + 1], None, ALU.mult))
                for h in range(NG):
                    dve.tensor_scalar(pext.rearrange("p (k g u c) -> p g u k c", k=4, g=NG, u=QUADS)[:, h],
                                      pc.rearrange("p (u k c) -> p u k c", u=QUADS, k=4), st[:, 13 + h:14 + h], None,
                                      ALU.mult).then_inc(nc_p, 1)

            def select(g):
                dve.wait_ge(ns_i, g + 1)
                by_i, by_j = impt.unsqueeze(1).broadcast_to([128, NBLK, NBLK]), bc(impt, NBLK)
                dve.tensor_tensor(rk1, by_i, by_j, ALU.is_gt)
                link(dve.tensor_tensor(rk2, by_i, by_j, ALU.is_equal))
                link(dve.tensor_tensor(rk2, rk2, k128("tie").rearrange("p (j i) -> p j i", j=NBLK), ALU.mult))
                link(dve.tensor_tensor(rk1, rk1, rk2, ALU.add))
                link(dve.tensor_reduce(rank, rk1, AX, ALU.add))
                link(dve.tensor_scalar(rank, rank, TOPK - 1.5, NEG, ALU.is_gt, ALU.mult))
                s3 = score[:, g, 0:PAST].rearrange("p (n c) -> p n c", n=NBLK)
                dve.wait_ge(nd_se, QUADS * (g + 1))
                link(dve.tensor_tensor(s3, s3, bc(rank, PAST // NBLK), ALU.add))
                negated_max(8, score[:, g, :]).then_inc(ns_x, 1)

            def selected_probs(g):
                dve.wait_ge(ns_e, g + 1)
                gate_over_sum(g, 1, 8)
                for k in range(5):
                    v = score[:, g, 512 * k:min(512 * k + 512, SCW)]
                    dve.tensor_scalar(v, v, st[:, 11:12], None, ALU.mult).then_inc(ns_p, 1)

            def to_mix(g):
                dve.wait_ge(nd_o, g + 1)
                dve.tensor_copy(osb, bank[7][:, 0:128]).then_inc(nd_oc, 1)
                dve.wait_ge(nd_ot, g + 1)
                for h in range(NG):
                    p = slice(64 * h, 64 * h + 64)
                    last = dve.tensor_copy(
                        mixt[p, 4:8, T + 16 * g:T + 16 * g + 16].rearrange("p j (s q) -> p s j q", s=SG),
                        bank[7][p, 128:256].rearrange("p (s h j q) -> p h s j q", s=SG, h=NG, j=GQ)[:, h])
                last.then_inc(nd_mx, 1)

            for g in range(GROUPS):
                window_scores(g)
                if g >= 1:
                    select(g - 1)
                    selected_probs(g - 1)
                    to_mix(g - 1)
                past_scores(g)
                compressed_probs(g)
            select(GROUPS - 1)
            selected_probs(GROUPS - 1)
            to_mix(GROUPS - 1)

            split_lo(dve, I_OUT)
            split_lo(dve, I_OUT + 1)
            for k in range(KD):
                dve.wait_ge(m_hi, k + 1)
                low(dve, mixt_lo[:, k, :], mixt[:, k, :], arena_hi[:, k, :]).then_inc(m_lo, 1)

            def norm_dve(base):
                for m in range(KD):
                    if base == 0:
                        split_lo(dve, I_OUT + m + 2)
                        dve.wait_ge(w_used, I_OUT + m + 1)
                        dve.wait_ge(xin2, 16 * KD)
                        dve.scalar_tensor_tensor(out=xt[:, m, 0:T].rearrange("p (c t) -> p c t", c=2),
                                                 in0=xt[:, m, 0:T].rearrange("p (c t) -> p c t", c=2), scalar=ALPHA,
                                                 in1=q4[m % 2][:, :, 0:HALF], op0=ALU.mult, op1=ALU.add)
                        dve.scalar_tensor_tensor(out=xt[:, m, T:NT], in0=xt[:, m, T:NT], scalar=ALPHA,
                                                 in1=q4[m % 2][:, 1, HALF:HALF + NS], op0=ALU.mult,
                                                 op1=ALU.add).then_inc(ln_r, 1)
                    else:
                        for c in range(DOWN_PARTS):
                            i = I_DOWN + DOWN_PARTS * m + c
                            if i + 2 < len(ITEMS):
                                split_lo(dve, i + 2)
                        dve.wait_ge(f_y, m + 1)
                        link(dve.tensor_tensor(xt[:, m, :], xt_lo[:, m, :].bitcast(F32), x1_hi[:, m, :].bitcast(F32), ALU.add))
                        dve.scalar_tensor_tensor(out=xt[:, m, :], in0=xt[:, m, :], scalar=ALPHA,
                                                 in1=ybuf[:, m % 2, :], op0=ALU.mult, op1=ALU.add).then_inc(ln_r, 1)
                dve.wait_ge(ln_m, base // KD + 1)
                for m in range(KD):
                    dve.tensor_tensor(xt[:, m, 0:T].rearrange("p (c t) -> p c t", c=2),
                                      xt[:, m, 0:T].rearrange("p (c t) -> p c t", c=2), q4[2][:, :, 0:HALF],
                                      ALU.subtract)
                    dve.tensor_tensor(xt[:, m, T:NT], xt[:, m, T:NT], q4[2][:, 1, HALF:HALF + NS],
                                      ALU.subtract).then_inc(ln_c, 1)
                dve.wait_ge(ln_s, base // KD + 1)
                link(dve.reciprocal(rstd, rstd))
                dve.wait_ge(ln_q, base + KD)
                for m in range(KD):
                    dve.tensor_tensor(xt[:, m, :], xt[:, m, :], rstd, ALU.mult).then_inc(ln_h, 1)

            norm_dve(0)
            for m in range(KD):
                dve.wait_ge(y_hi, m + 1)
                low(dve, xt_lo[:, m, :], xt[:, m, :], x1_hi[:, m, :]).then_inc(y_lo, 1)

            def gated_lo(i):
                dve.wait_ge(f_hi, i + 1)
                low(dve, zt_lo[:, i, :], zt[:, i, :], f_hi_of(i)).then_inc(f_lo, 1)

            def gate(i):
                dve.wait_ge(f_gelu, i + 1)
                dve.wait_ge(f_conv, 2 * i + 2)
                t1, t2 = tf[:, 2 * i % 4, :], tf[:, (2 * i + 1) % 4, :]
                s1, s2 = (by_sequence(tf, n, 6)[:, :, 0:TS] for n in (2 * i, 2 * i + 1))
                dve.tensor_tensor(zt[:, i, 0:T], t1[:, 0:T], t2[:, 0:T], ALU.mult)
                dve.tensor_tensor(zt[:, i, T:NT].rearrange("p (b t) -> p b t", b=NB), s1, s2,
                                  ALU.mult).then_inc(f_done, 1)

            for n in range(UP):
                split_lo(dve, I_UP + n + 2)
                dve.wait_ge(f_u, n + 1)
                u, t = uf[:, n % 4, :], tf[:, n % 4, 0:560]
                link(dve.tensor_scalar(t, u[:, 0:560], vec("fconv_w", n), vec("fconv_b", n), ALU.mult, ALU.add))
                link(dve.scalar_tensor_tensor(out=t, in0=u[:, 1:561], scalar=vec("fconv_w", UP + n),
                                              in1=t, op0=ALU.mult, op1=ALU.add))
                dve.tensor_copy(fc[:, n, 0:2], u[:, 512:514])
                dve.tensor_copy(fc[:, n, 2:18].rearrange("p (b t) -> p b t", b=NB), by_sequence(uf, n, 6)[:, :, 4:6])
                dve.scalar_tensor_tensor(out=t, in0=u[:, 2:562], scalar=vec("fconv_w", 2 * UP + n),
                                         in1=t, op0=ALU.mult, op1=ALU.add).then_inc(f_conv, 1)
                if n % 2 == 0 and n >= 2:
                    gate(n // 2 - 1)
                    if n >= 4:
                        gated_lo(n // 2 - 2)
            gate(FT - 1)
            gated_lo(FT - 2)
            gated_lo(FT - 1)
            norm_dve(KD)

        @block.tensor
        def _(pe):
            def project(out, first, parts, hi, lo, kt, split=None):
                for c in range(parts):
                    i = first + c
                    pe.wait_ge(w_lo, i + 1)
                    for k in range(kt):
                        kk = c * kt + k
                        if split is not None:
                            pe.wait_ge(split, kk + 1)
                        wh = whi[:, i % 2, 128 * k:128 * k + 128]
                        wl = wring_r[:, i % RING, 128 * k:128 * k + 128]
                        end = kk == parts * kt - 1
                        for n, (w, x) in enumerate(((wh, hi(kk)), (wh, lo(kk)), (wl, hi(kk)))):
                            pe.matmul(out[:, 0, 0:HALF], w, x[:, 0:HALF], start=(kk == 0 and n == 0),
                                      stop=(end and n == 2))
                            mm = pe.matmul(out[:, 1, 0:HALF + NS], w, x[:, HALF:NT], start=(kk == 0 and n == 0),
                                           stop=(end and n == 2))
                    mm.then_inc(w_used, 1)

            def by_k(t):
                return lambda k: t[:, k, :]

            for n in range(ZT):
                if 2 <= n <= Z_G + 2:
                    pe.wait_ge(z_act, n - 1)
                if n == Z_G + 2:
                    pe.wait_ge(g_pre, 1)
                if n > Z_G + 2:
                    pe.wait_ge(z_dve, n - Z_G - 2)
                if n == 2:
                    pe.wait_ge(consts, NCONST)
                    for c in range(2):
                        mm = pe.matmul(q4[3][0:8, c, 0:NREL // 2], relp[0:32, 128:136],
                                       ohp[:, c * NREL // 2:(c + 1) * NREL // 2], start=True, stop=True)
                    mm.then_inc(rel_mm, 1)
                project(q4[n % 2], n, 1, by_k(arena_hi), by_k(xt_lo), KD, x_lo if n == 0 else None)

            pe.wait_ge(rel_sb, 1)
            pe.wait_ge(g_rdy, 1)
            b6 = bank[6]
            for i in range(QT):
                pe.transpose(b6[:, 8 * i:8 * i + 8], gi[:, 128 * i:128 * i + 128], ident[0:8, 0:8])
                pe.transpose(b6[:, 32 + 8 * i:40 + 8 * i], lnb[:, 128 * i:128 * i + 128], ident[0:8, 0:8])
            pe.matmul(b6[:, 64:72], ones[0:8, :], ga[:, 512:520], start=True, stop=True)
            pe.transpose(b6[0:32, 72:80], gi[:, T:NT], ident[0:8, 0:8])
            pe.transpose(b6[0:32, 80:88], gf[:, T:NT], ident[0:8, 0:8])
            pe.wait_ge(z_act, Z_G + 1)
            for i in range(QT + 1):
                n = 128 if i < QT else NS
                mm = pe.transpose(b6[0:n, 96 + 24 * i:120 + 24 * i], gsig[:, 128 * i:128 * i + n], ident[0:24, 0:24])
            mm.then_inc(g_tr, 1)

            pe.wait_ge(silu_done, Z_MO)
            pe.wait_ge(z_dve, ZT - Z_MV)
            for i in range(QT + 1):
                n = 128 if i < QT else NS
                for b, tiles, done, free in ((4, range(Z_MV, Z_MV + 4), tok_v, tok_v_ev),
                                             (5, range(Z_MK, Z_MK + 4), tok_k, tok_k_ev),
                                             (7, (Z_CK, Z_CV, Z_SV, Z_WV), tok_kv, tok_kv_ev)):
                    if i >= 1:
                        pe.wait_ge(free, i)
                    for c, t in enumerate(tiles):
                        mm = pe.transpose(bank[b][0:n, 128 * c:128 * c + 128], zt[:, t, 128 * i:128 * i + n], ident)
                    mm.then_inc(done, 1)

            def scores(u):
                h, i = u // 4, u % 4
                p = slice(64 * (h % 2), 64 * (h % 2) + 64)
                if i == 0:
                    if h >= 2:
                        pe.wait_ge(ml_x, 4 * (h - 1))
                    pe.matmul(bank[2 + h % 2], ident[0:8, h:h + 1].broadcast_to([8, 128]), gm[:, :],
                              start=True, stop=True).then_inc(ml_mb, 1)
                if u >= 2:
                    pe.wait_ge(ml_a, u - 1)
                pe.matmul(bank[u % 2][:, 0:T - 128 * i], zt[p, Z_MK + h // 2, 128 * i:128 * i + 128],
                          zt[p, Z_MQ + h // 2, 128 * i:T], start=True, stop=True).then_inc(ml_s, 1)

            def values(h):
                pe.wait_ge(ml_a, 4 * h + 4)
                if h == 0:
                    pe.wait_ge(tok_v_ev, QT + 1)
                    pe.wait_ge(tok_k_ev, QT + 1)
                if h >= 2:
                    pe.wait_ge(ml_n, h - 1)
                for j in range(QT):
                    for i in range(j + 1):
                        at = (0, 512, 896, 1152)[i] + 128 * (j - i)
                        mm = pe.matmul(bank[4 + h % 2][:, 65 * j:65 * j + 65], aw[:, h % 2, at:at + 128],
                                       tv[:, i, h, :], start=(i == 0 and j == 0), stop=(i == j),
                                       skip_group_check=True)
                mm.then_inc(ml_o, 1)

            for u in range(4 * H):
                scores(u)
                if u % 4 == 1 and u >= 5:
                    values(u // 4 - 1)
            values(H - 1)
            pe.wait_ge(ml_wv, QT)
            pe.wait_ge(g_col, 1)
            for h in range(H):
                for i in range(QT):
                    mm = pe.matmul(b6[0:65, HD * h:HD * h + HD], wv[:, i, h, :], tk[:, i, HD * h:HD * h + HD],
                                   start=(i == 0), stop=(i == QT - 1))
            mm.then_inc(ml_c, 1)
            pe.wait_ge(ml_hn, 1)
            for t in range(4):
                if t >= 2:
                    pe.wait_ge(ml_mx, t - 1)
                for j in range(QT):
                    mm = pe.transpose(bank[t % 2][:, 128 * j:128 * j + 128],
                                      hc[:, j, 2 * t:2 * t + 2, :].rearrange("p h d -> p (h d)"), ident)
                mm.then_inc(ml_t, 1)

            b7, b5, b4 = bank[7], bank[5], bank[4]
            half = lambda h: slice(64 * (h % 2), 64 * (h % 2) + 64)
            pe.matmul(b7[0:32, 0:8], k32("trib"), gcol[0:32, 80:88], start=True, stop=True).then_inc(sd_pe, 1)
            pe.wait_ge(sd_dve, 1)
            pe.matmul(b7[0:32, 64:320], ones[0:32, 0:32], gd, start=True, stop=True).then_inc(sd_pe, 1)
            pe.wait_ge(ml_n, H)
            pe.wait_ge(sd_in, 64)
            for h in (0, 2, 4, 6, 1, 3, 5, 7):
                if h == 1:
                    step(pe, "pe", mm)
                q = zt[half(h), Z_MQ + h // 2, T:NT]
                pe.matmul(b5[0:32, 32 * h:32 * h + 32], q, zt[half(h), Z_MK + h // 2, T:NT], start=True, stop=True)
                mm = pe.matmul(b5[0:32, 256 + 8 * h:264 + 8 * h], q, ntv[half(h), h // 2, :], start=True, stop=True)
            mm.then_inc(sd_pe, 1)
            pe.wait_ge(sd_dve, 2)
            pe.matmul(b7[0:32, 8:16], k32("selend"), s32[:, 16:24], start=True, stop=True).then_inc(sd_pe, 1)
            pe.wait_ge(sd_dve, 3)
            for h in range(H):
                mm = pe.transpose(b4[0:32, 32 * h:32 * h + 32], aa[:, 32 * h:32 * h + 32], ident[0:32, 0:32])
            mm.then_inc(sd_pe, 1)
            for h in range(H):
                if h >= 2:
                    pe.wait_ge(sd_iv, h - 1)
                pe.matmul(bank[2 + h % 2][0:32, :], zt[half(h), Z_MQ + h // 2, T:NT], ctv[half(h), h // 2, :],
                          start=True, stop=True).then_inc(sd_int, 1)
            pe.wait_ge(sd_at, 1)
            pe.wait_ge(ml_ce, 1)
            for h in range(H):
                mm = pe.matmul(b6[0:32, HD * h:HD * h + HD], at_sb[:, 32 * h:32 * h + 32],
                               tvs[:, HD * h:HD * h + HD], start=True, stop=True)
            mm.then_inc(sd_pe, 1)
            pe.wait_ge(sd_e, 1)
            for bp in range(4):
                pe.matmul(b7[:, 320 + 8 * bp:328 + 8 * bp], k32("selc")[:, 128 * bp:128 * bp + 128], s32[:, 80:88],
                          start=True, stop=True)
            pe.matmul(b7[0:8, 352:360], k32("selb"), s32[:, 80:88], start=True, stop=True).then_inc(sd_pe, 1)
            pe.wait_ge(sd_dve, 5)
            pe.matmul(b5[0:8, :], k32("bm"), wks, start=True, stop=True).then_inc(sd_pe, 1)
            for bp in range(4):
                pe.wait_ge(sd_vx, bp + 1)
                if bp < 2:
                    pe.wait_ge(sd_iv, H)
                else:
                    pe.wait_ge(sd_cn, bp - 1)
                for h in range(H):
                    mm = pe.matmul(bank[2 + bp % 2][:, HD * h:HD * h + HD],
                                   vexp[:, bp % 2, 128 * h:128 * h + 128], tk[0:32, QT, HD * h:HD * h + HD],
                                   start=True, stop=True)
                mm.then_inc(sd_u, 1)
            pe.wait_ge(sd_hn, 2)
            for t in range(4):
                mm = pe.transpose(b4[:, 32 * t:32 * t + 32], hcs[:, 2 * t:2 * t + 2, :].rearrange("p h d -> p (h d)"),
                                  ident[0:32, 0:32])
            mm.then_inc(sd_pe, 1)

            for i in range(QT):
                for g in range(NG):
                    p = slice(64 * g, 64 * g + 64)
                    pe.matmul(b6[p, 4 * i:4 * i + 4], tkv[:, i, 0, p], wkey[:, g, :], start=True, stop=True)
                    mm = pe.matmul(b7[p, 0:HD], wrep[:, g, 16 - 4 * i:80 - 4 * i], tkv[:, i, 1, p], start=(i == 0), stop=(i == QT - 1))
            mm.then_inc(np_kv, 1)
            pe.wait_ge(np_kvs, 2)
            pe.wait_ge(sd_end, 2)

            def q_of(h, i):
                return zt[64 * (h // 4):64 * (h // 4) + 64, Z_NQ + h % 4, 128 * i:128 * i + 128]

            def cmp_scores(i):
                if i >= 1:
                    pe.wait_ge(np_mx, i)
                for h in range(H):
                    if h == GQ:
                        step(pe, "pe", mm)
                    mm = pe.matmul(b6[:, 16 * h:16 * h + 4 * i + 4], q_of(h, i),
                                   kcp[64 * (h // 4):64 * (h // 4) + 64, 0:4 * i + 4], start=True, stop=True)
                mm.then_inc(np_cs, 1)

            def cmp_values(i):
                pe.wait_ge(np_ce, i + 1)
                if i >= 1:
                    pe.wait_ge(np_cv, i)
                pe.transpose(b7[:, 0:128], scp.rearrange("p h c -> p (h c)"), ident).then_inc(np_ct, 1)
                pe.wait_ge(np_cv, i + 1)
                if i >= 1:
                    pe.wait_ge(np_g, 3 * i - 1)
                pe.matmul(bank[4 + 3 * i % 2], cpt, vblk.rearrange("p h d -> p (h d)"), start=True,
                          stop=True).then_inc(np_o, 1)

            def scores_n(n):
                i, k, h = n // 16, n // 8 % 2, n % 8
                if n >= 2:
                    pe.wait_ge(np_x, n - 1)
                w = 128 * i + 128
                pe.matmul(bank[n % 2][:, 0:w], q_of(h, i),
                          zt[64 * (h // 4):64 * (h // 4) + 64, (Z_SK, Z_WK)[k], 0:w],
                          start=True, stop=True).then_inc(np_s, 1)

            def transposed(n):
                pe.wait_ge(np_e, n + 1)
                if n >= 2:
                    pe.wait_ge(np_te, n - 1)
                for kk in range(n // 16 + 1):
                    mm = pe.transpose(bank[2 + n % 2][:, 128 * kk:128 * kk + 128],
                                      pb[:, n % 2, 128 * kk:128 * kk + 128], ident)
                mm.then_inc(np_t, 1)

            def values_n(n):
                i, k, h = n // 16, n // 8 % 2, n % 8
                o = 3 * i + 1 + k
                pe.wait_ge(np_te, n + 1)
                if h == 0 and o >= 2:
                    pe.wait_ge(np_g, o - 1)
                for kk in range(i + 1):
                    mm = pe.matmul(bank[4 + o % 2][:, HD * h:HD * h + HD], ptb[:, n % 2, 128 * kk:128 * kk + 128],
                                   tkv[:, kk, 2 + k, 64 * (h // 4):64 * (h // 4) + 64],
                                   start=(h == 0 and kk == 0), stop=(kk == i), skip_group_check=True)
                mm.then_inc(np_pv, 1)

            for i in range(QT):
                cmp_scores(i)
                for n in range(16 * i, 16 * i + 18):
                    if n < 16 * i + 16:
                        scores_n(n)
                    if n == 16 * i:
                        cmp_values(i)
                    if 16 * i + 1 <= n < 16 * i + 17:
                        transposed(n - 1)
                    if n >= 16 * i + 2:
                        values_n(n - 2)
                pe.wait_ge(np_g, 3 * i + 3)
                for j in range(GQ):
                    mm = pe.transpose(b6[:, 128 * j:128 * j + 128],
                                      mxa[:, 128 * j:128 * j + 128], ident)
                mm.then_inc(np_mt, 1)
            pe.wait_ge(np_mx, QT)
            pe.wait_ge(np_g, 3 * QT)
            pe.matmul(bank[0], relp[:, 0:128], k128("onehot")[:, 0:512], start=True, stop=True).then_inc(nd_pe, 1)
            pe.matmul(bank[1][:, 0:68], relp[:, 0:128], k128("onehot")[:, 512:580], start=True,
                      stop=True).then_inc(nd_pe, 1)
            for g in range(GROUPS):
                mm = pe.matmul(bank[2][:, 24 * g:24 * g + 24], k32("rowsel")[:, 128 * g:128 * g + 128],
                               gcol[0:32, 192:216], start=True, stop=True)
            mm.then_inc(nd_pe, 1)
            pe.wait_ge(nd_qb, 1)
            pe.wait_ge(nd_pp, 1)

            bundles, key_bundle = [0], {}

            def bundle():
                n = bundles[0]
                bundles[0] += 1
                if n >= 2:
                    pe.wait_ge(nd_te, n - 1)
                return bank[4 + n % 2]

            def new_scores(g):
                t = bundle()
                q = qb.rearrange("p b m -> p (b m)")[:, 128 * g:128 * g + 128]
                pe.matmul(t[:, 0:32], q, zt[:, Z_SK, T:NT], start=True, stop=True)
                pe.matmul(t[:, 32:64], q, zt[:, Z_WK, T:NT], start=True, stop=True).then_inc(nd_t, 1)

            def window_keys(b, m):
                pe.wait_ge(wk_land[b % 2], 16 * (b // 2 + 1))
                key_bundle[m] = bundles[0]
                t = bundle()
                for k in range(4):
                    mm = pe.transpose(t[:, 128 * k:128 * k + 128], wk[:, b % 2, k, :], ident)
                mm.then_inc(nd_t, 1)

            def page_keys(i, m):
                key_bundle[m] = bundles[0]
                t = bundle()
                for k in range(4):
                    n = 4 * i + k
                    pe.wait_ge(pg_land[n % PAGE_RING], 16 * (n // PAGE_RING + 1))
                    mm = pe.transpose(t[:, 128 * k:128 * k + 128], pages[:, n % PAGE_RING, 256:384], ident)
                mm.then_inc(nd_t, 1)

            def scores_d(g, m):
                pe.wait_ge(nd_te, key_bundle[KEY_BUNDLES * g + m] + 1)
                if m < SG:
                    s, u = m, QUADS - 1
                    if m == 0 and g >= 1:
                        pe.wait_ge(nd_se, QUADS * g)
                else:
                    s, u = (m - SG) // QUADS, (m - SG) % QUADS
                    if s == 0 and u == QUADS - 1:
                        pe.wait_ge(nd_wr, g + 1)
                pe.matmul(bank[u][ROWS * s:ROWS * s + ROWS, :], qb[:, SG * g + s, :], skt[:, (KEY_BUNDLES * g + m) % 2, :],
                          start=True, stop=True).then_inc(nd_s, 1)

            def compress(i):
                b, u = i // QUADS, i % QUADS
                if u == 0 and b >= 1:
                    pe.wait_ge(nd_ce, b)
                for k in range(4):
                    n, rows = 4 * i + k, slice(32 * k, 32 * k + 32)
                    pg = pages[:, n % PAGE_RING, :]
                    for e in range(2):
                        mm = pe.matmul(bank[6][rows, 128 * e:128 * e + 128], wslide[:, e, 12 - 4 * u:44 - 4 * u],
                                       pg[:, 128 * e:128 * e + 128], start=(u == 0 and e == 0), stop=(u == QUADS - 1),
                                       skip_group_check=True)
                    mm.then_inc(pg_used, 1)

            def cmp_keys_t(b):
                t = bundle()
                pe.wait_ge(nd_ce, b + 1)
                pe.transpose(t[:, 0:128], craw, ident).then_inc(nd_t, 1)

            def cmp_scores_d(b):
                copied, t, s = bundles[0], bundle(), b % SG
                pe.wait_ge(nd_te, copied)
                pe.matmul(t[ROWS * s:ROWS * s + ROWS, 0:64], qb[:, b, :], kct, start=True, stop=True).then_inc(nd_t, 1)

            def rows_t(out, src):
                return pe.transpose(out, src, ident)

            def window_t(g):
                pe.wait_ge(nw_p, g + 1)
                t = bundle()
                for k in range(4):
                    mm = rows_t(t[:, 128 * k:128 * k + 128], sw[:, 128 * k:128 * k + 128])
                mm.then_inc(nd_t, 1)
                rows_t(bundle()[0:32, 0:128], sw[:, 512:544]).then_inc(nd_t, 1)

            def output(s, probs, v, start=False, stop=False):
                return pe.matmul(bank[7][ROWS * s:ROWS * s + ROWS, 0:128], probs[:, ROWS * s:ROWS * s + ROWS], v,
                                 start=start, stop=stop, skip_group_check=True)

            def outputs_window(g):
                pe.wait_ge(nd_te, bundles[0])
                pe.wait_ge(wv_land, 16 * SG * (g + 1))
                if g >= 1:
                    pe.wait_ge(nd_mx, g)
                for s in range(SG):
                    output(s, ptn[:, 1, :], vnt[:, 1, :], start=True)
                    for k in range(4):
                        mm = output(s, ptw[:, 128 * k:128 * k + 128], wvl[:, s, k, :])
                mm.then_inc(nd_ow, 1)

            def importance_t(g):
                pe.wait_ge(nc_pr, g + 1)
                t = bundle()
                pe.matmul(t[:, 0:32], k128("jsum"), pair, start=True, stop=True)
                pe.wait_ge(nc_p, NG * (g + 1))
                rows_t(t[:, 128:256], pext).then_inc(nd_t, 1)

            def outputs_compressed(g):
                pe.wait_ge(nd_te, bundles[0])
                for s in range(SG):
                    output(s, ptc, vcs[:, SG * g + s, :])

            def selected_t(g, k):
                pe.wait_ge(ns_p, 5 * g + k + 1)
                t = bundle()
                if k < 4:
                    for c in range(4 * k, 4 * k + 4):
                        mm = rows_t(t[:, 128 * (c % 4):128 * (c % 4) + 128], score[:, g, 128 * c:128 * c + 128])
                else:
                    mm = rows_t(t[0:32, 0:128], score[:, g, PAST:SCW])
                mm.then_inc(nd_t, 1)
                return bundles[0]

            def outputs_selected(g, k, copied):
                pe.wait_ge(nd_te, copied)
                if k < 4:
                    if k == 0:
                        if g == 0:
                            pe.wait_ge(v_land[0], 16 * SG * PAGES)
                        else:
                            pe.wait_ge(v_land[1], 16 * SG * PAGES // 2)
                            pe.wait_ge(v_land[2], 16 * SG * PAGES // 2)
                    for s in range(SG):
                        for c in range(4 * k, 4 * k + 4):
                            output(s, pts[:, 128 * c:128 * c + 128], vsel[g][:, s, c, :])
                else:
                    for s in range(SG):
                        mm = output(s, ptn[:, 0, :], vnt[:, 0, :], stop=True)
                    mm.then_inc(nd_o, 1)

            def output_t(g):
                pe.wait_ge(nd_oc, g + 1)
                rows_t(bank[7][:, 128:256], osb).then_inc(nd_ot, 1)

            for g in range(GROUPS):
                new_scores(g)
                for s in range(SG):
                    window_keys(SG * g + s, KEY_BUNDLES * g + s)
                    if s >= 1:
                        scores_d(g, s - 1)
                for i in range(SG * QUADS):
                    page_keys(SG * QUADS * g + i, KEY_BUNDLES * g + SG + i)
                    scores_d(g, SG + i - 1)
                    if i % QUADS == 0 and i >= QUADS:
                        cmp_keys_t(SG * g + i // QUADS - 1)
                    if i % QUADS == 1 and i >= QUADS:
                        cmp_scores_d(SG * g + i // QUADS - 1)
                    compress(SG * QUADS * g + i)
                    if g >= 1:
                        if i == 2:
                            importance_t(g - 1)
                        if i == 3:
                            outputs_compressed(g - 1)
                        if 9 <= i < 14:
                            outputs_selected(g - 1, i - 9, copied)
                        if 8 <= i < 13:
                            copied = selected_t(g - 1, i - 8)
                    if i == 13:
                        window_t(g)
                    if i == 14:
                        if g >= 1:
                            output_t(g - 1)
                        outputs_window(g)
                scores_d(g, SG + SG * QUADS - 1)
                cmp_keys_t(SG * g + SG - 1)
                cmp_scores_d(SG * g + SG - 1)
            g = GROUPS - 1
            importance_t(g)
            outputs_compressed(g)
            for k in range(6):
                if k < 5:
                    next_copied = selected_t(g, k)
                if k >= 1:
                    outputs_selected(g, k - 1, copied)
                copied = next_copied
            output_t(g)

            def average(base, src, out, m):
                pe.matmul(out[:, 0, 0:HALF], avg, src[:, 0:HALF], start=(m == 0), stop=(m == KD - 1))
                return pe.matmul(out[:, 1, 0:HALF + NS], avg, src[:, HALF:NT], start=(m == 0), stop=(m == KD - 1))

            def norm_pe(base, tile):
                for m in range(KD + 1):
                    if m < KD:
                        tile(m)
                    if m >= 1:
                        pe.wait_ge(ln_r, base + m)
                        mm = average(base, xt[:, m - 1, :], q4[2], m - 1)
                mm.then_inc(ln_m, 1)
                for m in range(KD):
                    pe.wait_ge(ln_q, base + m + 1)
                    mm = average(base, sqb[:, m % 2, :], q4[3], m)
                    mm.then_inc(ln_v, 1)

            def out_tile(m):
                if m >= 2:
                    pe.wait_ge(ln_r, m - 1)
                project(q4[m % 2], I_OUT + m, 1, by_k(arena_hi), by_k(mixt_lo), KD, m_lo if m == 0 else None)

            def down_tile(m):
                if m >= 2:
                    pe.wait_ge(f_y, m - 1)
                else:
                    pe.wait_ge(f_u, UP - 1 + m)
                project(q4[m % 2], I_DOWN + DOWN_PARTS * m, DOWN_PARTS, f_hi_of, by_k(zt_lo), KP,
                        f_lo if m == 0 else None)

            pe.wait_ge(nd_mx, GROUPS)
            norm_pe(0, out_tile)
            for n in range(UP):
                if n >= 2:
                    pe.wait_ge(f_u, n - 1)
                project(q4[n % 2], I_UP + n, 1, by_k(x1_hi), by_k(xt_lo), KD, y_lo if n == 0 else None)
            norm_pe(KD, down_tile)


def feature_columns():
    groups = [2 * 512, 512, 512, 8, 8, 512] + [128] * 6 + [24]
    start = np.cumsum([0] + groups)
    qk, v, o, i, f, nq = start[0:6]
    tiles = [list(range(qk + 128 * n, qk + 128 * n + 128)) for n in range(8)]
    tiles += [list(range(o + 128 * n, o + 128 * n + 128)) for n in range(4)]
    gates = [-1] * 128
    gates[G_I:G_I + 8] = range(i, i + 8)
    gates[G_F:G_F + 8] = range(f, f + 8)
    gates[G_N:G_N + 24] = range(start[12], start[12] + 24)
    tiles.append(gates)
    tiles += [list(range(v + 128 * n, v + 128 * n + 128)) for n in range(4)]
    tiles += [[nq + HD * (g * GQ + j) + d for g in range(NG) for d in range(HD)] for j in range(GQ)]
    tiles += [list(range(start[6 + n], start[6 + n] + 128)) for n in range(6)]
    return np.array(tiles)


def take(w, tiles):
    out = np.zeros(w.shape[:-1] + tiles.shape, w.dtype)
    out[..., tiles >= 0] = w[..., tiles[tiles >= 0]]
    return out


def pieces(w, kt):
    k, n, _ = w.shape
    w = w.reshape(k // (128 * kt), kt, 128, n, 128).transpose(3, 0, 2, 1, 4)
    return np.ascontiguousarray(w.reshape(-1, 128, kt * 128))


def columns(v):
    return v.reshape(-1, 128).T


def lay_out(i):
    f = np.float32
    g = {k: np.asarray(v) for k, v in i.items()}
    o = {}
    x = np.concatenate([g["x_prompt"].reshape(T, D), g["x_sample"].reshape(NS, D)], 0)
    o["xt"] = x.T.reshape(KD, 128, NT).transpose(1, 0, 2)
    tiles = feature_columns()
    up = np.array([[128 * (n // 2) + 128 * FT * (n % 2) + c for c in range(128)] for n in range(UP)])
    o["w_in"] = pieces(take(g["w_in"], tiles), KD)
    o["w_up"] = pieces(take(g["w_up"], up), KD)
    o["w_down"] = pieces(g["w_down"].reshape(FT * 128, KD, 128), KP)
    rows = list(range(512)) + [512 + HD * (gg * GQ + j) + d for j in range(GQ) for gg in range(NG) for d in range(HD)]
    o["w_out"] = pieces(g["w_out"][rows].reshape(D, KD, 128), KD)
    o["cols"] = np.concatenate([
        take(g["b_in"], tiles).T, *[columns(g["mlstm_conv_w"][j]) for j in range(4)], columns(g["mlstm_conv_b"]),
        columns(g["mlstm_norm_w"]), columns(g["ln1_w"]), columns(g["ln1_b"]), take(g["b_up"], up).T,
        *[take(g["ffn_conv_w"][j], up).T for j in range(3)], take(g["ffn_conv_b"], up).T, columns(g["b_down"]),
        columns(g["ln2_w"]), columns(g["ln2_b"])], 1)
    rel = g["rel_bias"]
    relp = np.zeros((4, 32, 136), f)
    for q in range(TS):
        for h in range(H):
            for s in range(SG):
                relp[q, :, ROWS * s + h * TS + q] = rel[:, h]
    relp[0, :, 128:136] = rel
    o["relp"] = relp.reshape(128, 136)
    wkey, wrep, wslide = np.zeros((128, NG, 4), f), np.zeros((128, NG, 80), f), np.zeros((128, 2, CW), f)
    for c in range(4):
        rows = slice(32 * c, 32 * c + 32)
        wkey[rows, :, c] = g["nsa_pool_w"][0]
        for gg in range(NG):
            wslide[rows, :, 12 + 16 * gg + c] = g["nsa_pool_w"][:, :, gg].T
        for x in range(c, 80, 16):
            wrep[rows, :, x] = g["nsa_pool_w"][1]
    o["wpad"] = np.concatenate([w.reshape(128, -1) for w in (wkey, wrep, wslide)], 1)
    o["hm"] = g["state_mlstm_conv"].transpose(2, 0, 1).reshape(8, 128, NB * 3).transpose(1, 0, 2)
    o["hf"] = g["state_ffn_conv"].transpose(2, 0, 1).reshape(2 * FT * 128, NB * 2)[up.reshape(-1)] \
        .reshape(UP, 128, NB * 2).transpose(1, 0, 2)
    o["m0"] = np.repeat(g["state_mlstm_m"], TS, 0)
    c = g["state_mlstm_c"]
    o["cn"] = c.reshape(4, 2, H, HD, HD).transpose(1, 3, 0, 2, 4).reshape(128, 4, H, HD)
    o["ct"] = c.reshape(NB, 4, 2, HD, HD).transpose(2, 4, 1, 0, 3).reshape(128, 4, NB * HD)
    o["n0"] = g["state_mlstm_n"].reshape(NB, H * HD)
    o["nt"] = g["state_mlstm_n"].reshape(NB, 4, 2, HD).transpose(2, 3, 1, 0).reshape(128, 4, NB)
    o["pool"] = g["cache_nsa_kv"].reshape(POOL_PAGES, 128, 512)
    o["win"] = g["cache_win_kv"].reshape(NB, WIN, 256)
    o["ptab"] = g["page_table"].reshape(1, NB * PAGES)
    o["c128"], o["c32"], o["ohp"] = constants()
    return {k: np.ascontiguousarray(v) for k, v in o.items()}


OUTS = {"y": (128, KD, NT), "zkv": (128, 6, NT), "mconv": (128, 8, 27), "fconv": (128, UP, 18),
        "c_p": (65, H * HD), "m_p": (8, 1), "c_s": (128, 4, H, HD), "n_s": (NB, H * HD), "m_s": (NS, H),
        "win_s": (NB, WIN - TS, 256)}


def kernel(**inputs):
    import concourse.bacc as bacc
    from concourse.bass_utils import run_bass_kernel_spmd

    nc = bacc.Bacc("TRN2", target_bir_lowering=False, num_devices=1)
    arrays = {f"in_{k}": v for k, v in lay_out(inputs).items()}
    a = {k[3:]: nc.dram_tensor(k, v.shape, mybir.dt.from_np(v.dtype), kind="ExternalInput").ap()
         for k, v in arrays.items()}
    for k, shape in OUTS.items():
        a["out_" + k] = nc.dram_tensor(f"out_{k}", shape, F32, kind="ExternalOutput").ap()
    layer(nc, a)
    r = run_bass_kernel_spmd(nc, [arrays], core_ids=[0]).results[0]
    o = {k: np.asarray(r[f"out_{k}"]) for k in OUTS}

    y = o["y"].transpose(2, 1, 0).reshape(NT, D)
    z = o["zkv"].transpose(2, 1, 0)
    z = z.reshape(NT, 6, NG, HD)
    kv, win = z[:, 0:4], z[:, 4:6]
    mc = o["mconv"].transpose(1, 0, 2).reshape(D, 27)
    inv = np.empty(2 * FT * 128, np.int64)
    inv[np.array([[128 * (n // 2) + 128 * FT * (n % 2) + c for c in range(128)] for n in range(UP)]).reshape(-1)] = \
        np.arange(2 * FT * 128)
    fc = o["fconv"].transpose(1, 0, 2).reshape(-1, 18)[inv]
    cp = o["c_p"].reshape(65, H, HD)
    cs = o["c_s"].reshape(2, HD, 4, H, HD).transpose(2, 0, 3, 1, 4).reshape(NB, H, HD, HD)
    win_s = np.concatenate([o["win_s"].reshape(NB, WIN - TS, 2, NG, HD), win[T:].reshape(NB, TS, 2, NG, HD)], 1)
    return (y[None, :T], y[T:].reshape(NB, TS, D), kv[None, :T], kv[T:].reshape(NB, TS, 4, NG, HD),
            win[None, :T], win_s, cp[None, :64].transpose(0, 2, 1, 3), cs, cp[None, 64], o["n_s"].reshape(NB, H, HD),
            o["m_p"].reshape(1, H), o["m_s"].reshape(NB, TS, H)[:, TS - 1],
            mc[:, 0:3].T[None], mc[:, 3:].reshape(D, NB, 3).transpose(1, 2, 0),
            fc[:, 0:2].T[None], fc[:, 2:].reshape(-1, NB, 2).transpose(1, 2, 0))
```
